# Optimizing a Trainium2 kernel written in Bass

```python
import math
import jax, jax.numpy as jnp
from jax import lax
import numpy as np

D_MODEL = 1024
BATCH = 1
SEQ = 512
DEPTH = 1

N_MIXERS = 3
N_LAYERS_NSA = len(range(0, DEPTH, N_MIXERS))
N_LAYERS_GDN = len(range(1, DEPTH, N_MIXERS))
N_LAYERS_DIFF = len(range(2, DEPTH, N_MIXERS))

NSA_HEADS = 16
NSA_GROUPS = 4
NSA_HPG = NSA_HEADS // NSA_GROUPS
NSA_HEAD_DIM = D_MODEL // NSA_HEADS
NSA_KV_WIDTH = NSA_GROUPS * NSA_HEAD_DIM
NSA_IN_WIDTH = D_MODEL + 6 * NSA_KV_WIDTH + 3 * NSA_HEADS
CMP_BLOCK = 32
CMP_STRIDE = 16
CMP_HIDDEN = 256
SEL_BLOCK = 64
N_SEL_BLOCKS = 16
WINDOW = 512
NSA_QBLOCK = 32

GDN_HEADS = 8
GDN_HEAD_DIM = D_MODEL // GDN_HEADS
GDN_WIDTH = GDN_HEADS * GDN_HEAD_DIM
GDN_IN_WIDTH = 4 * GDN_WIDTH + 2 * GDN_HEADS
GDN_CONV = 4
GDN_CHUNK = 64

DIFF_HEADS = 8
DIFF_HEAD_DIM = D_MODEL // (2 * DIFF_HEADS)
DIFF_IN_WIDTH = 3 * D_MODEL
ATTN_QBLOCK = 128

MEM_TOKENS = 256
MEM_HEADS = 4
MEM_HEAD_DIM = D_MODEL // MEM_HEADS

D_FF = 2816
FFN_CONV = 3

RMS_EPS = 1e-6
NEG_INF = -1e30
FORCE_SCORE = 1e4


def rmsnorm(x, w):
    xf = x.astype(jnp.float32)
    y = xf * lax.rsqrt(jnp.mean(xf * xf, axis=-1, keepdims=True) + RMS_EPS)
    return (y * w.astype(jnp.float32)).astype(x.dtype)

def l2norm(x):
    return x * lax.rsqrt(jnp.sum(x * x, axis=-1, keepdims=True) + RMS_EPS)

def masked_softmax(s, mask):
    s = s.astype(jnp.float32)
    m = jnp.max(jnp.where(mask, s, NEG_INF), axis=-1, keepdims=True)
    e = jnp.exp(jnp.where(mask, s - m, NEG_INF))
    denom = jnp.sum(e, axis=-1, keepdims=True)
    return e / jnp.where(denom > 0, denom, 1.0)

def causal_dwconv(x, w):
    K = w.shape[0]
    S = x.shape[1]
    xp = jnp.pad(x, ((0, 0), (K - 1, 0), (0, 0)))
    return sum(xp[:, j:j + S] * w[j] for j in range(K))

def _compress(t, pe, w1, w2):
    B, S, G, dk = t.shape
    n_chunks = S // CMP_STRIDE
    r = CMP_BLOCK // CMP_STRIDE
    n_cmp = n_chunks - r + 1
    c = t.reshape(B, n_chunks, CMP_STRIDE, G, dk)
    blk = jnp.concatenate([c[:, j:j + n_cmp] for j in range(r)], axis=2)
    blk = (blk + pe[:, None, :]).transpose(0, 1, 3, 2, 4).reshape(B, n_cmp, G, CMP_BLOCK * dk)
    return jax.nn.gelu(blk @ w1) @ w2

def nsa_mixer(h, w_in, pe_k, pe_v, ck_w1, ck_w2, cv_w1, cv_w2, w_out):
    B, S, _ = h.shape
    G, Hg, dk, QB = NSA_GROUPS, NSA_HPG, NSA_HEAD_DIM, NSA_QBLOCK
    cuts = [D_MODEL + i * NSA_KV_WIDTH for i in range(7)]
    q, kc, vc, ks, vs, kw, vw, gl = jnp.split(h @ w_in, cuts, axis=-1)
    q = q.reshape(B, S, G, Hg, dk) * dk ** -0.5
    gates = jax.nn.sigmoid(gl).reshape(B, S, G, Hg, 3)

    def kv(t):
        return t.reshape(B, S, G, dk)

    k_cmp = _compress(kv(kc), pe_k, ck_w1, ck_w2)
    v_cmp = _compress(kv(vc), pe_v, cv_w1, cv_w2)
    n_cmp = k_cmp.shape[1]
    n_blk = S // SEL_BLOCK
    n_sel = min(N_SEL_BLOCKS, n_blk)
    k_sel = kv(ks).reshape(B, n_blk, SEL_BLOCK, G, dk).transpose(0, 3, 1, 2, 4)
    v_sel = kv(vs).reshape(B, n_blk, SEL_BLOCK, G, dk).transpose(0, 3, 1, 2, 4)
    pad = ((0, 0), (WINDOW, 0), (0, 0), (0, 0))
    k_win = jnp.pad(kv(kw), pad)
    v_win = jnp.pad(kv(vw), pad)

    cmp_end = jnp.arange(n_cmp) * CMP_STRIDE + CMP_BLOCK - 1
    sel_start = jnp.arange(n_blk) * SEL_BLOCK
    overlap = ((cmp_end[:, None] - CMP_BLOCK + 1 <= sel_start[None, :] + SEL_BLOCK - 1)
               & (cmp_end[:, None] >= sel_start[None, :])).astype(jnp.float32)
    b_idx = jnp.arange(B)[:, None, None]
    g_idx = jnp.arange(G)[None, :, None]
    blk_ids = jnp.arange(n_blk)[None, :]

    def one_block(args):
        q_blk, g_blk, blk = args
        t = blk * QB + jnp.arange(QB)
        qg = q_blk.transpose(0, 2, 3, 1, 4)
        p_cmp = masked_softmax(jnp.einsum('bghtd,bngd->bghtn', qg, k_cmp), cmp_end[None, :] <= t[:, None])
        o_cmp = jnp.einsum('bghtn,bngd->btghd', p_cmp.astype(v_cmp.dtype), v_cmp)
        imp = jnp.einsum('bghtn,nj->btgj', p_cmp, overlap)
        cur = (t // SEL_BLOCK)[:, None]
        forced = ((blk_ids == 0) | (blk_ids == cur) | (blk_ids == cur - 1))[:, None, :]
        valid = (sel_start[None, :] <= t[:, None])[:, None, :]
        imp = jnp.where(forced, FORCE_SCORE, jnp.where(valid, imp, -FORCE_SCORE))
        _, top = lax.top_k(imp, n_sel)
        top = top.transpose(0, 2, 1, 3)
        flat = top.reshape(B, G, QB * n_sel)
        k_g = k_sel[b_idx, g_idx, flat].reshape(B, G, QB, n_sel * SEL_BLOCK, dk)
        v_g = v_sel[b_idx, g_idx, flat].reshape(B, G, QB, n_sel * SEL_BLOCK, dk)
        pos = (top[..., None] * SEL_BLOCK + jnp.arange(SEL_BLOCK)).reshape(B, G, QB, n_sel * SEL_BLOCK)
        p_sel = masked_softmax(jnp.einsum('bghtd,bgtkd->bghtk', qg, k_g), (pos <= t[:, None])[:, :, None])
        o_sel = jnp.einsum('bghtk,bgtkd->btghd', p_sel.astype(v_g.dtype), v_g)
        start = blk * QB
        k_w = lax.dynamic_slice_in_dim(k_win, start, WINDOW + QB, axis=1)
        v_w = lax.dynamic_slice_in_dim(v_win, start, WINDOW + QB, axis=1)
        wpos = start - WINDOW + jnp.arange(WINDOW + QB)
        wmask = ((wpos[None, :] <= t[:, None]) & (wpos[None, :] > t[:, None] - WINDOW)
                 & (wpos[None, :] >= 0))
        p_win = masked_softmax(jnp.einsum('bghtd,bkgd->bghtk', qg, k_w), wmask)
        o_win = jnp.einsum('bghtk,bkgd->btghd', p_win.astype(v_w.dtype), v_w)
        o = g_blk[..., 0:1] * o_cmp + g_blk[..., 1:2] * o_sel + g_blk[..., 2:3] * o_win
        return o.reshape(B, QB, G * Hg * dk)

    nqb = S // QB
    q_blocks = q.reshape(B, nqb, QB, G, Hg, dk).transpose(1, 0, 2, 3, 4, 5)
    g_blocks = gates.reshape(B, nqb, QB, G, Hg, 3).transpose(1, 0, 2, 3, 4, 5)
    o = lax.map(one_block, (q_blocks, g_blocks, jnp.arange(nqb)))
    o = o.transpose(1, 0, 2, 3).reshape(B, S, D_MODEL)
    return o @ w_out

def chunk_gated_delta_rule(q, k, v, g, beta):
    B, S, H, dk = q.shape
    dv = v.shape[-1]
    C = GDN_CHUNK
    N = S // C

    def to_chunks(t):
        return t.reshape(B, N, C, H, t.shape[-1]).transpose(0, 3, 1, 2, 4)

    q, k, v = to_chunks(q), to_chunks(k), to_chunks(v)
    g = g.reshape(B, N, C, H).transpose(0, 3, 1, 2)
    beta = beta.reshape(B, N, C, H).transpose(0, 3, 1, 2)
    gc = jnp.cumsum(g, axis=-1)
    tri = jnp.tril(jnp.ones((C, C), dtype=bool))
    strict = jnp.tril(jnp.ones((C, C), dtype=bool), -1)
    diff = gc[..., :, None] - gc[..., None, :]
    decay = jnp.where(tri, jnp.exp(jnp.where(tri, diff, 0.0)), 0.0)
    kb = k * beta[..., None]
    vb = v * beta[..., None]
    a_mat = jnp.where(strict, jnp.einsum('bhncd,bhnmd->bhncm', kb, k) * decay, 0.0) + jnp.eye(C, dtype=q.dtype)
    rhs = jnp.concatenate([vb, kb * jnp.exp(gc)[..., None]], axis=-1)
    sol = lax.linalg.triangular_solve(a_mat, rhs, left_side=True, lower=True, unit_diagonal=True)
    u, w = sol[..., :dv], sol[..., dv:]
    qk = jnp.einsum('bhncd,bhnmd->bhncm', q, k) * decay
    q_dec = q * jnp.exp(gc)[..., None]
    k_dec = k * jnp.exp(gc[..., -1:] - gc)[..., None]
    g_last = jnp.exp(gc[..., -1])
    xs = (jnp.moveaxis(q_dec, 2, 0), jnp.moveaxis(k_dec, 2, 0), jnp.moveaxis(u, 2, 0),
          jnp.moveaxis(w, 2, 0), jnp.moveaxis(qk, 2, 0), jnp.moveaxis(g_last, 2, 0))

    def step(state, inp):
        qd, kd, uc, wc, qkc, gl = inp
        v_new = uc - jnp.einsum('bhcd,bhde->bhce', wc, state)
        o = jnp.einsum('bhcd,bhde->bhce', qd, state) + jnp.einsum('bhcm,bhme->bhce', qkc, v_new)
        state = state * gl[..., None, None] + jnp.einsum('bhcd,bhce->bhde', kd, v_new)
        return state, o

    _, o = lax.scan(step, jnp.zeros((B, H, dk, dv), q.dtype), xs)
    return o.transpose(1, 0, 3, 2, 4).reshape(B, S, H, dv)

def gdn_mixer(h, w_in, conv_w, a_log, dt_bias, norm_w, w_out):
    B, S, _ = h.shape
    H, d = GDN_HEADS, GDN_HEAD_DIM
    qkv, z, b_raw, a_raw = jnp.split(h @ w_in, [3 * GDN_WIDTH, 4 * GDN_WIDTH, 4 * GDN_WIDTH + H], axis=-1)
    qkv = jax.nn.silu(causal_dwconv(qkv, conv_w)).astype(jnp.float32)
    q, k, v = jnp.split(qkv, 3, axis=-1)
    q = l2norm(q.reshape(B, S, H, d)) * d ** -0.5
    k = l2norm(k.reshape(B, S, H, d))
    v = v.reshape(B, S, H, d)
    beta = jax.nn.sigmoid(b_raw.astype(jnp.float32))
    g = -jnp.exp(a_log.astype(jnp.float32)) * jax.nn.softplus(a_raw.astype(jnp.float32) + dt_bias.astype(jnp.float32))
    o = chunk_gated_delta_rule(q, k, v, g, beta)
    o = rmsnorm(o, norm_w) * jax.nn.silu(z.reshape(B, S, H, d).astype(jnp.float32))
    return o.reshape(B, S, GDN_WIDTH).astype(h.dtype) @ w_out

def diff_mixer(h, w_in, lq1, lk1, lq2, lk2, subln_w, w_out, lambda_init):
    B, S, _ = h.shape
    H, dh, QB = DIFF_HEADS, DIFF_HEAD_DIM, ATTN_QBLOCK
    q, k, v = jnp.split(h @ w_in, 3, axis=-1)
    q = q.reshape(B, S, H, 2, dh) * dh ** -0.5
    k = k.reshape(B, S, H, 2, dh)
    v = v.reshape(B, S, H, 2 * dh)
    f32 = jnp.float32
    lam = (jnp.exp(jnp.sum(lq1.astype(f32) * lk1.astype(f32))) - jnp.exp(jnp.sum(lq2.astype(f32) * lk2.astype(f32)))
           + lambda_init)
    kpos = jnp.arange(S)

    def one_block(args):
        q_blk, blk = args
        t = blk * QB + jnp.arange(QB)
        p = masked_softmax(jnp.einsum('bqhcd,bkhcd->bhcqk', q_blk, k), kpos[None, :] <= t[:, None])
        a = p[:, :, 0] - lam * p[:, :, 1]
        return jnp.einsum('bhqk,bkhd->bqhd', a.astype(v.dtype), v)

    nqb = S // QB
    q_blocks = q.reshape(B, nqb, QB, H, 2, dh).transpose(1, 0, 2, 3, 4, 5)
    o = lax.map(one_block, (q_blocks, jnp.arange(nqb)))
    o = o.transpose(1, 0, 2, 3, 4).reshape(B, S, H, 2 * dh)
    o = rmsnorm(o, subln_w) * (1.0 - lambda_init)
    return o.reshape(B, S, D_MODEL) @ w_out

def memory_cross_attention(h, mem_n, wq, wkv, wo):
    B, S, _ = h.shape
    M = mem_n.shape[1]
    q = (h @ wq).reshape(B, S, MEM_HEADS, MEM_HEAD_DIM) * MEM_HEAD_DIM ** -0.5
    k, v = jnp.split(mem_n @ wkv, 2, axis=-1)
    k = k.reshape(B, M, MEM_HEADS, MEM_HEAD_DIM)
    v = v.reshape(B, M, MEM_HEADS, MEM_HEAD_DIM)
    p = jax.nn.softmax(jnp.einsum('bshd,bmhd->bhsm', q, k).astype(jnp.float32), axis=-1)
    o = jnp.einsum('bhsm,bmhd->bshd', p.astype(v.dtype), v)
    return o.reshape(B, S, D_MODEL) @ wo

def conv_ffn(h, w_up, conv_w, w_down):
    gate, val = jnp.split(h @ w_up, 2, axis=-1)
    return (jax.nn.silu(causal_dwconv(gate, conv_w)) * val) @ w_down

def first_inputs(seed: int = 0) -> dict:
    key = jax.random.key(seed)
    keys = iter(jax.random.split(key, 48))

    def nrm(shape, scale):
        return scale * jax.random.normal(next(keys), shape, jnp.float32)

    def gain(shape):
        return 1.0 + nrm(shape, 0.02)

    D = D_MODEL
    nA, nB, nC = N_LAYERS_NSA, N_LAYERS_GDN, N_LAYERS_DIFF
    dk = NSA_HEAD_DIM
    inp = {}
    inp['x'] = nrm((BATCH, SEQ, D), 1.0)
    inp['mem'] = nrm((BATCH, MEM_TOKENS, D), 1.0)
    inp['mem_norm_w'] = gain((D,))
    inp['final_norm_w'] = gain((D,))
    inp['norm_mix_w'] = gain((DEPTH, D))
    inp['norm_cross_w'] = gain((DEPTH, D))
    inp['norm_ffn_w'] = gain((DEPTH, D))
    inp['ca_wq'] = nrm((DEPTH, D, D), D ** -0.5)
    inp['ca_wkv'] = nrm((DEPTH, D, 2 * D), D ** -0.5)
    inp['ca_wo'] = nrm((DEPTH, D, D), D ** -0.5)
    inp['ffn_w_up'] = nrm((DEPTH, D, 2 * D_FF), D ** -0.5)
    inp['ffn_conv_w'] = nrm((DEPTH, FFN_CONV, D_FF), FFN_CONV ** -0.5)
    inp['ffn_w_down'] = nrm((DEPTH, D_FF, D), D_FF ** -0.5)
    inp['nsa_w_in'] = nrm((nA, D, NSA_IN_WIDTH), D ** -0.5)
    inp['nsa_pe_k'] = nrm((nA, CMP_BLOCK, dk), 0.02)
    inp['nsa_pe_v'] = nrm((nA, CMP_BLOCK, dk), 0.02)
    inp['nsa_ck_w1'] = nrm((nA, CMP_BLOCK * dk, CMP_HIDDEN), (CMP_BLOCK * dk) ** -0.5)
    inp['nsa_ck_w2'] = nrm((nA, CMP_HIDDEN, dk), CMP_HIDDEN ** -0.5)
    inp['nsa_cv_w1'] = nrm((nA, CMP_BLOCK * dk, CMP_HIDDEN), (CMP_BLOCK * dk) ** -0.5)
    inp['nsa_cv_w2'] = nrm((nA, CMP_HIDDEN, dk), CMP_HIDDEN ** -0.5)
    inp['nsa_w_out'] = nrm((nA, D, D), D ** -0.5)
    inp['gdn_w_in'] = nrm((nB, D, GDN_IN_WIDTH), D ** -0.5)
    inp['gdn_conv_w'] = nrm((nB, GDN_CONV, 3 * GDN_WIDTH), GDN_CONV ** -0.5)
    inp['gdn_a_log'] = jnp.log(jax.random.uniform(next(keys), (nB, GDN_HEADS), jnp.float32, 1.0, 16.0))
    dt = jnp.exp(jax.random.uniform(next(keys), (nB, GDN_HEADS), jnp.float32, math.log(1e-3), math.log(1e-1)))
    inp['gdn_dt_bias'] = dt + jnp.log(-jnp.expm1(-dt))
    inp['gdn_norm_w'] = gain((nB, GDN_HEAD_DIM))
    inp['gdn_w_out'] = nrm((nB, GDN_WIDTH, D), GDN_WIDTH ** -0.5)
    inp['diff_w_in'] = nrm((nC, D, DIFF_IN_WIDTH), D ** -0.5)
    inp['diff_lq1'] = nrm((nC, DIFF_HEAD_DIM), 0.1)
    inp['diff_lk1'] = nrm((nC, DIFF_HEAD_DIM), 0.1)
    inp['diff_lq2'] = nrm((nC, DIFF_HEAD_DIM), 0.1)
    inp['diff_lk2'] = nrm((nC, DIFF_HEAD_DIM), 0.1)
    inp['diff_subln_w'] = gain((nC, 2 * DIFF_HEAD_DIM))
    inp['diff_w_out'] = nrm((nC, D, D), D ** -0.5)
    return inp

def first_block(x, mem, mem_norm_w, final_norm_w, norm_mix_w, norm_cross_w, norm_ffn_w,
              ca_wq, ca_wkv, ca_wo, ffn_w_up, ffn_conv_w, ffn_w_down,
              nsa_w_in, nsa_pe_k, nsa_pe_v, nsa_ck_w1, nsa_ck_w2, nsa_cv_w1, nsa_cv_w2, nsa_w_out,
              gdn_w_in, gdn_conv_w, gdn_a_log, gdn_dt_bias, gdn_norm_w, gdn_w_out,
              diff_w_in, diff_lq1, diff_lk1, diff_lq2, diff_lk2, diff_subln_w, diff_w_out):
    mem_n = rmsnorm(mem, mem_norm_w)
    for i in range(DEPTH):
        kind, j = i % N_MIXERS, i // N_MIXERS
        h = rmsnorm(x, norm_mix_w[i])
        if kind == 0:
            y = nsa_mixer(h, nsa_w_in[j], nsa_pe_k[j], nsa_pe_v[j], nsa_ck_w1[j], nsa_ck_w2[j],
                          nsa_cv_w1[j], nsa_cv_w2[j], nsa_w_out[j])
        elif kind == 1:
            y = gdn_mixer(h, gdn_w_in[j], gdn_conv_w[j], gdn_a_log[j], gdn_dt_bias[j], gdn_norm_w[j], gdn_w_out[j])
        else:
            lambda_init = 0.8 - 0.6 * math.exp(-0.3 * i)
            y = diff_mixer(h, diff_w_in[j], diff_lq1[j], diff_lk1[j], diff_lq2[j], diff_lk2[j],
                           diff_subln_w[j], diff_w_out[j], lambda_init)
        x = x + y
        x = x + memory_cross_attention(rmsnorm(x, norm_cross_w[i]), mem_n, ca_wq[i], ca_wkv[i], ca_wo[i])
        x = x + conv_ffn(rmsnorm(x, norm_ffn_w[i]), ffn_w_up[i], ffn_conv_w[i], ffn_w_down[i])
    return rmsnorm(x, final_norm_w)


PLE_DIM = 256
ML_HEADS = 4
ML_DQK = 128
ML_DV = 256
ML_CONV = 4
ML_CHUNK = 64
SW_Q_HEADS = 16
SW_KV_HEADS = 4
SW_HEAD_DIM = 64
SW_WINDOW = 128
D_FF_2 = 4 * D_MODEL
EPS = 1e-6

ML_QK_W = ML_HEADS * ML_DQK
ML_V_W = ML_HEADS * ML_DV
SW_Q_W = SW_Q_HEADS * SW_HEAD_DIM
SW_KV_W = SW_KV_HEADS * SW_HEAD_DIM
SPLIT_SIZES = (2 * ML_QK_W, ML_V_W, ML_V_W, 2 * ML_HEADS, SW_Q_W, SW_KV_W, SW_KV_W, D_MODEL, D_MODEL)
N_IN = sum(SPLIT_SIZES)


def rmsnorm_2(x, g):
    xf = x.astype(jnp.float32)
    xf = xf * lax.rsqrt(jnp.mean(xf * xf, axis=-1, keepdims=True) + EPS)
    return xf.astype(x.dtype) * g.astype(x.dtype)

def causal_depthwise_conv(x, w):
    c = x.shape[-1]
    return lax.conv_general_dilated(
        x, w.astype(x.dtype)[:, None, :], window_strides=(1,), padding=((ML_CONV - 1, 0),),
        dimension_numbers=("NWC", "WIO", "NWC"), feature_group_count=c)

def mlstm_chunkwise(q, k, v, ig, lf):
    B, S = q.shape[:2]
    L = ML_CHUNK
    nc = S // L

    def to_chunks(t):
        t = t.astype(jnp.float32).reshape((B, nc, L) + t.shape[2:])
        return jnp.moveaxis(jnp.moveaxis(t, 1, 0), 3, 2)

    xs = (to_chunks(q), to_chunks(k), to_chunks(v), to_chunks(ig), to_chunks(lf))
    causal = jnp.tril(jnp.ones((L, L), dtype=bool))

    def step(carry, chunk):
        C, n, m = carry
        qc, kc, vc, ic, fc = chunk
        b = jnp.cumsum(fc, axis=-1)
        log_d = jnp.where(causal, b[..., :, None] - b[..., None, :] + ic[..., None, :], -jnp.inf)
        inter = b + m[..., None]
        m_t = jnp.maximum(inter, jnp.max(log_d, axis=-1))
        scores = jnp.einsum("bhtk,bhsk->bhts", qc, kc) * jnp.exp(log_d - m_t[..., None])
        w_inter = jnp.exp(inter - m_t)
        num = (w_inter[..., None] * jnp.einsum("bhvk,bhtk->bhtv", C, qc)
               + jnp.einsum("bhts,bhsv->bhtv", scores, vc))
        den = w_inter * jnp.einsum("bhk,bhtk->bht", n, qc) + jnp.sum(scores, axis=-1)
        h = num / jnp.maximum(jnp.abs(den), jnp.exp(-m_t))[..., None]
        b_last = b[..., -1]
        log_w = b_last[..., None] - b + ic
        m_new = jnp.maximum(b_last + m, jnp.max(log_w, axis=-1))
        w = jnp.exp(log_w - m_new[..., None])
        decay = jnp.exp(b_last + m - m_new)
        C_new = decay[..., None, None] * C + jnp.einsum("bhs,bhsv,bhsk->bhvk", w, vc, kc)
        n_new = decay[..., None] * n + jnp.einsum("bhs,bhsk->bhk", w, kc)
        return (C_new, n_new, m_new), h

    H, dk, dv = q.shape[2], q.shape[3], v.shape[3]
    init = (jnp.zeros((B, H, dv, dk), jnp.float32), jnp.zeros((B, H, dk), jnp.float32),
            jnp.zeros((B, H), jnp.float32))
    _, h = lax.scan(step, init, xs)
    h = jnp.moveaxis(jnp.moveaxis(h, 2, 3), 0, 1)
    return h.reshape(B, S, H, dv)

def swa_with_sinks(q, k, v, sinks):
    B, S = q.shape[:2]
    W = SW_WINDOW
    nb = S // W
    G = SW_Q_HEADS // SW_KV_HEADS
    qb = q.reshape(B, nb, W, SW_KV_HEADS, G, SW_HEAD_DIM)

    def band(t):
        tb = t.reshape(B, nb, W, SW_KV_HEADS, SW_HEAD_DIM)
        prev = jnp.pad(tb, ((0, 0), (1, 0), (0, 0), (0, 0), (0, 0)))[:, :-1]
        return jnp.concatenate([prev, tb], axis=2)

    kb, vb = band(k), band(v)
    logits = jnp.einsum("bnqhgd,bnkhd->bnhgqk", qb, kb).astype(jnp.float32) * (SW_HEAD_DIM ** -0.5)
    qi = jnp.arange(W)[:, None]
    ki = jnp.arange(2 * W)[None, :]
    diff = qi + W - ki
    band_mask = (diff >= 0) & (diff < W)
    valid = band_mask[None] & ((jnp.arange(nb)[:, None, None] > 0) | (ki >= W)[None])
    logits = jnp.where(valid[None, :, None, None], logits, -jnp.inf)
    sink = sinks.astype(jnp.float32).reshape(SW_KV_HEADS, G)[None, None, :, :, None, None]
    m = jnp.maximum(jnp.max(logits, axis=-1, keepdims=True), sink)
    pexp = jnp.exp(logits - m)
    probs = pexp / (jnp.sum(pexp, axis=-1, keepdims=True) + jnp.exp(sink - m))
    out = jnp.einsum("bnhgqk,bnkhd->bnqhgd", probs.astype(v.dtype), vb)
    return out.reshape(B, S, SW_Q_W)

def second_inputs(seed: int = 0) -> dict:
    key = jax.random.key(seed)
    ks = jax.random.split(key, 20)
    f32 = jnp.float32
    nrm = lambda k, shape, s: jax.random.normal(k, shape, f32) * s
    gain = lambda k, shape: 1.0 + 0.05 * jax.random.normal(k, shape, f32)
    b_if = jnp.concatenate([
        0.1 * jax.random.normal(ks[3], (DEPTH, ML_HEADS), f32),
        3.0 + 0.5 * jax.random.normal(ks[4], (DEPTH, ML_HEADS), f32),
    ], axis=-1)
    return {
        "x": jax.random.normal(ks[0], (BATCH, SEQ, D_MODEL), f32),
        "p": jax.random.normal(ks[1], (DEPTH, BATCH, SEQ, PLE_DIM), f32),
        "norm_mix_g": gain(ks[2], (DEPTH, D_MODEL)),
        "w_in": nrm(ks[5], (DEPTH, D_MODEL, N_IN), D_MODEL ** -0.5),
        "conv_qk": nrm(ks[6], (DEPTH, ML_CONV, 2 * ML_QK_W), ML_CONV ** -0.5),
        "b_if": b_if,
        "mlstm_norm_g": gain(ks[7], (DEPTH, ML_V_W)),
        "sinks": nrm(ks[8], (DEPTH, SW_Q_HEADS), 0.5),
        "w_branch_a": nrm(ks[9], (DEPTH, ML_V_W, D_MODEL), ML_V_W ** -0.5),
        "w_branch_b": nrm(ks[10], (DEPTH, SW_Q_W, D_MODEL), SW_Q_W ** -0.5),
        "w_out": nrm(ks[11], (DEPTH, D_MODEL, D_MODEL), D_MODEL ** -0.5),
        "norm_mlp_g": gain(ks[12], (DEPTH, D_MODEL)),
        "w_up": nrm(ks[13], (DEPTH, D_MODEL, D_FF_2), D_MODEL ** -0.5),
        "w_down": nrm(ks[14], (DEPTH, D_FF_2, D_MODEL), D_FF_2 ** -0.5),
        "norm_ple_g": gain(ks[15], (DEPTH, D_MODEL)),
        "w_ple_gate": nrm(ks[16], (DEPTH, D_MODEL, D_MODEL), D_MODEL ** -0.5),
        "w_ple_proj": nrm(ks[17], (DEPTH, PLE_DIM, D_MODEL), PLE_DIM ** -0.5),
        "final_norm_g": gain(ks[18], (D_MODEL,)),
    }

def second_block(x, p, norm_mix_g, w_in, conv_qk, b_if, mlstm_norm_g, sinks, w_branch_a, w_branch_b,
              w_out, norm_mlp_g, w_up, w_down, norm_ple_g, w_ple_gate, w_ple_proj, final_norm_g):
    B, S, _ = x.shape
    split_idx = [int(v) for v in np.cumsum(SPLIT_SIZES)[:-1]]
    for i in range(DEPTH):
        h = rmsnorm_2(x, norm_mix_g[i])
        proj = h @ w_in[i]
        qk_ml, v_ml, o_ml, if_pre, q_sw, k_sw, v_sw, g_a, g_b = jnp.split(proj, split_idx, axis=-1)

        qk_ml = jax.nn.silu(causal_depthwise_conv(qk_ml, conv_qk[i]))
        q_ml, k_ml = jnp.split(qk_ml, 2, axis=-1)
        q_ml = q_ml.reshape(B, S, ML_HEADS, ML_DQK) * (ML_DQK ** -0.5)
        k_ml = k_ml.reshape(B, S, ML_HEADS, ML_DQK)
        gates = (if_pre + b_if[i].astype(if_pre.dtype)).astype(jnp.float32)
        ig = gates[..., :ML_HEADS]
        lf = jax.nn.log_sigmoid(gates[..., ML_HEADS:])
        h_ml = mlstm_chunkwise(q_ml, k_ml, v_ml.reshape(B, S, ML_HEADS, ML_DV), ig, lf)
        h_ml = h_ml * lax.rsqrt(jnp.mean(h_ml * h_ml, axis=-1, keepdims=True) + EPS)
        h_ml = h_ml.reshape(B, S, ML_V_W).astype(x.dtype) * mlstm_norm_g[i].astype(x.dtype)
        y_a = jax.nn.sigmoid(o_ml) * h_ml

        y_b = swa_with_sinks(q_sw.reshape(B, S, SW_Q_HEADS, SW_HEAD_DIM),
                             k_sw.reshape(B, S, SW_KV_HEADS, SW_HEAD_DIM),
                             v_sw.reshape(B, S, SW_KV_HEADS, SW_HEAD_DIM), sinks[i])

        merged = jax.nn.sigmoid(g_a) * (y_a @ w_branch_a[i]) + jax.nn.sigmoid(g_b) * (y_b @ w_branch_b[i])
        x = x + merged @ w_out[i]

        u = rmsnorm_2(x, norm_mlp_g[i]) @ w_up[i]
        x = x + jnp.square(jax.nn.relu(u)) @ w_down[i]

        gate = jax.nn.sigmoid(rmsnorm_2(x, norm_ple_g[i]) @ w_ple_gate[i])
        x = x + gate * (p[i].astype(x.dtype) @ w_ple_proj[i])
    return rmsnorm_2(x, final_norm_g)


def setup_inputs(seed=0):
    out = dict(first_inputs(seed))
    for name, value in second_inputs(seed + 1).items():
        if name != "x":
            out[name + "_2"] = value
    return out


def reference(
    x, mem, mem_norm_w, final_norm_w, norm_mix_w, norm_cross_w, norm_ffn_w, ca_wq, ca_wkv,
    ca_wo, ffn_w_up, ffn_conv_w, ffn_w_down, nsa_w_in, nsa_pe_k, nsa_pe_v, nsa_ck_w1, nsa_ck_w2,
    nsa_cv_w1, nsa_cv_w2, nsa_w_out, gdn_w_in, gdn_conv_w, gdn_a_log, gdn_dt_bias, gdn_norm_w,
    gdn_w_out, diff_w_in, diff_lq1, diff_lk1, diff_lq2, diff_lk2, diff_subln_w, diff_w_out, p_2,
    norm_mix_g_2, w_in_2, conv_qk_2, b_if_2, mlstm_norm_g_2, sinks_2, w_branch_a_2,
    w_branch_b_2, w_out_2, norm_mlp_g_2, w_up_2, w_down_2, norm_ple_g_2, w_ple_gate_2,
    w_ple_proj_2, final_norm_g_2,
):
    x = first_block(
        x, mem, mem_norm_w, final_norm_w, norm_mix_w, norm_cross_w, norm_ffn_w, ca_wq, ca_wkv,
        ca_wo, ffn_w_up, ffn_conv_w, ffn_w_down, nsa_w_in, nsa_pe_k, nsa_pe_v, nsa_ck_w1,
        nsa_ck_w2, nsa_cv_w1, nsa_cv_w2, nsa_w_out, gdn_w_in, gdn_conv_w, gdn_a_log,
        gdn_dt_bias, gdn_norm_w, gdn_w_out, diff_w_in, diff_lq1, diff_lk1, diff_lq2, diff_lk2,
        diff_subln_w, diff_w_out,
    )
    return second_block(
        x, p_2, norm_mix_g_2, w_in_2, conv_qk_2, b_if_2, mlstm_norm_g_2, sinks_2, w_branch_a_2,
        w_branch_b_2, w_out_2, norm_mlp_g_2, w_up_2, w_down_2, norm_ple_g_2, w_ple_gate_2,
        w_ple_proj_2, final_norm_g_2,
    )


_drawn_inputs = setup_inputs


def setup_inputs(seed=0):
    import zlib

    import numpy as np

    out = dict(_drawn_inputs(seed))
    spreads = {}
    factors = {'mem_norm_w': 8.0,
     'final_norm_w': 2.679,
     'norm_mix_w': 8.0,
     'norm_cross_w': 8.0,
     'norm_ffn_w': 9.898,
     'nsa_pe_k': 8.0,
     'nsa_pe_v': 6.961,
     'mlstm_norm_g_2': 10.834,
     'sinks_2': 140.239,
     'norm_ple_g_2': 143.767,
     'norm_mlp_g_2': 3.297}
    for name, (base, spread) in spreads.items():
        noise = np.random.default_rng([zlib.crc32(name.encode()), seed]).standard_normal(out[name].shape)
        drawn = base * np.exp(spread * noise) if base else spread * noise
        out[name] = __import__('jax').numpy.asarray(drawn.astype(out[name].dtype))
    for name, factor in factors.items():
        out[name] = (out[name] * factor).astype(out[name].dtype)
    return out
```

```python
from contextlib import ExitStack

import concourse.bass as bass
from concourse import mybir
import numpy as np

F32 = mybir.dt.float32
BF16 = mybir.dt.bfloat16
ALU = mybir.AluOpType
ACT = mybir.ActivationFunctionType
AX_X = mybir.AxisListType.X

P = 128
S = 512
D = 1024
KD = D // P
NT = S // P
MEM = 256
FF = 2816
FC = FF // P
F2 = 4096
F2C = F2 // P
PLE = 256
PANEL = 16 * P
EPS = 1e-6
NEG = -1e30

HD = 64
G = 4
PAIRS = 8
NCMP = 31
CMPW = G * NCMP
MLH = 4

NORMS = ["mem", "mix", "cross", "ffn", "final", "mix2", "mlp2", "ple2", "final2", "mlstm"]
COL = {name: 8 * i for i, name in enumerate(NORMS)}
COL["ffn_conv"] = 80
COL["ml_conv"] = COL["ffn_conv"] + 3 * FC
COL["pe_k"] = COL["ml_conv"] + 4 * 8
COL["pe_v"] = COL["pe_k"] + 16
COL["sink"] = COL["pe_v"] + 16
COL["b_i"] = COL["sink"] + 16
COL["b_f"] = COL["b_i"] + 1
NPAR = COL["b_f"] + 1

PHASES = [
    ("mem_k", 2, 4), ("mem_v", 2, 2),
    ("nsa_v", 1, 4), ("nsa_g", 0, 4), ("cmp_kv", 1, 4), ("nsa_k", 1, 4), ("cmp_w1", 2, 2), ("cmp_w2", 0, 2),
    ("nsa_q", 2, 4), ("nsa_out", 2, 4),
    ("ca_q", 2, 4), ("ca_out", 2, 4),
    ("ffn_up", FC // 2, 4), ("ffn_down", 8, 1),
    ("ml_qk", 2, 4), ("ml_v", 2, 4), ("ml_o", 2, 4), ("ml_if", 0, 2), ("merge_a", 4, 4),
    ("sw_q", 2, 4), ("sw_kv", 1, 6), ("merge_b", 4, 4), ("mix_out", 2, 4),
    ("mlp_up", F2C // 4, 4), ("mlp_down", 8, 1),
    ("ple", 4, 4),
]
WIDTH = {"ffn_down": FC // 2 * P, "ple": (KD + PLE // P) * P}
ML_AT = [0, 512, 896, 1152]
GATED = {"ffn": FC, "ml": FC + 8, "mlp": FC + 8 + F2C}
PAIR0, TILE0 = {}, {}
_r, _t = 0, 2
for _name, _pairs, _tiles in PHASES:
    PAIR0[_name], TILE0[_name] = _r, _t
    _r += _pairs
    _t += max(_pairs, 1) * _tiles
NPAIRS, NTILES = _r, _t


def loop(engine, n):
    from contextlib import nullcontext
    return engine.Fori(0, n) if n > 1 else nullcontext(0)


def cols(buf, first, n=S):
    return buf[:, bass.ds(first, n)]


class Count:

    def __init__(self, sem):
        self.sem, self.n, self.i, self.per = sem, 0, 0, 0

    def enter(self, i, per):
        self.i, self.per, self.start = i, per, self.n

    def leave(self, steps):
        assert self.n - self.start == self.per, (self.n - self.start, self.per)
        self.n = self.start + steps * self.per
        self.i, self.per = 0, 0

    @property
    def at(self):
        return self.n + self.per * self.i if self.per else self.n


def nsa_units():
    units = []
    for qt in range(NT):
        units.append(dict(qt=qt, br=0, k0=0, nk=NCMP, first=True, last=False))
        units.append(dict(qt=qt, br=1, k0=0, nk=(qt + 1) * P, first=False, last=False))
        units.append(dict(qt=qt, br=2, k0=0, nk=(qt + 1) * P, first=False, last=qt == NT - 1))
    return units


def sw_units():
    return [dict(qt=qt, br=0, k0=max(qt - 1, 0) * P, nk=P if qt == 0 else 2 * P, first=True, last=qt == NT - 1)
            for qt in range(NT)]


def ca_units():
    return [dict(qt=qt, hp=hp, nk=MEM, first=True, last=True) for hp in range(2) for qt in range(NT)]


def program(nc, a, out):
    with ExitStack() as ctx:
        def sb(name, shape, dt=F32):
            return ctx.enter_context(nc.sbuf_tensor(name, shape, dt))

        def sem(name):
            return ctx.enter_context(nc.semaphore(name))

        xt = sb("xt", [P, KD * S])
        ht = sb("ht", [P, KD * S])
        ring = sb("ring", [P, 2 * PANEL])
        big = sb("big", [P, 32 * S])
        memk = sb("memk", [P, KD * MEM])
        memv = sb("memv", [P, 2 * D])
        params = sb("params", [P, NPAR])
        w_gate = sb("w_gate", [P, KD * 48])
        w_if = sb("w_if", [P, KD * 8])
        w2_k = sb("w2_k", [P, 2 * P])
        w2_v = sb("w2_v", [P, 2 * HD])
        ident = sb("ident", [P, P])
        ones = sb("ones", [P, P])
        ident_bf = sb("ident_bf", [P, P], BF16)
        causal = sb("causal", [P, P], BF16)
        band = sb("band", [P, 2 * P], BF16)
        cmp_mask = sb("cmp_mask", [P, NT * NCMP], BF16)
        cmp_any = sb("cmp_any", [P, NT])
        ml_mask = sb("ml_mask", [P, P])
        select = sb("select", [MLH, MLH * P])
        eps = sb("eps", [P, 1])
        start = sb("start", [P, 3])
        acc = sb("acc", [P, S])
        sqt = sb("sqt", [P, S])
        std = sb("std", [P, S])
        rstd = sb("rstd", [P, S])
        tmp = sb("tmp", [P, 2 * S])
        act_o = sb("act_o", [P, 2 * S])
        gates = sb("gates", [P, NT * 48])
        hid = sb("hid", [P, 2 * 2 * CMPW])
        kcmp = sb("kcmp", [P, CMPW])
        vcmp = sb("vcmp", [NCMP, G * HD])
        probs = sb("probs", [P, 2 * 2 * S])
        probs_t = sb("probs_t", [P, 2 * 2 * S])
        q_st = sb("q_st", [P, 2 * S])
        o_acc = sb("o_acc", [P, 2 * S])
        negmax = sb("negmax", [P, 4])
        total = sb("total", [P, 4])
        coef = sb("coef", [P, 8])
        sink_arg = sb("sink_arg", [P, 4])
        sink_e = sb("sink_e", [P, 4])
        neg_sink = sb("neg_sink", [P, 16])
        ig = sb("ig", [MLH, S])
        fz = sb("fz", [MLH, S])
        fe = sb("fe", [MLH, S])
        fcum = sb("fcum", [MLH, S])
        u_row = sb("u_row", [MLH, S])
        m_row = sb("m_row", [MLH, S])
        nm_row = sb("nm_row", [MLH, S])
        u_col = sb("u_col", [P, NT * MLH])

        psum = ctx.enter_context(nc.psum_tensor("psum", [P, 8, S], F32))

        def bank(b, n=S):
            return psum[:, b, 0:n]

        def chunk(i):
            return big[:, i * S:(i + 1) * S]

        w_full = [sem("w_full0"), sem("w_full1")]
        tile_done = sem("tile_done")
        evac = [sem("evac0"), sem("evac1")]
        x_in, mem_in, par_in, small_in, ple_in = (sem(n) for n in ("x_in", "mem_in", "par_in", "small_in", "ple_in"))
        consts = sem("consts")
        dve_step, pool_step = sem("dve_step"), sem("pool_step")
        squares = sem("squares")
        stat = sem("stat")
        std_done = sem("std_done")
        normed = sem("normed")
        shifted = sem("shifted")
        blocks = sem("blocks")
        conv_done = sem("conv_done")
        gated = sem("gated")
        ml_step = {n: sem("ml_" + n) for n in (
            "u_col", "z", "e", "l", "rows", "bc", "bc_used", "scores", "decay", "weighted", "sums", "recip", "h",
            "sq", "ssq", "std", "y")}
        att = {}
        for name in ("nsa", "ca", "sw"):
            att[name] = {n: sem(f"{name}_{n}") for n in (
                "staged", "scores", "negmax", "probs", "transposed", "copied_a", "copied_d", "summed",
                "combined", "turned", "stored")}
        merged = sem("merged")
        stored = sem("stored")

        def tiles(name, i, k):
            per = dict((n, t) for n, _, t in PHASES)[name]
            return TILE0[name] + per * i + k

        def half(name, i, k):
            per = dict((n, t) for n, _, t in PHASES)[name]
            assert per % 2 == 0
            return TILE0[name] // 2 + (per // 2) * i + k // 2

        block = ctx.enter_context(nc.Block())

        NU = len(nsa_units())
        def att_dims(name):
            return {"nsa": (PAIRS // 2, 2, NU), "sw": (PAIRS // 2, 2, NT), "ca": (1, 2 * NT, 1)}[name]

        @block.sync
        def _(sp):
            sp.dma_start(big[:, 0:KD * MEM], a["mem"]).then_inc(mem_in, 16)
            before = None
            for name, pairs, per in PHASES:
                if not pairs:
                    continue
                width = WIDTH.get(name, PANEL)
                r0 = PAIR0[name]
                frees = {"mem_v": (2, 2), "nsa_v": (4, 4), "cmp_w1": (2, 2), "ml_v": (4, 4), "ffn_down": (1, 1),
                         "mlp_down": (1, 1), "sw_kv": (2, 6)}.get(name, (2, 4))
                for j in range(2):
                    if before is not None:
                        sp.wait_ge(tile_done, before[j])
                    sp.dma_start(ring[:, j * PANEL:j * PANEL + width], a["panels"][2 * r0 + j, :, 0:width]) \
                        .then_inc(w_full[j], 16)
                if name == "mem_k":
                    sp.dma_start(xt[:, :], a["x"]).then_inc(x_in, 16)
                if name == "ple":
                    sp.wait_ge(tile_done, TILE0["mlp_down"] + 8)
                    sp.dma_start(big[:, 0:2 * S], a["ple"]).then_inc(ple_in, 16)
                if pairs > 1:
                    with sp.Fori(0, pairs - 1) as i:
                        for j in range(2):
                            sp.wait_ge(tile_done, TILE0[name] + frees[j] + per * i)
                            sp.dma_start(ring[:, j * PANEL:j * PANEL + width],
                                         a["panels"][2 * r0 + 2 + 2 * i + j, :, 0:width]).then_inc(w_full[j], 16)
                before = [TILE0[name] + per * (pairs - 1) + f for f in frees]
            for c in range(KD):
                sp.wait_ge(normed, 8 * 8 + c + 1)
                sp.dma_start(out[:, c * S:(c + 1) * S], ht[:, c * S:(c + 1) * S]).then_inc(stored, 16)
            sp.wait_ge(stored, 16 * KD)

        @block.tensor
        def _(pe):
            def mm(o, l, r, start, stop, **kw):
                return nc.tensor.matmul(o, l, r, start=start, stop=stop, **kw)

            def weights_here(name, i, j):
                pe.wait_ge(w_full[j], 16 * (PAIR0[name] + 1) + 16 * i)

            def bank_free(name, i, k):
                pe.wait_ge(evac[k % 2], half(name, i, k))

            def product(name, pairs, rhs, n=S, fresh=None):
                with loop(pe, pairs) as i:
                    for j in range(2):
                        weights_here(name, i, j)
                        for t in range(2):
                            bank_free(name, i, 2 * j + t)
                            for k in range(KD):
                                if fresh is not None and j == 0 and t == 0:
                                    pe.wait_ge(normed, 8 * fresh + k + 1)
                                w0 = j * PANEL + (t * KD + k) * P
                                last = mm(bank(t, n), ring[:, w0:w0 + P], rhs(k), k == 0, k == KD - 1)
                            last.then_inc(tile_done, 1)

            def product_tokens(name, pairs, lhs, tiles_, fresh=None):
                with loop(pe, pairs) as i:
                    for j in range(2):
                        weights_here(name, i, j)
                    for t in range(tiles_):
                        bank_free(name, i, t)
                        for k in range(KD):
                            if fresh is not None and t == 0:
                                pe.wait_ge(normed, 8 * fresh + k + 1)
                            last = mm(bank(t % 2), lhs(k, t), ring[:, k * S:(k + 1) * S], k == 0, k == KD - 1)
                        last.then_inc(tile_done, 1)

            def product_down(name, k_panel, pairs):
                with loop(pe, pairs // 2) as i:
                    for t in range(2):
                        pe.wait_ge(evac[t], TILE0[name] // 2 + i)
                        for j in range(2):
                            pe.wait_ge(w_full[j], 16 * (PAIR0[name] + 1 + t) + 32 * i)
                            for k in range(k_panel):
                                last = mm(bank(t), ring[:, j * PANEL + k * P:j * PANEL + (k + 1) * P],
                                          chunk(j * k_panel + k), j == 0 and k == 0, j == 1 and k == k_panel - 1)
                        last.then_inc(tile_done, 1)

            def partition_sum(m, b, n=S):
                pe.wait_ge(squares, KD * (m + 1))
                mm(bank(b, n), ones[:, :], acc[:, 0:n], True, True).then_inc(stat, 1)

            def attention(name, qk, mask, pv, units):
                s = att[name]
                steps, groups, per = att_dims(name)
                flat = [u for _ in range(groups) for u in units] if name != "ca" else units
                n_units = len(flat)
                with loop(pe, steps) as i:
                    u0 = n_units * i

                    def scores(u):
                        g = u // per
                        if u % per == 0 and name != "ca":
                            pe.wait_ge(s["staged"], groups * i + g + 1)
                        if u >= 2:
                            pe.wait_ge(s["probs"], u0 + (u - 1))
                        for hd in range(2):
                            ops = qk(flat[u], g % 2, hd)
                            b = 2 + 2 * (u % 2) + hd
                            m = mask(flat[u])
                            for n, (l, r) in enumerate(ops):
                                last = mm(bank(b, flat[u]["nk"]), l, r, n == 0, m is None and n == len(ops) - 1)
                            if m is not None:
                                c0 = flat[u]["nk"] - m.shape[1]
                                last = mm(psum[:, b, c0:flat[u]["nk"]], ident_bf[:, :], m, False, True)
                        last.then_inc(s["scores"], 1)

                    def transposes(u):
                        pe.wait_ge(s["probs"], u0 + (u + 1))
                        if u >= 1:
                            pe.wait_ge(s["copied_a"], u0 + u)
                            pe.wait_ge(s["copied_d"], u0 + u)
                        nk = flat[u]["nk"]
                        for hd in range(2):
                            for k in range(0, nk, P):
                                w = min(P, nk - k)
                                p0 = (2 * (u % 2) + hd) * S + k
                                last = nc.tensor.transpose(psum[0:w, 6 + hd, k:k + P], probs[:, p0:p0 + w], ident[:, :])
                        last.then_inc(s["transposed"], 1)

                    def values(u):
                        g = u // per
                        pe.wait_ge(s["copied_a"], u0 + (u + 1))
                        pe.wait_ge(s["copied_d"], u0 + (u + 1))
                        if u >= 1:
                            pe.wait_ge(s["combined"], u0 + u)
                        for hd in range(2):
                            ops, o0, ow = pv(flat[u], g % 2, hd, u % 2)
                            for n, (l, r) in enumerate(ops):
                                last = mm(psum[:, 0, o0:o0 + ow], l, r, n == 0, n == len(ops) - 1)
                        last.then_inc(s["summed"], 1)

                    def turn(g):
                        pe.wait_ge(s["combined"], u0 + per * (g + 1))
                        if g:
                            pe.wait_ge(s["stored"], groups * i + g)
                        for t in range(NT):
                            o0 = (g % 2) * S + t * P
                            last = nc.tensor.transpose(psum[:, 1, t * P:(t + 1) * P], o_acc[:, o0:o0 + P], ident[:, :])
                        last.then_inc(s["turned"], 1)

                    scores(0)
                    for u in range(n_units):
                        if u + 1 < n_units:
                            scores(u + 1)
                        if u >= 1:
                            values(u - 1)
                        if u >= 2 and flat[u - 2]["last"]:
                            turn((u - 2) // per)
                        transposes(u)
                    values(n_units - 1)
                    if n_units > 1 and flat[n_units - 2]["last"]:
                        turn((n_units - 2) // per)
                    turn(groups - 1)

            pe.wait_ge(consts, 1)
            partition_sum(0, 2, MEM)
            partition_sum(1, 3)
            product("mem_k", 2, lambda k: big[:, (KD + k) * MEM:(KD + k + 1) * MEM], MEM, fresh=0)
            product_tokens("mem_v", 2, lambda k, t: big[:, (KD + k) * MEM + t * P:(KD + k) * MEM + (t + 1) * P], 2)
            hk = lambda k: ht[:, k * S:(k + 1) * S]
            htok = lambda k, t: ht[:, k * S + t * P:k * S + (t + 1) * P]
            product_tokens("nsa_v", 1, htok, 4, fresh=1)
            pe.wait_ge(small_in, 64)
            for t in range(NT):
                bank_free("nsa_g", 0, t)
                for k in range(KD):
                    last = mm(bank(t % 2, 48), htok(k, t), w_gate[:, k * 48:(k + 1) * 48], k == 0, k == KD - 1)
                last.then_inc(tile_done, 1)
            product("cmp_kv", 1, hk)
            product("nsa_k", 1, hk)
            with pe.Fori(0, 2) as i:
                pe.wait_ge(blocks, 16 * i + 16)
                for t in range(2):
                    bank_free("cmp_w1", i, t)
                    for j in range(2):
                        if t == 0:
                            weights_here("cmp_w1", i, j)
                        for k in range(8):
                            w0 = j * PANEL + k * 2 * P + t * P
                            last = mm(bank(t, CMPW), ring[:, w0:w0 + P],
                                      cols(big, i * (4 * S) + 24 * S + (8 * j + k) * CMPW, CMPW),
                                      j == 0 and k == 0, j == 1 and k == 7)
                    last.then_inc(tile_done, 1)
            pe.wait_ge(evac[0], half("cmp_w2", 0, 0))
            pe.wait_ge(evac[1], half("cmp_w2", 0, 0))
            for k in range(2):
                last = mm(bank(0, CMPW), w2_k[:, k * P:(k + 1) * P], hid[:, k * CMPW:(k + 1) * CMPW], k == 0, k == 1)
            last.then_inc(tile_done, 1)
            for g in range(G):
                for k in range(2):
                    h0 = (2 + k) * CMPW + g * NCMP
                    last = mm(psum[0:NCMP, 1, g * HD:(g + 1) * HD], hid[:, h0:h0 + NCMP],
                              w2_v[:, k * HD:(k + 1) * HD], k == 0, k == 1)
            last.then_inc(tile_done, 1)
            product("nsa_q", 2, hk)

            def nsa_qk(u, par, hd):
                rows = slice(64 * hd, 64 * hd + 64)
                q = q_st[rows, par * S + u["qt"] * P:par * S + (u["qt"] + 1) * P]
                if u["br"] == 0:
                    k0 = (2 * par + hd) * NCMP
                    return [(q, kcmp[rows, k0:k0 + NCMP])]
                k0 = (8 + 2 * (u["br"] - 1) + par) * S
                return [(q, big[rows, k0:k0 + u["nk"]])]

            def nsa_mask(u):
                return cmp_mask[:, u["qt"] * NCMP:(u["qt"] + 1) * NCMP] if u["br"] == 0 else causal[:, :]

            def nsa_pv(u, par, hd, up):
                p0 = (2 * up + hd) * S
                if u["br"] == 0:
                    v0 = (2 * par + hd) * HD
                    return [(probs_t[0:NCMP, p0:p0 + P], vcmp[:, v0:v0 + HD])], hd * HD, HD
                ops = []
                for kt in range(u["nk"] // P):
                    v0 = (12 + kt) * S + (u["br"] - 1) * 256 + (2 * par + hd) * HD
                    ops.append((probs_t[:, p0 + kt * P:p0 + (kt + 1) * P], big[:, v0:v0 + HD]))
                return ops, hd * HD, HD

            attention("nsa", nsa_qk, nsa_mask, nsa_pv, nsa_units())
            pe.wait_ge(att["nsa"]["stored"], PAIRS)
            product("nsa_out", 2, hk)
            partition_sum(2, 2)
            product("ca_q", 2, hk, fresh=2)

            def ca_qk(u, par, hd):
                h = 2 * u["hp"] + hd
                return [(big[:, (2 * h + c) * S + u["qt"] * P:(2 * h + c) * S + (u["qt"] + 1) * P],
                         memk[:, (2 * h + c) * MEM:(2 * h + c + 1) * MEM]) for c in range(2)]

            def ca_pv(u, par, hd, up):
                h = 2 * u["hp"] + hd
                p0 = (2 * up + hd) * S
                return [(probs_t[:, p0 + kt * P:p0 + (kt + 1) * P],
                         memv[:, kt * D + h * 256:kt * D + (h + 1) * 256]) for kt in range(2)], hd * 256, 256

            pe.wait_ge(evac[0], half("ca_out", 0, 0))
            pe.wait_ge(evac[1], half("ca_out", 0, 0))
            attention("ca", ca_qk, lambda u: None, ca_pv, ca_units())
            pe.wait_ge(att["ca"]["stored"], 2 * NT)
            product("ca_out", 2, hk)
            partition_sum(3, 2)
            product("ffn_up", FC // 2, hk, fresh=3)
            pe.wait_ge(evac[1], TILE0["ffn_down"] // 2)
            product_down("ffn_down", 11, 8)
            partition_sum(4, 2)
            partition_sum(5, 2)
            product("ml_qk", 2, hk, fresh=5)
            product_tokens("ml_v", 2, htok, 4)
            product("ml_o", 2, hk)
            for t in range(2):
                bank_free("ml_if", 0, t)
                for k in range(KD):
                    last = mm(psum[0:MLH, t, :], w_if[:, k * 8 + 4 * t:k * 8 + 4 * t + 4], hk(k), k == 0, k == KD - 1)
                last.then_inc(tile_done, 1)
            ml = ml_step
            pe.wait_ge(ml["rows"], 5)
            for st in range(NT):
                last = mm(psum[:, 2, st * MLH:(st + 1) * MLH], u_row[:, st * P:(st + 1) * P], ident[0:MLH, 0:MLH],
                          True, True)
            last.then_inc(ml["u_col"], 1)
            pe.wait_ge(ml["u_col"], 2)
            for t in range(2):
                pe.wait_ge(evac[t], TILE0["merge_a"] // 2)
            for h in range(MLH):
                if h:
                    pe.wait_ge(ml["recip"], 3 * h)
                    pe.wait_ge(ml["std"], h)
                mm(bank(6), select[:, h * P:(h + 1) * P], m_row[:, :], True, True)
                mm(bank(7), select[:, h * P:(h + 1) * P], nm_row[:, :], True, True).then_inc(ml["bc"], 1)
                for st in range(NT):
                    mm(psum[:, 2 + st, 0:S - st * P], big[:, (4 + h) * S + st * P:(4 + h) * S + (st + 1) * P],
                       big[:, h * S + st * P:(h + 1) * S], True, True).then_inc(ml["scores"], 1)
                pe.wait_ge(ml["bc_used"], 2 * (h + 1))
                if h:
                    pe.wait_ge(ml["h"], 2 * h)
                for st in range(NT):
                    pe.wait_ge(ml["weighted"], NT * h + st + 1)
                    pt = probs_t[:, ML_AT[st]:ML_AT[st] + S - st * P]
                    for dv in range(2):
                        v0 = (8 * S) + st * D + h * 256 + dv * P
                        mm(psum[:, dv, st * P:S], big[:, v0:v0 + P], pt, st == 0, st == NT - 1)
                    last = mm(psum[:, 6, st * P:S], ones[:, :], pt, st == 0, st == NT - 1)
                last.then_inc(ml["sums"], 1)
                pe.wait_ge(ml["sq"], 2 * h + 2)
                for dv in range(2):
                    last = mm(bank(7), ones[:, :], chunk(28 + dv), dv == 0, dv == 1)
                last.then_inc(ml["ssq"], 1)
            pe.wait_ge(ml["y"], 2 * MLH)

            def merge(name, rhs, k1=KD, fresh=None):
                with pe.Fori(0, 4) as i:
                    for j in range(2):
                        weights_here(name, i, j)
                        for t in range(2):
                            bank_free(name, i, 2 * j + t)
                            n_k = KD if t == 0 else k1
                            for k in range(n_k):
                                if fresh is not None and j == 0 and t == 0:
                                    pe.wait_ge(normed, 8 * fresh + k + 1)
                                w0 = j * PANEL + (t * KD + k) * P
                                last = mm(bank(t), ring[:, w0:w0 + P], hk(k) if t == 0 else rhs(k),
                                          k == 0, k == n_k - 1)
                            last.then_inc(tile_done, 1)

            merge("merge_a", lambda k: chunk(16 + k))
            product("sw_q", 2, hk)
            for j in range(2):
                weights_here("sw_kv", 0, j)
                for t in range(2 if j == 0 else NT):
                    bank_free("sw_kv", 0, t + 2 * j)
                    for k in range(KD):
                        if j == 0:
                            w0 = (t * KD + k) * P
                            last = mm(bank(t), ring[:, w0:w0 + P], hk(k), k == 0, k == KD - 1)
                        else:
                            w0 = PANEL + k * 256
                            last = mm(bank(t % 2, 256), htok(k, t), ring[:, w0:w0 + 256], k == 0, k == KD - 1)
                    last.then_inc(tile_done, 1)

            def sw_qk(u, par, hd):
                rows = slice(64 * hd, 64 * hd + 64)
                q = q_st[rows, par * S + u["qt"] * P:par * S + (u["qt"] + 1) * P]
                k0 = (24 + par) * S + u["k0"]
                return [(q, big[rows, k0:k0 + u["nk"]])]

            def sw_mask(u):
                return causal[:, :] if u["qt"] == 0 else band[:, :]

            def sw_pv(u, par, hd, up):
                p0 = (2 * up + hd) * S
                ops = []
                for n in range(u["nk"] // P):
                    v0 = 26 * S + (u["k0"] // P + n) * 256 + (2 * par + hd) * HD
                    ops.append((probs_t[:, p0 + n * P:p0 + (n + 1) * P], big[:, v0:v0 + HD]))
                return ops, hd * HD, HD

            attention("sw", sw_qk, sw_mask, sw_pv, sw_units())
            pe.wait_ge(att["sw"]["stored"], PAIRS)
            merge("merge_b", lambda k: chunk(16 + k))
            pe.wait_ge(merged, KD)
            product("mix_out", 2, lambda k: chunk(k))
            partition_sum(6, 2)
            product("mlp_up", F2C // 4, hk, fresh=6)
            pe.wait_ge(gated, GATED["mlp"])
            product_down("mlp_down", 16, 8)
            partition_sum(7, 2)
            pe.wait_ge(ple_in, 16)
            merge("ple", chunk, k1=PLE // P, fresh=7)
            partition_sum(8, 2)

        @block.scalar
        def _(act):
            act.dma_start(params[:, :], a["params"]).then_inc(par_in, 16)
            for dst, src in ((w_gate, "w_gate"), (w_if, "w_if"), (w2_k, "w2_k"), (w2_v, "w2_v")):
                act.dma_start(dst[:, :], a[src]).then_inc(small_in, 16)

            def norm(m, b, n=S):
                act.wait_ge(stat, m + 1)
                nc.scalar.activation(std[:, 0:n], bank(b, n), ACT.Sqrt, bias=eps[:, 0:1], scale=1.0 / D) \
                    .then_inc(std_done, 1)

            def take(name, pairs, dst, n=S, func=ACT.Copy, scale=1.0):
                per = dict((x, t) for x, _, t in PHASES)[name]
                with loop(act, pairs) as i:
                    for k in range(per):
                        act.wait_ge(tile_done, TILE0[name] + per * i + k + 1)
                        nc.scalar.activation(dst(i, k), bank(k % 2, n), func, scale=scale).then_inc(evac[k % 2], 1)

            def attention(name, units, dst, sinks=False):
                s = att[name]
                steps, groups, per = att_dims(name)
                flat = [u for _ in range(groups) for u in units] if name != "ca" else units
                n_units = len(flat)
                with loop(act, steps) as i:
                    u0 = n_units * i

                    def exps(u):
                        par, nk = u % 2, flat[u]["nk"]
                        act.wait_ge(s["negmax"], u0 + (u + 1))
                        if u >= 2:
                            act.wait_ge(s["transposed"], u0 + (u - 1))
                        for hd in range(2):
                            x = 2 * par + hd
                            last = nc.scalar.activation(probs[:, x * S:x * S + nk], bank(2 + x, nk), ACT.Exp,
                                                        bias=negmax[:, x:x + 1], accum_out=total[:, x:x + 1])
                        if sinks:
                            last = nc.scalar.activation(sink_e[:, 2 * par:2 * par + 2],
                                                        sink_arg[:, 2 * par:2 * par + 2], ACT.Exp)
                        last.then_inc(s["probs"], 1)

                    def copy(u):
                        par, nk = u % 2, flat[u]["nk"]
                        act.wait_ge(s["transposed"], u0 + (u + 1))
                        if u >= 2:
                            act.wait_ge(s["summed"], u0 + (u - 1))
                        h, w = min(nk, P), max(nk, P)
                        nc.scalar.copy(probs_t[0:h, 2 * par * S:2 * par * S + w], psum[0:h, 6, 0:w]) \
                            .then_inc(s["copied_a"], 1)

                    def store(g):
                        act.wait_ge(s["turned"], groups * i + (g + 1))
                        nc.scalar.copy(dst(i, g), psum[:, 1, :] if name != "ca" else
                                       psum[:, 1, :].rearrange("p (c t) -> p c t", c=4)).then_inc(s["stored"], 1)

                    exps(0)
                    for u in range(n_units):
                        if u + 1 < n_units:
                            exps(u + 1)
                        if u >= 2 and flat[u - 2]["last"]:
                            store((u - 2) // per)
                        copy(u)
                    if n_units > 1 and flat[n_units - 2]["last"]:
                        store((n_units - 2) // per)
                    store(groups - 1)

            act.wait_ge(consts, 1)
            norm(0, 2, MEM)
            act.wait_ge(normed, 1)
            norm(1, 3)
            take("mem_k", 2, lambda i, k: cols(memk, 4 * MEM * i + k * MEM, MEM), MEM)
            take("nsa_v", 1, lambda i, k: chunk(12 + k))
            take("nsa_g", 1, lambda i, k: gates[:, k * 48:(k + 1) * 48], 48, ACT.Sigmoid)
            for k in range(4):
                act.wait_ge(tile_done, TILE0["cmp_kv"] + k + 1)
                for g in range(2):
                    src = psum[64 * g:64 * g + 64, k % 2, :]
                    dst = chunk(16 + 2 * k + g)
                    nc.scalar.copy(dst[0:64, :], src)
                    last = nc.scalar.copy(dst[64:P, 0:S - 1], src[:, 1:S])
                last.then_inc(evac[k % 2], 1)
            take("nsa_k", 1, lambda i, k: chunk(8 + k))
            take("cmp_w1", 2, lambda i, k: cols(hid, 2 * CMPW * i + k * CMPW, CMPW), CMPW, ACT.Gelu_apprx_tanh)
            act.wait_ge(tile_done, TILE0["cmp_w2"] + 1)
            nc.scalar.copy(kcmp[:, :], bank(0, CMPW)).then_inc(evac[0], 1)
            act.wait_ge(tile_done, TILE0["cmp_w2"] + 2)
            nc.scalar.copy(vcmp[:, :], psum[0:NCMP, 1, 0:G * HD]).then_inc(evac[1], 1)
            take("nsa_q", 2, lambda i, k: cols(big, 4 * S * i + k * S), scale=HD ** -0.5)
            attention("nsa", nsa_units(), lambda i, g: cols(ht, 4 * g * S + S * i))
            norm(2, 2)
            take("ca_q", 2, lambda i, k: cols(big, 4 * S * i + k * S), scale=256 ** -0.5)
            attention("ca", ca_units(), lambda i, g: ht[:, :].rearrange("p (c t) -> p c t", c=KD)
                      [:, 4 * (g // NT):4 * (g // NT) + 4, (g % NT) * P:(g % NT + 1) * P])
            norm(3, 2)
            with act.Fori(0, FC // 2) as i:
                for j in range(2):
                    act.wait_ge(evac[0], TILE0["ffn_up"] // 2 + j + 1 + 2 * i)
                    nc.scalar.activation(act_o[:, j * S:(j + 1) * S], tmp[:, j * S:(j + 1) * S], ACT.Silu) \
                        .then_inc(gated, 1)
            norm(4, 2)
            norm(5, 2)
            with act.Fori(0, 2) as i:
                for k in range(4):
                    b = k % 2
                    act.wait_ge(evac[b], TILE0["ml_qk"] // 2 + k // 2 + 1 + 2 * i)
                    nc.scalar.activation(cols(big, 4 * S * i + k * S), tmp[:, b * S:(b + 1) * S], ACT.Silu) \
                        .then_inc(gated, 1)
            take("ml_v", 2, lambda i, k: cols(big, S * i + 8 * S + k * D))
            take("ml_o", 2, lambda i, k: cols(big, 4 * S * i + (16 + k) * S), func=ACT.Sigmoid)
            ml = ml_step
            act.wait_ge(tile_done, TILE0["ml_if"] + 1)
            nc.scalar.activation(ig[:, :], psum[0:MLH, 0, :], ACT.Identity,
                                 bias=params[0:MLH, COL["b_i"]:COL["b_i"] + 1]).then_inc(evac[0], 1)
            act.wait_ge(ml["z"], 2)
            nc.scalar.activation(fe[:, :], fe[:, :], ACT.Exp, scale=-1.0).then_inc(ml["e"], 1)
            act.wait_ge(ml["e"], 1)
            nc.scalar.activation(fe[:, :], fe[:, :], ACT.Ln, bias=ones[0:MLH, 0:1]).then_inc(ml["l"], 1)
            act.wait_ge(ml["u_col"], 1)
            nc.scalar.copy(u_col[:, :], bank(2, NT * MLH)).then_inc(ml["u_col"], 1)
            act.wait_ge(ml["u_col"], 2)
            for h in range(MLH):
                act.wait_ge(ml["bc"], h + 1)
                if h:
                    act.wait_ge(ml["recip"], 3 * h)
                nc.scalar.copy(q_st[:, 0:S], bank(6)).then_inc(ml["bc_used"], 1)
                nc.scalar.activation(tmp[:, 0:S], bank(7), ACT.Exp).then_inc(ml["bc_used"], 1)
                act.wait_ge(ml["decay"], (NT + 1) * h + 1)
                if h:
                    act.wait_ge(ml["weighted"], NT * h)
                for st in range(NT):
                    e0 = 24 * S + ML_AT[st]
                    w = S - (st + 1) * P
                    uc = u_col[:, st * MLH + h:st * MLH + h + 1]
                    last = nc.scalar.activation(big[:, e0:e0 + P], q_st[:, S + st * P:S + (st + 1) * P], ACT.Exp,
                                                bias=uc, scale=-1.0)
                    if w:
                        last = nc.scalar.activation(big[:, e0 + P:e0 + P + w], q_st[:, (st + 1) * P:S], ACT.Exp,
                                                    bias=uc, scale=-1.0)
                    last.then_inc(ml["decay"], 1)
                for dv in range(2):
                    act.wait_ge(ml["h"], 2 * h + dv + 1)
                    nc.scalar.activation(chunk(28 + dv), o_acc[:, dv * S:(dv + 1) * S], ACT.Square) \
                        .then_inc(ml["sq"], 1)
                act.wait_ge(ml["ssq"], h + 1)
                nc.scalar.activation(std[:, :], bank(7), ACT.Sqrt, bias=eps[:, 0:1], scale=1.0 / 256) \
                    .then_inc(ml["std"], 1)

            def gate(name):
                with act.Fori(0, 4) as i:
                    for j in range(2):
                        act.wait_ge(tile_done, TILE0[name] + 2 * j + 1 + 4 * i)
                        act.wait_ge(evac[1], TILE0[name] // 2 + j - 1 + 2 * i)
                        nc.scalar.activation(act_o[:, j * S:(j + 1) * S], bank(0), ACT.Sigmoid).then_inc(evac[0], 1)

            gate("merge_a")
            take("sw_q", 2, lambda i, k: cols(big, 4 * S * i + (8 + k) * S), scale=HD ** -0.5)
            for k in range(6):
                act.wait_ge(tile_done, TILE0["sw_kv"] + k + 1)
                src = bank(k % 2) if k < 2 else bank(k % 2, 256)
                dst = chunk(24 + k) if k < 2 else big[:, 26 * S + (k - 2) * 256:26 * S + (k - 1) * 256]
                nc.scalar.copy(dst, src).then_inc(evac[k % 2], 1)
            attention("sw", sw_units(), lambda i, g: cols(big, (16 + 4 * g) * S + S * i), sinks=True)
            gate("merge_b")
            norm(6, 2)
            with act.Fori(0, F2C // 4) as i:
                for k in range(4):
                    b = k % 2
                    act.wait_ge(tile_done, TILE0["mlp_up"] + k + 1 + 4 * i)
                    nc.scalar.activation(act_o[:, b * S:(b + 1) * S], bank(b), ACT.Relu).then_inc(evac[b], 1)
                    act.wait_ge(evac[b], TILE0["mlp_up"] // 2 + k // 2 + 1 + 2 * i)
                    nc.scalar.activation(cols(big, 4 * S * i + k * S), act_o[:, b * S:(b + 1) * S], ACT.Square) \
                        .then_inc(gated, 1)
            norm(7, 2)
            gate("ple")
            norm(8, 2)

        @block.vector
        def _(dve):
            V = nc.vector
            d = Count(dve_step)
            sq = Count(squares)
            nm = Count(normed)

            def step(ins):
                ins.then_inc(dve_step, 1)
                d.n += 1

            def settle():
                dve.wait_ge(dve_step, d.at)

            def square(src, n=S):
                step(V.tensor_tensor(sqt[:, 0:n], src, src, ALU.mult))
                settle()
                V.tensor_tensor(acc[:, 0:n], acc[:, 0:n], sqt[:, 0:n], ALU.add).then_inc(squares, 1)
                sq.n += 1
                dve.wait_ge(squares, sq.at)

            def clear_acc():
                step(V.memset(acc[:, :], 0.0))
                settle()

            def norm(m, name, src, dst, n=S, after=None):
                if nm.n:
                    dve.wait_ge(normed, nm.at)
                dve.wait_ge(std_done, m + 1)
                step(V.reciprocal(rstd[:, 0:n], std[:, 0:n]))
                settle()
                if m == 4:
                    clear_acc()
                for c in range(KD):
                    w = COL[name] + c
                    V.scalar_tensor_tensor(out=dst(c), in0=src(c), scalar=params[:, w:w + 1], in1=rstd[:, 0:n],
                                           op0=ALU.mult, op1=ALU.mult).then_inc(normed, 1)
                    nm.n += 1
                    if m == 4:
                        dve.wait_ge(normed, nm.at)
                        square(dst(c))

            xc = lambda c: xt[:, c * S:(c + 1) * S]
            hc = lambda c: ht[:, c * S:(c + 1) * S]

            def residual(name, steps, per):
                clear_acc()
                with dve.Fori(0, steps) as i:
                    d.enter(i, per)
                    sq.enter(i, per)
                    for k in range(per):
                        b = k % 2
                        x = cols(xt, per * S * i + k * S)
                        dve.wait_ge(tile_done, TILE0[name] + k + 1 + per * i)
                        V.tensor_tensor(x, bank(b), x, ALU.add).then_inc(evac[b], 1)
                        dve.wait_ge(evac[b], TILE0[name] // 2 + k // 2 + 1 + (per // 2) * i)
                        square(x)
                d.leave(steps)
                sq.leave(steps)

            def convolve(name, taps, col, n_ch, i, k, ch, bank_):
                t0 = (k % 2) * S
                for m in range(taps):
                    w = params[:, bass.ds(ch + (col + (taps - 1 - m) * n_ch), 1)]
                    src = psum[:, bank_, 0:S - m]
                    o = tmp[:, t0 + m:t0 + S]
                    if m == 0:
                        ins = V.tensor_scalar(o, src, w, None, ALU.mult)
                    else:
                        ins = V.scalar_tensor_tensor(out=o, in0=src, scalar=w, in1=o, op0=ALU.mult, op1=ALU.add)
                    if m < taps - 1:
                        step(ins)
                        settle()
                    else:
                        ins.then_inc(evac[bank_], 1)

            def attention(name, units, per_step, gate=None, sinks=False):
                s = att[name]
                steps, groups, per = att_dims(name)
                flat = [u for _ in range(groups) for u in units] if name != "ca" else units
                n_units = len(flat)
                width = 256 if name == "ca" else HD
                with loop(dve, steps) as i:
                    if steps > 1:
                        d.enter(i, per_step)
                    u0 = n_units * i

                    def maxima(u):
                        par, nk = u % 2, flat[u]["nk"]
                        dve.wait_ge(s["scores"], u0 + (u + 1))
                        nm_ = negmax[:, 2 * par:2 * par + 2]
                        ins = V.tensor_reduce(nm_, psum[:, 2 + 2 * par:4 + 2 * par, 0:nk], axis=AX_X, op=ALU.max,
                                              negate=True)
                        if sinks:
                            g = u // per
                            step(ins)
                            settle()
                            sink = bass.ds(8 * g + 2 * i, 2)
                            step(V.tensor_tensor(nm_, nm_, neg_sink[:, sink], ALU.min))
                            settle()
                            ins = V.tensor_tensor(sink_arg[:, 2 * par:2 * par + 2], nm_, neg_sink[:, sink],
                                                  ALU.subtract)
                        ins.then_inc(s["negmax"], 1)

                    def copy(u):
                        par, nk = u % 2, flat[u]["nk"]
                        dve.wait_ge(s["transposed"], u0 + (u + 1))
                        if u >= 2:
                            dve.wait_ge(s["summed"], u0 + (u - 1))
                        h, w = min(nk, P), max(nk, P)
                        V.tensor_copy(probs_t[0:h, (2 * par + 1) * S:(2 * par + 1) * S + w], psum[0:h, 7, 0:w]) \
                            .then_inc(s["copied_d"], 1)

                    def weights(u):
                        par, g = u % 2, u // per
                        t, c = total[:, 2 * par:2 * par + 2], coef[:, 2 * par:2 * par + 2]
                        if sinks:
                            step(V.tensor_tensor(t, t, sink_e[:, 2 * par:2 * par + 2], ALU.add))
                            settle()
                        step(V.reciprocal(c, t))
                        if gate is not None:
                            settle()
                            gt = gates[:, :].rearrange("p (x b) -> p x b", b=3)[
                                :, bass.ds(flat[u]["qt"] * 16 + 8 * g + 2 * i, 2), flat[u]["br"]]
                            if flat[u]["br"] == 0:
                                ins = V.scalar_tensor_tensor(out=c, in0=c, scalar=cmp_any[:, flat[u]["qt"]:flat[u]["qt"] + 1],
                                                             in1=gt, op0=ALU.mult, op1=ALU.mult)
                            else:
                                ins = V.tensor_tensor(c, c, gt, ALU.mult)
                            step(ins)

                    def combine(u):
                        par, g = u % 2, u // per
                        settle()
                        dve.wait_ge(s["summed"], u0 + (u + 1))
                        if not flat[u]["first"]:
                            dve.wait_ge(s["combined"], u0 + u)
                        for hd in range(2):
                            o0 = (g % 2) * S + hd * width + (0 if name == "ca" else flat[u]["qt"] * P)
                            o, c = o_acc[:, o0:o0 + width], coef[:, 2 * par + hd:2 * par + hd + 1]
                            src = psum[:, 0, hd * width:(hd + 1) * width]
                            if flat[u]["first"]:
                                last = V.tensor_scalar(o, src, c, None, ALU.mult)
                            else:
                                last = V.scalar_tensor_tensor(out=o, in0=src, scalar=c, in1=o, op0=ALU.mult,
                                                              op1=ALU.add)
                        last.then_inc(s["combined"], 1)

                    maxima(0)
                    for u in range(n_units):
                        if u + 1 < n_units:
                            maxima(u + 1)
                        if u >= 1:
                            combine(u - 1)
                        copy(u)
                        weights(u)
                    combine(n_units - 1)
                if steps > 1:
                    d.leave(steps)

            clear_acc()
            dve.wait_ge(mem_in, 16)
            for c in range(KD):
                square(big[:, c * MEM:(c + 1) * MEM], MEM)
            dve.wait_ge(stat, 1)
            clear_acc()
            dve.wait_ge(x_in, 16)
            for c in range(KD):
                square(xc(c))
            dve.wait_ge(par_in, 16)
            step(V.tensor_scalar(neg_sink[:, :], params[:, COL["sink"]:COL["sink"] + 16], -1.0, None, ALU.mult))
            norm(0, "mem", lambda c: big[:, c * MEM:(c + 1) * MEM], lambda c: big[:, (KD + c) * MEM:(KD + c + 1) * MEM], MEM)
            norm(1, "mix", xc, hc)
            with dve.Fori(0, 2) as i:
                for t in range(2):
                    dve.wait_ge(tile_done, TILE0["mem_v"] + t + 1 + 2 * i)
                    V.tensor_copy(cols(memv, S * i + t * D), bank(t)).then_inc(evac[t], 1)
            attention("nsa", nsa_units(), 2 * NU * 2, gate=True)
            residual("nsa_out", 2, 4)
            norm(2, "cross", xc, hc)
            attention("ca", ca_units(), 0)
            residual("ca_out", 2, 4)
            norm(3, "ffn", xc, hc)
            with dve.Fori(0, FC // 2) as i:
                d.enter(i, 4)
                for j in range(2):
                    dve.wait_ge(tile_done, TILE0["ffn_up"] + 2 * j + 1 + 4 * i)
                    convolve("ffn_up", 3, COL["ffn_conv"], FC, i, j, 2 * i + j, 0)
                    dve.wait_ge(tile_done, TILE0["ffn_up"] + 2 * j + 2 + 4 * i)
                    dve.wait_ge(gated, j + 1 + 2 * i)
                    V.tensor_tensor(cols(big, 2 * S * i + j * S), bank(1), act_o[:, j * S:(j + 1) * S], ALU.mult) \
                        .then_inc(evac[1], 1)
            d.leave(FC // 2)
            residual("ffn_down", 4, 2)
            norm(4, "final", xc, xc)
            norm(5, "mix2", xc, hc)
            with dve.Fori(0, 2) as i:
                d.enter(i, 12)
                for k in range(4):
                    dve.wait_ge(tile_done, TILE0["ml_qk"] + k + 1 + 4 * i)
                    dve.wait_ge(gated, GATED["ffn"] + k - 1 + 4 * i)
                    convolve("ml_qk", 4, COL["ml_conv"], 8, i, k, 4 * i + k, k % 2)
            d.leave(2)
            ml = ml_step
            dve.wait_ge(tile_done, TILE0["ml_if"] + 2)
            V.tensor_scalar(fz[:, :], psum[0:MLH, 1, :], params[0:MLH, COL["b_f"]:COL["b_f"] + 1], None, ALU.add) \
                .then_inc(evac[1], 1)
            dve.wait_ge(evac[1], TILE0["merge_a"] // 2)
            V.tensor_scalar(fe[:, :], fz[:, :], -1.0, None, ALU.mult).then_inc(ml["z"], 1)
            dve.wait_ge(ml["z"], 1)
            V.tensor_tensor(fe[:, :], fe[:, :], fz[:, :], ALU.max).then_inc(ml["z"], 1)
            step(V.memset(sqt[:, :], 1.0))
            dve.wait_ge(ml["l"], 1)
            V.scalar_tensor_tensor(out=fz[:, :], in0=fz[:, :], scalar=0.0, in1=fe[:, :], op0=ALU.min,
                                   op1=ALU.subtract).then_inc(ml["rows"], 1)
            settle()
            dve.wait_ge(ml["rows"], 1)
            V.tensor_tensor_scan(fcum[:, :], sqt[0:MLH, :], fz[:, :], 0.0, ALU.mult, ALU.add).then_inc(ml["rows"], 1)
            dve.wait_ge(ml["rows"], 2)
            dve.wait_ge(evac[0], TILE0["merge_a"] // 2)
            V.tensor_tensor(u_row[:, :], ig[:, :], fcum[:, :], ALU.subtract).then_inc(ml["rows"], 1)
            dve.wait_ge(ml["rows"], 3)
            V.tensor_tensor_scan(m_row[:, :], u_row[:, :], u_row[:, :], 0.0, ALU.max, ALU.max).then_inc(ml["rows"], 1)
            dve.wait_ge(ml["rows"], 4)
            V.scalar_tensor_tensor(out=nm_row[:, :], in0=fcum[:, :], scalar=-1.0, in1=m_row[:, :], op0=ALU.mult,
                                   op1=ALU.subtract).then_inc(ml["rows"], 1)
            for h in range(MLH):
                dve.wait_ge(ml["bc_used"], 2 * h + 1)
                V.tensor_tensor(q_st[:, S:2 * S].rearrange("p (c t) -> p c t", c=NT),
                                q_st[:, 0:S].rearrange("p (c t) -> p c t", c=NT),
                                ml_mask[:, :].unsqueeze(1).to_broadcast([P, NT, P]), ALU.add).then_inc(ml["decay"], 1)
                for st in range(NT):
                    dve.wait_ge(ml["scores"], NT * h + st + 1)
                    dve.wait_ge(ml["decay"], (NT + 1) * h + st + 2)
                    if h:
                        dve.wait_ge(ml["sums"], h)
                    w = S - st * P
                    e0 = 24 * S + ML_AT[st]
                    V.scalar_tensor_tensor(out=probs_t[:, ML_AT[st]:ML_AT[st] + w], in0=psum[:, 2 + st, 0:w],
                                           scalar=float(P) ** -0.5, in1=big[:, e0:e0 + w], op0=ALU.mult,
                                           op1=ALU.mult).then_inc(ml["weighted"], 1)
                dve.wait_ge(ml["sums"], h + 1)
                dve.wait_ge(ml["bc_used"], 2 * h + 2)
                V.scalar_tensor_tensor(out=tmp[:, S:2 * S], in0=bank(6), scalar=-1.0, in1=tmp[:, 0:S], op0=ALU.mult,
                                       op1=ALU.max).then_inc(ml["recip"], 1)
                dve.wait_ge(ml["recip"], 3 * h + 1)
                V.tensor_tensor(tmp[:, S:2 * S], bank(6), tmp[:, S:2 * S], ALU.max).then_inc(ml["recip"], 1)
                dve.wait_ge(ml["recip"], 3 * h + 2)
                V.reciprocal(sqt[:, :], tmp[:, S:2 * S]).then_inc(ml["recip"], 1)
                dve.wait_ge(ml["recip"], 3 * h + 3)
                for dv in range(2):
                    V.tensor_tensor(o_acc[:, dv * S:(dv + 1) * S], bank(dv), sqt[:, :], ALU.mult).then_inc(ml["h"], 1)
                dve.wait_ge(ml["std"], h + 1)
                step(V.reciprocal(rstd[:, :], std[:, :]))
                settle()
                for dv in range(2):
                    c = 2 * h + dv
                    w = COL["mlstm"] + c
                    step(V.scalar_tensor_tensor(out=o_acc[:, dv * S:(dv + 1) * S], in0=o_acc[:, dv * S:(dv + 1) * S],
                                                scalar=params[:, w:w + 1], in1=rstd[:, :], op0=ALU.mult, op1=ALU.mult))
                    settle()
                    V.tensor_tensor(chunk(16 + c), chunk(16 + c), o_acc[:, dv * S:(dv + 1) * S], ALU.mult) \
                        .then_inc(ml["y"], 1)
            with dve.Fori(0, 4) as i:
                for j in range(2):
                    dve.wait_ge(tile_done, TILE0["merge_a"] + 2 * j + 2 + 4 * i)
                    dve.wait_ge(evac[0], TILE0["merge_a"] // 2 + j + 1 + 2 * i)
                    V.tensor_tensor(cols(big, 2 * S * i + j * S), bank(1), act_o[:, j * S:(j + 1) * S], ALU.mult) \
                        .then_inc(evac[1], 1)
            attention("sw", sw_units(), 2 * NT * 4, sinks=True)
            with dve.Fori(0, 4) as i:
                for j in range(2):
                    dve.wait_ge(tile_done, TILE0["merge_b"] + 2 * j + 2 + 4 * i)
                    dve.wait_ge(evac[0], TILE0["merge_b"] // 2 + j + 1 + 2 * i)
                    V.tensor_tensor(tmp[:, j * S:(j + 1) * S], bank(1), act_o[:, j * S:(j + 1) * S], ALU.mult) \
                        .then_inc(evac[1], 1)
                    dve.wait_ge(evac[1], TILE0["merge_b"] // 2 + j + 1 + 2 * i)
                    m = cols(big, 2 * S * i + j * S)
                    V.tensor_tensor(m, m, tmp[:, j * S:(j + 1) * S], ALU.add).then_inc(merged, 1)
            residual("mix_out", 2, 4)
            norm(6, "mlp2", xc, hc)
            residual("mlp_down", 4, 2)
            norm(7, "ple2", xc, hc)
            clear_acc()
            with dve.Fori(0, 4) as i:
                d.enter(i, 4)
                sq.enter(i, 2)
                for j in range(2):
                    dve.wait_ge(tile_done, TILE0["ple"] + 2 * j + 2 + 4 * i)
                    dve.wait_ge(evac[0], TILE0["ple"] // 2 + j + 1 + 2 * i)
                    V.tensor_tensor(tmp[:, j * S:(j + 1) * S], bank(1), act_o[:, j * S:(j + 1) * S], ALU.mult) \
                        .then_inc(evac[1], 1)
                    dve.wait_ge(evac[1], TILE0["ple"] // 2 + j + 1 + 2 * i)
                    x = cols(xt, 2 * S * i + j * S)
                    step(V.tensor_tensor(x, x, tmp[:, j * S:(j + 1) * S], ALU.add))
                    settle()
                    square(x)
            d.leave(4)
            sq.leave(4)
            norm(8, "final2", xc, hc)

        @block.gpsimd
        def _(pool):
            g = nc.gpsimd
            for buf, value in ((ident, 0.0), (ones, 1.0), (causal, 0.0), (band, 0.0), (cmp_mask, 0.0), (cmp_any, 1.0),
                               (ml_mask, 0.0), (select, 0.0), (eps, EPS)):
                last = g.memset(buf[:, :], value)
            last.then_inc(pool_step, 1)
            g.memset(start[:, 0:1], 0.0).then_inc(tile_done, 2)
            g.memset(start[:, 1:2], 0.0).then_inc(evac[0], 1)
            g.memset(start[:, 2:3], 0.0).then_inc(evac[1], 1)
            pool.wait_ge(pool_step, 1)

            def keep(buf, pattern, base, per_row, fill, compare=ALU.is_ge):
                return g.affine_select(out=buf, in_=buf, pattern=pattern, compare_op=compare, fill=fill, base=base,
                                       channel_multiplier=per_row)

            keep(ident[:, :], [[-1, P]], 0, 1, 1.0, ALU.not_equal).then_inc(pool_step, 1)
            keep(causal[:, :], [[-1, P]], 0, 1, NEG)
            keep(band[:, 0:P], [[1, P]], -1, -1, NEG)
            keep(band[:, P:2 * P], [[-1, P]], 0, 1, NEG)
            keep(cmp_mask[:, :], [[P, NT], [-16, NCMP]], -31, 1, NEG)
            keep(cmp_any[:, :], [[P, NT]], -31, 1, 0.0)
            keep(ml_mask[:, :], [[1, P]], 0, -1, -NEG)
            keep(select[:, :], [[1, MLH], [0, P]], 0, -1, 1.0, ALU.not_equal)
            pool.wait_ge(pool_step, 2)
            g.tensor_copy(ident_bf[:, :], ident[:, :]).then_inc(consts, 1)

            pool.wait_ge(par_in, 16)
            for kind in range(2):
                for b in range(2):
                    pool.wait_ge(evac[b], TILE0["cmp_kv"] // 2 + kind + 1)
                src = big[:, (16 + 4 * kind) * S:(20 + 4 * kind) * S].rearrange("p (g t) -> p g t", g=G)
                for j in range(16):
                    d0 = (24 + 4 * kind) * S + j * CMPW
                    c = COL["pe_k" if kind == 0 else "pe_v"] + j
                    g.tensor_scalar(big[:, d0:d0 + CMPW].rearrange("p (g n) -> p g n", g=G),
                                    src[:, :, 2 * j:2 * j + 16 * (NCMP - 1) + 1:16], params[:, c:c + 1], None,
                                    ALU.add).then_inc(blocks, 1)

            def stage(name, q0, done):
                s = att[name]
                for half_ in range(2):
                    for b in range(2):
                        pool.wait_ge(evac[b], TILE0[done] // 2)
                    g.tensor_copy(q_st[:, half_ * S:(half_ + 1) * S], chunk(q0 + 4 * half_)).then_inc(s["staged"], 1)
                with pool.Fori(1, PAIRS // 2) as i:
                    for half_ in range(2):
                        pool.wait_ge(s["turned"], 2 * i + half_ - 1)
                        pool.wait_ge(evac[0], TILE0[done] // 2)
                        g.tensor_copy(q_st[:, half_ * S:(half_ + 1) * S], cols(big, (q0 + 4 * half_) * S + S * i)) \
                            .then_inc(s["staged"], 1)

            stage("nsa", 0, "nsa_out")
            stage("sw", 8, "merge_b")


def lay_out(x):
    def tiles(w):
        k, n = w.shape
        return w.reshape(k // P, P, n // P, P).transpose(0, 2, 1, 3)

    def by_output(w):
        t = tiles(w)
        k, n = t.shape[:2]
        return t.reshape(k, n // 2, 2, P, P).transpose(1, 3, 2, 0, 4).reshape(n // 2, P, 2 * k * P)

    def by_token(w):
        k, n = w.shape
        return w.reshape(2, 4, P, n // S, S).transpose(3, 0, 2, 1, 4).reshape(-1, P, PANEL)

    def in_pairs(v, w):
        tv, tw = tiles(v), tiles(w)
        n = tv.shape[1]
        p = [np.concatenate([t.transpose(1, 2, 0, 3).reshape(n, P, -1) for t in (tv, tw)], axis=2)]
        return pad(p[0])

    def down(w):
        t = tiles(w)
        k, n = t.shape[:2]
        return pad(t.reshape(2, k // 2, n, P, P).transpose(2, 0, 3, 1, 4).reshape(2 * n, P, k // 2 * P))

    def pad(p):
        return np.concatenate([p, np.zeros((*p.shape[:2], PANEL - p.shape[2]), p.dtype)], axis=2)

    def heads(w):
        return w.reshape(-1, 2, 2, 4, HD).transpose(0, 1, 3, 2, 4).reshape(w.shape)

    def feature_rows(w):
        return heads(w.T).T

    def column(v):
        return v.reshape(-1, P).T

    ws = x["nsa_w_in"][0]
    q, kc, vc, ks, vs, kw, vw, gl = np.split(ws, [D + 256 * i for i in range(7)], axis=1)
    w1 = [x[n][0].reshape(2, 8, P, 256).transpose(0, 2, 1, 3).reshape(2, P, PANEL) for n in ("nsa_ck_w1", "nsa_cv_w1")]
    w = x["w_in_2"][0]
    qk, v_ml, o_ml, if_, q_sw, k_sw, v_sw, g_a, g_b = np.split(w, np.cumsum([D, D, D, 8, D, 256, 256, D]), axis=1)
    up = x["ffn_w_up"][0]
    wkv = x["ca_wkv"][0]
    parts = {
        "mem_k": by_output(wkv[:, :D]), "mem_v": by_token(wkv[:, D:]),
        "nsa_v": by_token(np.concatenate([vs, vw], axis=1)), "cmp_kv": by_output(np.concatenate([kc, vc], axis=1)),
        "nsa_k": by_output(np.concatenate([ks, kw], axis=1)), "cmp_w1": np.concatenate(w1),
        "nsa_q": by_output(heads(q)), "nsa_out": by_output(feature_rows(x["nsa_w_out"][0])),
        "ca_q": by_output(x["ca_wq"][0]), "ca_out": by_output(x["ca_wo"][0]),
        "ffn_up": in_pairs(up[:, :FF], up[:, FF:]), "ffn_down": down(x["ffn_w_down"][0]),
        "ml_qk": by_output(qk), "ml_v": by_token(v_ml), "ml_o": by_output(o_ml),
        "merge_a": in_pairs(g_a, x["w_branch_a_2"][0]), "sw_q": by_output(heads(q_sw)),
        "sw_kv": np.concatenate([by_output(k_sw), v_sw.reshape(KD, P, 256).transpose(1, 0, 2).reshape(1, P, PANEL)]),
        "merge_b": in_pairs(g_b, feature_rows(x["w_branch_b_2"][0])), "mix_out": by_output(x["w_out_2"][0]),
        "mlp_up": by_output(x["w_up_2"][0]), "mlp_down": down(x["w_down_2"][0]),
        "ple": in_pairs(x["w_ple_gate_2"][0], x["w_ple_proj_2"][0]),
    }
    for name, pairs, _ in PHASES:
        assert not pairs or len(parts[name]) == 2 * pairs, name
    gl = gl.reshape(D, 2, 2, 4, 3).transpose(0, 1, 3, 2, 4).reshape(D, 48)
    sinks = x["sinks_2"][0].reshape(2, 2, 4).transpose(0, 2, 1).reshape(1, 16)
    norms = [x["mem_norm_w"], x["norm_mix_w"][0], x["norm_cross_w"][0], x["norm_ffn_w"][0], x["final_norm_w"],
             x["norm_mix_g_2"][0], x["norm_mlp_g_2"][0], x["norm_ple_g_2"][0], x["final_norm_g_2"],
             x["mlstm_norm_g_2"][0]]
    b_if = np.zeros((P, 2), np.float32)
    b_if[0:MLH] = x["b_if_2"][0].reshape(2, MLH).T
    params = np.concatenate(
        [column(v) for v in norms] + [column(v) for v in x["ffn_conv_w"][0]] + [column(v) for v in x["conv_qk_2"][0]]
        + [column(x["nsa_pe_k"][0].reshape(-1)), column(x["nsa_pe_v"][0].reshape(-1)), np.repeat(sinks, P, axis=0), b_if],
        axis=1)

    def chunks(v):
        return v.T.reshape(-1, P, v.shape[0]).transpose(1, 0, 2).reshape(P, -1)

    def rows(v):
        return v.reshape(-1, P, v.shape[1]).transpose(1, 0, 2).reshape(P, -1)

    ck2 = x["nsa_ck_w2"][0]
    return {
        "panels": np.concatenate([parts[n] for n, pairs, _ in PHASES if pairs]), "params": params,
        "x": chunks(x["x"][0]), "mem": chunks(x["mem"][0]), "ple": chunks(x["p_2"][0, 0]),
        "w_gate": rows(gl), "w_if": rows(if_), "w2_k": rows(np.concatenate([ck2, ck2], axis=1)),
        "w2_v": rows(x["nsa_cv_w2"][0]),
    }


def kernel(**inputs):
    import concourse.bacc as _bacc
    from concourse.bass_utils import run_bass_kernel_spmd as _run

    nc = _bacc.Bacc("TRN2", target_bir_lowering=False, num_devices=1)
    arrays, args = {}, {}
    for name, v in lay_out({k: np.asarray(v) for k, v in inputs.items()}).items():
        v = np.ascontiguousarray(v)
        arrays[f"in_{name}"] = v
        args[name] = nc.dram_tensor(f"in_{name}", v.shape, mybir.dt.from_np(v.dtype), kind="ExternalInput").ap()
    out = nc.dram_tensor("out", (P, KD * S), F32, kind="ExternalOutput").ap()
    program(nc, args, out)
    r = _run(nc, [arrays], core_ids=[0])
    y = r.results[0]["out"]
    return np.ascontiguousarray(y.reshape(P, KD, S).transpose(2, 1, 0).reshape(1, S, D))
```

```python
from contextlib import ExitStack

import concourse.bass as bass
from concourse import mybir
import numpy as np

F32 = mybir.dt.float32
F32R = mybir.dt.float32r
BF16 = mybir.dt.bfloat16
ALU = mybir.AluOpType
ACT = mybir.ActivationFunctionType
AX_X = mybir.AxisListType.X

P = 128
S = 512
D = 1024
KD = D // P
NT = S // P
MEM = 256
FF = 2816
FC = FF // P
F2 = 4096
F2C = F2 // P
PLE = 256
PANEL = 16 * P
EPS = 1e-6
TOKEN_BANK = (0, 1, 4, 5)
NEG = -1e30

HD = 64
G = 4
PAIRS = 8
NCMP = 31
CMPW = G * NCMP
MLH = 4

NORMS = ["mem", "mix", "cross", "ffn", "final", "mix2", "mlp2", "ple2", "final2", "mlstm"]
COL = {name: 8 * i for i, name in enumerate(NORMS)}
COL["ffn_conv"] = 80
COL["ml_conv"] = COL["ffn_conv"] + 3 * FC
COL["pe_k"] = COL["ml_conv"] + 4 * 8
COL["pe_v"] = COL["pe_k"] + 16
COL["sink"] = COL["pe_v"] + 16
COL["b_i"] = COL["sink"] + 16
COL["b_f"] = COL["b_i"] + 1
NPAR = COL["b_f"] + 1

PHASES = [
    ("nsa_v", 1, 4), ("nsa_g", 0, 4), ("cmp_kv", 1, 4), ("nsa_k", 1, 4), ("cmp_w1", 2, 2), ("cmp_w2", 0, 2),
    ("nsa_q", 2, 4), ("nsa_out", 2, 4),
    ("mem_k", 2, 4), ("mem_v", 2, 2), ("ca_q", 2, 4), ("ca_out", 2, 4),
    ("ffn_up_a", 6, 4), ("ffn_down_a", 4, 2), ("ffn_up_b", 5, 4), ("ffn_down_b", 4, 2),
    ("ml_qk", 2, 4), ("ml_v", 2, 4), ("ml_o", 2, 4), ("ml_if", 0, 2), ("merge_a", 4, 4),
    ("sw_q", 2, 4), ("sw_kv", 1, 6), ("merge_b", 4, 4), ("mix_out", 2, 4),
    ("mlp_up_a", 4, 4), ("mlp_down_a", 4, 2), ("mlp_up_b", 4, 4), ("mlp_down_b", 4, 2),
    ("ple", 4, 4),
]
PER = {name: per for name, _, per in PHASES}
HALF = {"ffn_a": 12, "ffn_b": FC - 12, "mlp_a": F2C // 2, "mlp_b": F2C // 2}
SPLIT0 = {"ffn_a": 0, "ffn_b": 12, "merged": FC, "mlp_a": FC + 8, "mlp_b": FC + 8 + F2C // 2}
ML_AT = [0, 512, 896, 1152]
PAIR0, TILE0 = {}, {}
_r, _t = 0, 2
for _name, _pairs, _tiles in PHASES:
    PAIR0[_name], TILE0[_name] = _r, _t
    _r += _pairs
    _t += max(_pairs, 1) * _tiles
NPAIRS, NTILES = _r, _t


def loop(engine, n):
    from contextlib import nullcontext
    return engine.Fori(0, n) if n > 1 else nullcontext(0)


def cols(buf, first, n=S):
    return buf[:, bass.ds(first, n)]


class Count:

    def __init__(self, sem):
        self.sem, self.n, self.i, self.per = sem, 0, 0, 0

    def enter(self, i, per):
        self.i, self.per, self.start = i, per, self.n

    def leave(self, steps):
        assert self.n - self.start == self.per, (self.n - self.start, self.per)
        self.n = self.start + steps * self.per
        self.i, self.per = 0, 0

    @property
    def at(self):
        return self.n + self.per * self.i if self.per else self.n


def nsa_units():
    units = []
    for qt in range(NT):
        units.append(dict(qt=qt, br=0, k0=0, nk=NCMP, first=True, last=False))
        units.append(dict(qt=qt, br=1, k0=0, nk=(qt + 1) * P, first=False, last=False))
        units.append(dict(qt=qt, br=2, k0=0, nk=(qt + 1) * P, first=False, last=qt == NT - 1))
    return units


def sw_units():
    return [dict(qt=qt, br=0, k0=max(qt - 1, 0) * P, nk=P if qt == 0 else 2 * P, first=True, last=qt == NT - 1)
            for qt in range(NT)]


def ca_units():
    return [dict(qt=qt, hp=hp, nk=MEM, first=True, last=True) for hp in range(2) for qt in range(NT)]


def program(nc, a, out):
    with ExitStack() as ctx:
        def sb(name, shape, dt=F32):
            return ctx.enter_context(nc.sbuf_tensor(name, shape, dt))

        def sem(name):
            return ctx.enter_context(nc.semaphore(name))

        at = [nc.sbuf_base // 4 if nc.sbuf_base % 32 == 0 else (nc.sbuf_base // 32 + 1) * 8]

        def sb(name, shape, dt=F32, twin=False):
            rows, n = shape
            size = 2 if dt == BF16 else 4
            words = -(-n * size // 32) * 8
            base = at[0] * 4
            at[0] += words
            t = nc.alloc_sbuf_tensor_at(name, [rows, n], dt, offset=base)
            if twin:
                return t, nc.alloc_sbuf_tensor_at(name + "_r", [rows, n], F32R, offset=base)
            return t

        def view(name, shape, on, first=0):
            return on[0:shape[0], first:first + shape[1]]

        xt = sb("xt", [P, KD * S])
        h_hi = sb("h_hi", [P, KD * S], F32R)
        h_lo = sb("h_lo", [P, KD * S], F32R)
        ring = sb("ring", [P, 2 * PANEL])
        w_hi32, w_hi = sb("w_hi", [P, 2 * PANEL], twin=True)
        w_lo = sb("w_lo", [P, 2 * PANEL], F32R)
        big, big_r = sb("big", [P, 32 * S], twin=True)
        params = sb("params", [P, NPAR])
        wi_hi = sb("wi_hi", [P, KD * 8], F32R)
        wi_lo = sb("wi_lo", [P, KD * 8], F32R)
        ident = sb("ident", [P, P])
        ones = sb("ones", [P, P])
        ident_bf = sb("ident_bf", [P, P], BF16)
        causal = sb("causal", [P, P], BF16)
        band = sb("band", [P, 2 * P], BF16)
        cmp_mask = sb("cmp_mask", [P, NT * NCMP], BF16)
        cmp_any = sb("cmp_any", [P, NT])
        ml_mask = sb("ml_mask", [P, P])
        eps = sb("eps", [P, 1])
        start = sb("start", [P, 3])
        acc = sb("acc", [P, S])
        sqt = sb("sqt", [P, S])
        rstd = sb("rstd", [P, S])
        tmp = sb("tmp", [P, 2 * S])
        o_acc = sb("o_acc", [P, 2 * S])
        act_o = o_acc
        gates = sb("gates", [P, NT * 48])
        hid = sb("hid", [P, 2 * 2 * CMPW])
        kcmp = sb("kcmp", [P, CMPW])
        vcmp = sb("vcmp", [NCMP, G * HD])
        probs, probs_r = sb("probs", [P, 2 * 2 * S], twin=True)
        probs_t, probs_tr = sb("probs_t", [P, 2 * 2 * S], twin=True)
        q_st = sb("q_st", [P, 4 * S])
        negmax = sb("negmax", [P, 4])
        total = sb("total", [P, 4])
        coef = sb("coef", [P, 8])
        sink_arg = sb("sink_arg", [P, 4])
        sink_e = sb("sink_e", [P, 4])
        neg_sink = sb("neg_sink", [P, 16])
        u_col = sb("u_col", [P, NT * MLH])
        assert at[0] * 4 <= nc.sbuf_usable_end, (at[0] * 4, nc.sbuf_usable_end)

        w2_k = view("w2_k", [P, 2 * P], probs)
        w2_v = view("w2_v", [P, 2 * HD], probs, 2 * P)
        w_gate = view("w_gate", [P, KD * 48], probs_t)
        wg_hi = view("wg_hi", [P, KD * 48], probs_tr, S)
        wg_lo = view("wg_lo", [P, KD * 48], probs_tr, 2 * S)
        w_if = view("w_if", [P, KD * 8], probs_t, 3 * S)
        ig, fz, fe, fcum = (view(n, [MLH, S], probs, i * S) for i, n in enumerate(("ig", "fz", "fe", "fcum")))
        u_row, m_row, nm_row = (view(n, [MLH, S], q_st, (1 + i) * S) for i, n in enumerate(("u", "m", "nm")))
        mem_raw = view("mem_raw", [P, KD * MEM], big, 16 * S)
        mem_hi = view("mem_hi", [P, KD * MEM], big_r, 20 * S)
        mem_lo = view("mem_lo", [P, KD * MEM], big_r, 24 * S)
        memk = view("memk", [P, KD * MEM], big, 28 * S)
        memv = view("memv", [P, 2 * D], big, 16 * S)
        ple_raw = view("ple_raw", [P, 2 * S], q_st)
        ple_hi = view("ple_hi", [P, 2 * S], probs_r)
        ple_lo = view("ple_lo", [P, 2 * S], probs_r, 2 * S)

        psum = ctx.enter_context(nc.psum_tensor("psum", [P, 8, S], F32))

        def bank(b, n=S):
            return psum[:, b, 0:n]

        def chunk(i):
            return big[:, i * S:(i + 1) * S]

        def chunk_r(i):
            return big_r[:, i * S:(i + 1) * S]

        def plain(x):
            return x.bitcast(F32)

        w_full = [sem("w_full0"), sem("w_full1")]
        hi_done = [sem("hi_done0"), sem("hi_done1")]
        lo_done = [sem("lo_done0"), sem("lo_done1")]
        slot0_free = sem("slot0_free")
        tile_done = sem("tile_done")
        evac = [sem("evac0"), sem("evac1")]
        x_in, mem_in, par_in, small_in, ple_in = (sem(n) for n in ("x_in", "mem_in", "par_in", "small_in", "ple_in"))
        consts, zeroed = sem("consts"), sem("zeroed")
        dve_step, pool_step = sem("dve_step"), sem("pool_step")
        squares = sem("squares")
        stat = sem("stat")
        std_done = sem("std_done")
        raw_x, hi_x = sem("raw_x"), sem("hi_x")
        normed = sem("normed")
        split_done = sem("split_done")
        squared = sem("squared")
        small_split = sem("small_split")
        shifted = sem("shifted")
        blocks = sem("blocks")
        conv_done = sem("conv_done")
        gated = sem("gated")
        ml_step = {n: sem("ml_" + n) for n in (
            "u_col", "z", "e", "l", "rows", "bc", "bc_used", "scores", "decay", "weighted", "sums", "recip", "h",
            "sq", "ssq", "std", "y")}
        att = {}
        for name in ("nsa", "ca", "sw"):
            att[name] = {n: sem(f"{name}_{n}") for n in (
                "staged", "scores", "negmax", "probs", "transposed", "copied_a", "copied_d", "summed",
                "combined", "turned", "stored", "split")}
        final_out = sem("final_out")
        stored = sem("stored")

        def half(name, i, k):
            per = PER[name]
            return TILE0[name] // 2 + (per // 2) * i + k // 2

        block = ctx.enter_context(nc.Block())

        NU = len(nsa_units())
        def att_dims(name):
            return {"nsa": (PAIRS // 2, 2, NU), "sw": (PAIRS // 2, 2, NT), "ca": (1, 2 * NT, 1)}[name]

        @block.sync
        def _(sp):
            def load(r, j):
                sp.dma_start(ring[:, j * PANEL:(j + 1) * PANEL], a["panels"][2 * r + j]).then_inc(w_full[j], 16)

            sp.dma_start(xt[:, 0:4 * S], a["x"][:, 0:4 * S]).then_inc(x_in, 16)
            sp.dma_start(xt[:, 4 * S:8 * S], a["x"][:, 4 * S:8 * S]).then_inc(x_in, 16)
            for j in range(2):
                load(0, j)
            with sp.Fori(1, NPAIRS) as r:
                for j in range(2):
                    sp.wait_ge(lo_done[j], r)
                    load(r, j)
            for c in range(KD):
                sp.wait_ge(final_out, c + 1)
                sp.dma_start(out[:, c * S:(c + 1) * S], chunk(c)).then_inc(stored, 16)
            sp.wait_ge(stored, 16 * KD)

        @block.tensor
        def _(pe):
            def mm(o, l, r, start, stop, **kw):
                return nc.tensor.matmul(o, l, r, start=start, stop=stop, **kw)

            def weights_here(name, i, j):
                pe.wait_ge(lo_done[j], PAIR0[name] + 1 + i)

            def bank_free(name, i, k):
                pe.wait_ge(evac[k % 2], half(name, i, k))

            def mm3(o, l, r, first, last):
                mm(o, l[0], r[0], first, False)
                mm(o, l[0], r[1], False, False)
                return mm(o, l[1], r[0], False, last)

            def w(at_, n=P):
                return w_hi[:, at_:at_ + n], w_lo[:, at_:at_ + n]

            def product(name, pairs, rhs, n=S, fresh=None, tile=bank):
                with loop(pe, pairs) as i:
                    for j in range(2):
                        weights_here(name, i, j)
                        for t in range(2):
                            bank_free(name, i, 2 * j + t)
                            for k in range(KD):
                                if fresh is not None and j == 0 and t == 0:
                                    pe.wait_ge(normed, KD * fresh + k + 1)
                                last = mm3(bank(t, n), w(j * PANEL + (t * KD + k) * P), rhs(k), k == 0, k == KD - 1)
                            last.then_inc(tile_done, 1)

            def product_tokens(name, pairs, lhs, tiles_, fresh=None):
                with loop(pe, pairs) as i:
                    for b in range(2):
                        pe.wait_ge(evac[b], half(name, i, 0))
                    for j in range(2):
                        weights_here(name, i, j)
                        for t in range(tiles_):
                            for k in range(4):
                                if fresh is not None and t == 0:
                                    pe.wait_ge(normed, KD * fresh + 4 * j + k + 1)
                                last = mm3(bank(TOKEN_BANK[t]), lhs(4 * j + k, t), w(j * PANEL + k * S, S),
                                           j == 0 and k == 0, j == 1 and k == 3)
                            if j == 1:
                                last.then_inc(tile_done, 1)
                        if j == 0:
                            last.then_inc(slot0_free, 1)

            def product_down(name, n_k, done):
                with pe.Fori(0, 4) as i:
                    for j in range(2):
                        weights_here(name, i, j)
                        bank_free(name, i, j)
                        for k in range(n_k):
                            if j == 0:
                                pe.wait_ge(split_done, done + k + 1)
                            last = mm3(bank(j), w(j * PANEL + k * P), (chunk_r(k), chunk_r(16 + k)), k == 0,
                                       k == n_k - 1)
                        last.then_inc(tile_done, 1)

            def partition_sum(m, b, n=S):
                pe.wait_ge(squares, KD * (m + 1))
                mm(bank(b, n), ones[:, :], acc[:, 0:n], True, True).then_inc(stat, 1)

            def attention(name, qk, mask, pv, units):
                s = att[name]
                steps, groups, per = att_dims(name)
                flat = [u for _ in range(groups) for u in units] if name != "ca" else units
                n_units = len(flat)
                with loop(pe, steps) as i:
                    u0 = n_units * i

                    def scores(u):
                        g = u // per
                        if u % per == 0 and name != "ca":
                            pe.wait_ge(s["staged"], groups * i + g + 1)
                        if u >= 2:
                            pe.wait_ge(s["probs"], u0 + (u - 1))
                        for hd in range(2):
                            ops = qk(flat[u], g % 2, hd)
                            b = 2 + 2 * (u % 2) + hd
                            m = mask(flat[u])
                            for n, (l, r) in enumerate(ops):
                                last = mm(bank(b, flat[u]["nk"]), l, r, n == 0, m is None and n == len(ops) - 1)
                            if m is not None:
                                c0 = flat[u]["nk"] - m.shape[1]
                                last = mm(psum[:, b, c0:flat[u]["nk"]], ident_bf[:, :], m, False, True)
                        last.then_inc(s["scores"], 1)

                    def transposes(u):
                        pe.wait_ge(s["probs"], u0 + (u + 1))
                        if u >= 1:
                            pe.wait_ge(s["copied_a"], u0 + u)
                            pe.wait_ge(s["copied_d"], u0 + u)
                        nk = flat[u]["nk"]
                        for hd in range(2):
                            for k in range(0, nk, P):
                                w = min(P, nk - k)
                                p0 = (2 * (u % 2) + hd) * S + k
                                last = nc.tensor.transpose(psum[0:w, 6 + hd, k:k + P], probs[:, p0:p0 + w], ident[:, :])
                        last.then_inc(s["transposed"], 1)

                    def values(u):
                        g = u // per
                        pe.wait_ge(s["copied_a"], u0 + (u + 1))
                        pe.wait_ge(s["copied_d"], u0 + (u + 1))
                        if u >= 1:
                            pe.wait_ge(s["combined"], u0 + u)
                        for hd in range(2):
                            ops, o0, ow = pv(flat[u], g % 2, hd, u % 2)
                            for n, (l, r) in enumerate(ops):
                                last = mm(psum[:, 0, o0:o0 + ow], l, r, n == 0, n == len(ops) - 1)
                        last.then_inc(s["summed"], 1)

                    def turn(g):
                        pe.wait_ge(s["combined"], u0 + per * (g + 1))
                        if g:
                            pe.wait_ge(s["split"], groups * i + g)
                        for t in range(NT):
                            o0 = (g % 2) * S + t * P
                            last = nc.tensor.transpose(psum[:, 1, t * P:(t + 1) * P], o_acc[:, o0:o0 + P], ident[:, :])
                        last.then_inc(s["turned"], 1)

                    scores(0)
                    for u in range(n_units):
                        if u + 1 < n_units:
                            scores(u + 1)
                        if u >= 1:
                            values(u - 1)
                        if u >= 2 and flat[u - 2]["last"]:
                            turn((u - 2) // per)
                        transposes(u)
                    values(n_units - 1)
                    if n_units > 1 and flat[n_units - 2]["last"]:
                        turn((n_units - 2) // per)
                    turn(groups - 1)

            pe.wait_ge(consts, 1)
            hk = lambda k: (h_hi[:, k * S:(k + 1) * S], h_lo[:, k * S:(k + 1) * S])
            htok = lambda k, t: tuple(x[:, k * S + t * P:k * S + (t + 1) * P] for x in (h_hi, h_lo))
            partition_sum(0, 2)
            product_tokens("nsa_v", 1, htok, 4, fresh=0)
            pe.wait_ge(small_split, 4)
            for t in range(NT):
                bank_free("nsa_g", 0, t)
                for k in range(KD):
                    last = mm3(bank(t % 2, 48), htok(k, t), (wg_hi[:, k * 48:(k + 1) * 48], wg_lo[:, k * 48:(k + 1) * 48]),
                               k == 0, k == KD - 1)
                last.then_inc(tile_done, 1)
            product("cmp_kv", 1, hk)
            product("nsa_k", 1, hk)
            with pe.Fori(0, 2) as i:
                pe.wait_ge(blocks, 16 * i + 16)
                for b in range(2):
                    pe.wait_ge(evac[b], half("cmp_w1", i, 0))
                for j in range(2):
                    weights_here("cmp_w1", i, j)
                    for t in range(2):
                        for k in range(8):
                            w0 = j * PANEL + k * 2 * P + t * P
                            last = mm(bank(t, CMPW), w_hi32[:, w0:w0 + P],
                                      cols(big, i * (4 * S) + 24 * S + (8 * j + k) * CMPW, CMPW),
                                      j == 0 and k == 0, j == 1 and k == 7)
                        if j == 1:
                            last.then_inc(tile_done, 1)
                    if j == 0:
                        last.then_inc(slot0_free, 1)
            for b in range(2):
                pe.wait_ge(evac[b], half("cmp_w2", 0, 0))
            pe.wait_ge(small_in, 64)
            for k in range(2):
                last = mm(bank(0, CMPW), w2_k[:, k * P:(k + 1) * P], hid[:, k * CMPW:(k + 1) * CMPW], k == 0, k == 1)
            last.then_inc(tile_done, 1)
            for g in range(G):
                for k in range(2):
                    h0 = (2 + k) * CMPW + g * NCMP
                    last = mm(psum[0:NCMP, 1, g * HD:(g + 1) * HD], hid[:, h0:h0 + NCMP],
                              w2_v[:, k * HD:(k + 1) * HD], k == 0, k == 1)
            last.then_inc(tile_done, 1)
            partition_sum(1, 2, MEM)
            product("nsa_q", 2, hk)

            def nsa_qk(u, par, hd):
                q0 = (2 * par + hd) * S + u["qt"] * P
                q = q_st[:, q0:q0 + P]
                if u["br"] == 0:
                    k0 = (2 * par + hd) * NCMP
                    return [(q, kcmp[:, k0:k0 + NCMP])]
                k0 = (8 + 2 * (u["br"] - 1) + par) * S
                return [(q, big[:, k0:k0 + u["nk"]])]

            def nsa_mask(u):
                return cmp_mask[:, u["qt"] * NCMP:(u["qt"] + 1) * NCMP] if u["br"] == 0 else causal[:, :]

            def nsa_pv(u, par, hd, up):
                p0 = (2 * up + hd) * S
                if u["br"] == 0:
                    v0 = 2 * par * HD
                    return [(probs_t[0:NCMP, p0:p0 + P], vcmp[:, v0:v0 + P])], hd * P, P
                ops = []
                for kt in range(u["nk"] // P):
                    v0 = (12 + kt) * S + (u["br"] - 1) * 256 + 2 * par * HD
                    ops.append((probs_t[:, p0 + kt * P:p0 + (kt + 1) * P], big[:, v0:v0 + P]))
                return ops, hd * P, P

            attention("nsa", nsa_qk, nsa_mask, nsa_pv, nsa_units())
            pe.wait_ge(att["nsa"]["split"], PAIRS)
            product("nsa_out", 2, hk)
            partition_sum(2, 2)
            pe.wait_ge(normed, KD * 2)
            product("mem_k", 2, lambda k: (mem_hi[:, k * MEM:(k + 1) * MEM], mem_lo[:, k * MEM:(k + 1) * MEM]), MEM)
            product_tokens("mem_v", 2, lambda k, t: tuple(x[:, k * MEM + t * P:k * MEM + (t + 1) * P]
                                                          for x in (mem_hi, mem_lo)), 2)
            product("ca_q", 2, hk, fresh=2)

            def ca_qk(u, par, hd):
                h = 2 * u["hp"] + hd
                return [(big[:, (2 * h + c) * S + u["qt"] * P:(2 * h + c) * S + (u["qt"] + 1) * P],
                         memk[:, (2 * h + c) * MEM:(2 * h + c + 1) * MEM]) for c in range(2)]

            def ca_pv(u, par, hd, up):
                h = 2 * u["hp"] + hd
                p0 = (2 * up + hd) * S
                return [(probs_t[:, p0 + kt * P:p0 + (kt + 1) * P],
                         memv[:, kt * D + h * 256:kt * D + (h + 1) * 256]) for kt in range(2)], hd * 256, 256

            pe.wait_ge(evac[0], half("ca_out", 0, 0))
            pe.wait_ge(evac[1], half("ca_out", 0, 0))
            attention("ca", ca_qk, lambda u: None, ca_pv, ca_units())
            pe.wait_ge(att["ca"]["split"], 2 * NT)
            product("ca_out", 2, hk)
            partition_sum(3, 2)
            product("ffn_up_a", HALF["ffn_a"] // 2, hk, fresh=3)
            product_down("ffn_down_a", HALF["ffn_a"], SPLIT0["ffn_a"])
            product("ffn_up_b", HALF["ffn_b"] // 2, hk)
            product_down("ffn_down_b", HALF["ffn_b"], SPLIT0["ffn_b"])
            partition_sum(4, 2)
            partition_sum(5, 2)
            product("ml_qk", 2, hk, fresh=4)
            product_tokens("ml_v", 2, htok, 4)
            product("ml_o", 2, hk)
            for t in range(2):
                bank_free("ml_if", 0, t)
                for k in range(KD):
                    g0 = k * 8 + 4 * t
                    last = mm3(psum[0:MLH, t, :], (wi_hi[:, g0:g0 + 4], wi_lo[:, g0:g0 + 4]), hk(k), k == 0, k == KD - 1)
                last.then_inc(tile_done, 1)
            ml = ml_step
            pe.wait_ge(ml["rows"], 5)
            for st in range(NT):
                last = mm(psum[:, 2, st * MLH:(st + 1) * MLH], u_row[:, st * P:(st + 1) * P], ident[0:MLH, 0:MLH],
                          True, True)
            last.then_inc(ml["u_col"], 1)
            pe.wait_ge(ml["u_col"], 2)
            for t in range(2):
                pe.wait_ge(evac[t], TILE0["merge_a"] // 2)
            for h in range(MLH):
                if h:
                    pe.wait_ge(ml["recip"], 3 * h)
                    pe.wait_ge(ml["std"], h)
                mm(bank(6), ident[0:MLH, h:h + 1].to_broadcast([MLH, P]), m_row[:, :], True, True)
                mm(bank(7), ident[0:MLH, h:h + 1].to_broadcast([MLH, P]), nm_row[:, :], True, True).then_inc(ml["bc"], 1)
                for st in range(NT):
                    mm(psum[:, 2 + st, 0:S - st * P], big[:, (4 + h) * S + st * P:(4 + h) * S + (st + 1) * P],
                       big[:, h * S + st * P:(h + 1) * S], True, True).then_inc(ml["scores"], 1)
                pe.wait_ge(ml["bc_used"], 2 * (h + 1))
                if h:
                    pe.wait_ge(ml["h"], 2 * h)
                for st in range(NT):
                    pe.wait_ge(ml["weighted"], NT * h + st + 1)
                    pt = probs_t[:, ML_AT[st]:ML_AT[st] + S - st * P]
                    for dv in range(2):
                        v0 = (8 * S) + st * D + h * 256 + dv * P
                        mm(psum[:, dv, st * P:S], big[:, v0:v0 + P], pt, st == 0, st == NT - 1)
                    last = mm(psum[:, 6, st * P:S], ones[:, :], pt, st == 0, st == NT - 1)
                last.then_inc(ml["sums"], 1)
                pe.wait_ge(ml["sq"], 2 * h + 2)
                for dv in range(2):
                    last = mm(bank(7), ones[:, :], chunk(28 + dv), dv == 0, dv == 1)
                last.then_inc(ml["ssq"], 1)
            pe.wait_ge(ml["y"], 2 * MLH)

            def merge(name, rhs, k1=KD, fresh=None):
                with pe.Fori(0, 4) as i:
                    for j in range(2):
                        weights_here(name, i, j)
                        for t in range(2):
                            bank_free(name, i, 2 * j + t)
                            n_k = KD if t == 0 else k1
                            for k in range(n_k):
                                if fresh is not None and j == 0 and t == 0:
                                    pe.wait_ge(normed, KD * fresh + k + 1)
                                last = mm3(bank(t), w(j * PANEL + (t * KD + k) * P), hk(k) if t == 0 else rhs(k),
                                           k == 0, k == n_k - 1)
                            last.then_inc(tile_done, 1)

            merge("merge_a", lambda k: (chunk_r(16 + k), chunk_r(k // 2 + 4 * (k % 2))))
            product("sw_q", 2, hk)
            for j in range(2):
                weights_here("sw_kv", 0, j)
                for t in range(2 if j == 0 else NT):
                    bank_free("sw_kv", 0, t + 2 * j)
                    for k in range(KD):
                        if j == 0:
                            last = mm3(bank(t), w((t * KD + k) * P), hk(k), k == 0, k == KD - 1)
                        else:
                            last = mm3(bank(t % 2, 256), htok(k, t), w(PANEL + k * 256, 256), k == 0, k == KD - 1)
                    last.then_inc(tile_done, 1)

            def sw_qk(u, par, hd):
                q0 = (2 * par + hd) * S + u["qt"] * P
                k0 = (24 + par) * S + u["k0"]
                return [(q_st[:, q0:q0 + P], big[:, k0:k0 + u["nk"]])]

            def sw_mask(u):
                return causal[:, :] if u["qt"] == 0 else band[:, :]

            def sw_pv(u, par, hd, up):
                p0 = (2 * up + hd) * S
                ops = []
                for n in range(u["nk"] // P):
                    v0 = 26 * S + (u["k0"] // P + n) * 256 + 2 * par * HD
                    ops.append((probs_t[:, p0 + n * P:p0 + (n + 1) * P], big[:, v0:v0 + P]))
                return ops, hd * P, P

            attention("sw", sw_qk, sw_mask, sw_pv, sw_units())
            pe.wait_ge(att["sw"]["split"], PAIRS)
            merge("merge_b", lambda k: (chunk_r(k), chunk_r(16 + k)))
            pe.wait_ge(split_done, SPLIT0["mlp_a"])
            product("mix_out", 2, lambda k: (chunk_r(8 + k), chunk_r(24 + k)))
            partition_sum(6, 2)
            product("mlp_up_a", F2C // 8, hk, fresh=5)
            product_down("mlp_down_a", HALF["mlp_a"], SPLIT0["mlp_a"])
            product("mlp_up_b", F2C // 8, hk)
            product_down("mlp_down_b", HALF["mlp_b"], SPLIT0["mlp_b"])
            partition_sum(7, 2)
            pe.wait_ge(small_split, 6)
            merge("ple", lambda k: (ple_hi[:, k * S:(k + 1) * S], ple_lo[:, k * S:(k + 1) * S]), k1=PLE // P, fresh=6)
            partition_sum(8, 2)

        @block.scalar
        def _(act):
            act.dma_start(params[:, :], a["params"]).then_inc(par_in, 16)
            for dst, src in ((w_gate, "w_gate"), (w_if, "w_if"), (w2_k, "w2_k"), (w2_v, "w2_v")):
                act.dma_start(dst, a[src]).then_inc(small_in, 16)

            def hi(r, j, whole=False):
                act.wait_ge(w_full[j], 16 * r + 16)
                dst = w_hi32 if whole else w_hi
                nc.scalar.copy(dst[:, j * PANEL:(j + 1) * PANEL], ring[:, j * PANEL:(j + 1) * PANEL]) \
                    .then_inc(hi_done[j], 1)

            def norm(m, b, n=S):
                act.wait_ge(stat, m + 1)
                nc.scalar.activation(rstd[:, 0:n], bank(b, n), ACT.Sqrt, bias=eps[:, 0:1], scale=1.0 / D) \
                    .then_inc(std_done, 1)

            def norm_hi(m, hi_buf, n=S):
                for c in range(KD):
                    act.wait_ge(raw_x, KD * m + c + 1)
                    nc.scalar.copy(hi_buf[:, c * n:(c + 1) * n], tmp[:, (c % 2) * S:(c % 2) * S + n]) \
                        .then_inc(hi_x, 1)

            def phase(name, pairs, slot, last=False, tokens=None):
                def pair(i, next_):
                    for j in range(2):
                        if tokens is not None and j == 0:
                            if next_:
                                act.wait_ge(slot0_free, tokens + i + 1)
                                hi(PAIR0[name] + 1 + i, 0)
                            continue
                        slot(i, j)
                        if next_:
                            hi(PAIR0[name] + 1 + i, j)

                with loop(act, pairs - 1 if last else pairs) as i:
                    pair(i, True)
                if last:
                    pair(pairs - 1, False)

            def wait_tile(name, i, k):
                act.wait_ge(tile_done, TILE0[name] + k + 1 + PER[name] * i)

            def take(name, pairs, dst, n=S, func=ACT.Copy, scale=1.0, tokens=None, banks=(0, 1, 0, 1)):
                def slot(i, j):
                    ks = range(PER[name]) if tokens is not None else range(2 * j, 2 * j + 2)
                    for k in ks:
                        wait_tile(name, i, k)
                        nc.scalar.activation(dst(i, k), bank(banks[k], n), func, scale=scale).then_inc(evac[k % 2], 1)
                phase(name, pairs, slot, tokens=tokens)

            def through(name, pairs):
                def slot(i, j):
                    per = PER[name] // 2
                    wait_tile(name, i, per * j + per - 1)
                phase(name, pairs, slot)

            def attention(name, units, dst, sinks=False):
                s = att[name]
                steps, groups, per = att_dims(name)
                flat = [u for _ in range(groups) for u in units] if name != "ca" else units
                n_units = len(flat)
                with loop(act, steps) as i:
                    u0 = n_units * i

                    def exps(u):
                        par, nk = u % 2, flat[u]["nk"]
                        act.wait_ge(s["negmax"], u0 + (u + 1))
                        if u >= 2:
                            act.wait_ge(s["transposed"], u0 + (u - 1))
                        for hd in range(2):
                            x = 2 * par + hd
                            last = nc.scalar.activation(probs[:, x * S:x * S + nk], bank(2 + x, nk), ACT.Exp,
                                                        bias=negmax[:, x:x + 1], accum_out=total[:, x:x + 1])
                        if sinks:
                            last = nc.scalar.activation(sink_e[:, 2 * par:2 * par + 2],
                                                        sink_arg[:, 2 * par:2 * par + 2], ACT.Exp)
                        last.then_inc(s["probs"], 1)

                    def copy(u):
                        par, nk = u % 2, flat[u]["nk"]
                        act.wait_ge(s["transposed"], u0 + (u + 1))
                        if u >= 2:
                            act.wait_ge(s["summed"], u0 + (u - 1))
                        h, w = min(nk, P), max(nk, P)
                        nc.scalar.copy(probs_t[0:h, 2 * par * S:2 * par * S + w], psum[0:h, 6, 0:w]) \
                            .then_inc(s["copied_a"], 1)

                    def store(g):
                        act.wait_ge(s["turned"], groups * i + (g + 1))
                        nc.scalar.copy(dst(i, g), psum[:, 1, :] if name != "ca" else
                                       psum[:, 1, :].rearrange("p (c t) -> p c t", c=4)).then_inc(s["stored"], 1)

                    exps(0)
                    for u in range(n_units):
                        if u + 1 < n_units:
                            exps(u + 1)
                        if u >= 2 and flat[u - 2]["last"]:
                            store((u - 2) // per)
                        copy(u)
                    if n_units > 1 and flat[n_units - 2]["last"]:
                        store((n_units - 2) // per)
                    store(groups - 1)

            for j in range(2):
                hi(0, j)
            act.wait_ge(consts, 1)
            norm(0, 2)
            norm_hi(0, h_hi)
            take("nsa_v", 1, lambda i, k: chunk(12 + k), tokens=0, banks=TOKEN_BANK)
            for k in range(NT):
                wait_tile("nsa_g", 0, k)
                nc.scalar.activation(gates[:, k * 48:(k + 1) * 48], bank(k % 2, 48), ACT.Sigmoid).then_inc(evac[k % 2], 1)

            def cmp_input(i, j):
                for k in range(2 * j, 2 * j + 2):
                    wait_tile("cmp_kv", i, k)
                    for g in range(2):
                        src = psum[64 * g:64 * g + 64, k % 2, :]
                        dst = chunk(16 + 2 * k + g)
                        nc.scalar.copy(dst[0:64, :], src)
                        last = nc.scalar.copy(dst[64:P, 0:S - 1], src[:, 1:S])
                    last.then_inc(evac[k % 2], 1)

            phase("cmp_kv", 1, cmp_input)
            for j in range(2):
                for k in range(2 * j, 2 * j + 2):
                    wait_tile("nsa_k", 0, k)
                    nc.scalar.copy(chunk(8 + k), bank(k % 2)).then_inc(evac[k % 2], 1)
                hi(PAIR0["cmp_w1"], j, whole=True)
            act.wait_ge(blocks, 32)
            act.dma_start(mem_raw, a["mem"]).then_inc(mem_in, 16)
            for i in range(2):
                act.wait_ge(slot0_free, 2 + i)
                hi(PAIR0["cmp_w1"] + 1 + i, 0, whole=i == 0)
                for k in range(2):
                    wait_tile("cmp_w1", i, k)
                    h0 = (2 * i + k) * CMPW
                    nc.scalar.activation(hid[:, h0:h0 + CMPW], bank(k, CMPW), ACT.Gelu_apprx_tanh).then_inc(evac[k], 1)
                hi(PAIR0["cmp_w1"] + 1 + i, 1, whole=i == 0)
            wait_tile("cmp_w2", 0, 0)
            nc.scalar.copy(kcmp[:, :], bank(0, CMPW)).then_inc(evac[0], 1)
            wait_tile("cmp_w2", 0, 1)
            nc.scalar.copy(vcmp[:, :], psum[0:NCMP, 1, 0:G * HD]).then_inc(evac[1], 1)
            norm(1, 2, MEM)
            norm_hi(1, mem_hi, MEM)
            take("nsa_q", 2, lambda i, k: cols(big, 4 * S * i + k * S), scale=HD ** -0.5)
            attention("nsa", nsa_units(), lambda i, g: cols(h_hi, 4 * g * S + S * i))
            through("nsa_out", 2)
            norm(2, 2)
            norm_hi(2, h_hi)
            take("mem_k", 2, lambda i, k: cols(memk, 4 * MEM * i + k * MEM, MEM), MEM)
            take("mem_v", 2, lambda i, k: cols(memv, S * i + k * D), tokens=3, banks=TOKEN_BANK)
            take("ca_q", 2, lambda i, k: cols(big, 4 * S * i + k * S), scale=256 ** -0.5)
            attention("ca", ca_units(), lambda i, g: h_hi[:, :].rearrange("p (c t) -> p c t", c=KD)
                      [:, 4 * (g // NT):4 * (g // NT) + 4, (g % NT) * P:(g % NT + 1) * P])
            through("ca_out", 2)
            norm(3, 2)
            norm_hi(3, h_hi)

            def ffn_gate(part, done):
                def slot(i, j):
                    act.wait_ge(evac[0], TILE0[part] // 2 + j + 1 + 2 * i)
                    nc.scalar.activation(act_o[:, j * S:(j + 1) * S], tmp[:, j * S:(j + 1) * S], ACT.Silu) \
                        .then_inc(gated, 1)
                    wait_tile(part, i, 2 * j + 1)
                return slot

            phase("ffn_up_a", HALF["ffn_a"] // 2, ffn_gate("ffn_up_a", 0))
            through("ffn_down_a", 4)
            phase("ffn_up_b", HALF["ffn_b"] // 2, ffn_gate("ffn_up_b", 12))
            through("ffn_down_b", 4)
            norm(4, 2)
            norm(5, 2)
            norm_hi(4, h_hi)

            def ml_silu(i, j):
                for k in range(2 * j, 2 * j + 2):
                    b = k % 2
                    act.wait_ge(evac[b], TILE0["ml_qk"] // 2 + k // 2 + 1 + 2 * i)
                    nc.scalar.activation(cols(big, 4 * S * i + k * S), tmp[:, b * S:(b + 1) * S], ACT.Silu) \
                        .then_inc(gated, 1)

            phase("ml_qk", 2, ml_silu)
            take("ml_v", 2, lambda i, k: cols(big, S * i + 8 * S + k * D), tokens=5, banks=TOKEN_BANK)
            take("ml_o", 2, lambda i, k: cols(big, 4 * S * i + (16 + k) * S), func=ACT.Sigmoid)
            ml = ml_step
            act.wait_ge(tile_done, TILE0["ml_if"] + 1)
            nc.scalar.activation(ig[:, :], psum[0:MLH, 0, :], ACT.Identity,
                                 bias=params[0:MLH, COL["b_i"]:COL["b_i"] + 1]).then_inc(evac[0], 1)
            act.wait_ge(ml["z"], 2)
            nc.scalar.activation(fe[:, :], fe[:, :], ACT.Exp, scale=-1.0).then_inc(ml["e"], 1)
            act.wait_ge(ml["e"], 1)
            nc.scalar.activation(fe[:, :], fe[:, :], ACT.Ln, bias=ones[0:MLH, 0:1]).then_inc(ml["l"], 1)
            act.wait_ge(ml["u_col"], 1)
            nc.scalar.copy(u_col[:, :], bank(2, NT * MLH)).then_inc(ml["u_col"], 1)
            act.wait_ge(ml["u_col"], 2)
            for h in range(MLH):
                act.wait_ge(ml["bc"], h + 1)
                if h:
                    act.wait_ge(ml["recip"], 3 * h)
                nc.scalar.copy(q_st[:, 0:S], bank(6)).then_inc(ml["bc_used"], 1)
                nc.scalar.activation(tmp[:, 0:S], bank(7), ACT.Exp).then_inc(ml["bc_used"], 1)
                act.wait_ge(ml["decay"], (NT + 1) * h + 1)
                if h:
                    act.wait_ge(ml["weighted"], NT * h)
                for st in range(NT):
                    e0 = 24 * S + ML_AT[st]
                    w = S - (st + 1) * P
                    uc = u_col[:, st * MLH + h:st * MLH + h + 1]
                    last = nc.scalar.activation(big[:, e0:e0 + P], q_st[:, S + st * P:S + (st + 1) * P], ACT.Exp,
                                                bias=uc, scale=-1.0)
                    if w:
                        last = nc.scalar.activation(big[:, e0 + P:e0 + P + w], q_st[:, (st + 1) * P:S], ACT.Exp,
                                                    bias=uc, scale=-1.0)
                    last.then_inc(ml["decay"], 1)
                for dv in range(2):
                    act.wait_ge(ml["h"], 2 * h + dv + 1)
                    nc.scalar.activation(chunk(28 + dv), o_acc[:, dv * S:(dv + 1) * S], ACT.Square) \
                        .then_inc(ml["sq"], 1)
                act.wait_ge(ml["ssq"], h + 1)
                nc.scalar.activation(rstd[:, :], bank(7), ACT.Sqrt, bias=eps[:, 0:1], scale=1.0 / 256) \
                    .then_inc(ml["std"], 1)

            def gate(name, last=False):
                def slot(i, j):
                    wait_tile(name, i, 2 * j)
                    act.wait_ge(evac[1], TILE0[name] // 2 + j - 1 + 2 * i)
                    nc.scalar.activation(act_o[:, j * S:(j + 1) * S], bank(0), ACT.Sigmoid).then_inc(evac[0], 1)
                    wait_tile(name, i, 2 * j + 1)
                phase(name, 4, slot, last=last)

            act.wait_ge(ml["y"], 2 * MLH)
            gate("merge_a")
            take("sw_q", 2, lambda i, k: cols(big, 4 * S * i + k * S), scale=HD ** -0.5)

            def sw_kv(i, j):
                for k in ((0, 1), (2, 3, 4, 5))[j]:
                    wait_tile("sw_kv", 0, k)
                    src = bank(k % 2) if k < 2 else bank(k % 2, 256)
                    dst = chunk(24 + k) if k < 2 else big[:, 26 * S + (k - 2) * 256:26 * S + (k - 1) * 256]
                    nc.scalar.copy(dst, src).then_inc(evac[k % 2], 1)

            phase("sw_kv", 1, sw_kv)
            attention("sw", sw_units(), lambda i, g: cols(big_r, 4 * g * S + S * i), sinks=True)
            act.wait_ge(att["sw"]["split"], PAIRS)
            act.dma_start(ple_raw, a["ple"]).then_inc(ple_in, 16)
            gate("merge_b")
            through("mix_out", 2)
            norm(6, 2)
            norm_hi(5, h_hi)

            def squared_relu(part, done):
                def slot(i, j):
                    for k in range(2 * j, 2 * j + 2):
                        b = k % 2
                        wait_tile(part, i, k)
                        nc.scalar.activation(act_o[:, b * S:(b + 1) * S], bank(b), ACT.Relu).then_inc(evac[b], 1)
                        act.wait_ge(evac[b], TILE0[part] // 2 + k // 2 + 1 + 2 * i)
                        act.wait_ge(split_done, done + k - 1 + 4 * i)
                        nc.scalar.activation(tmp[:, b * S:(b + 1) * S], act_o[:, b * S:(b + 1) * S], ACT.Square) \
                            .then_inc(squared, 1)
                return slot

            phase("mlp_up_a", 4, squared_relu("mlp_up_a", SPLIT0["mlp_a"]))
            through("mlp_down_a", 4)
            phase("mlp_up_b", 4, squared_relu("mlp_up_b", SPLIT0["mlp_b"]))
            through("mlp_down_b", 4)
            norm(7, 2)
            norm_hi(6, h_hi)
            gate("ple", last=True)
            norm(8, 2)

        @block.vector
        def _(dve):
            V = nc.vector
            d = Count(dve_step)
            sq = Count(squares)
            nm = Count(normed)

            def step(ins):
                ins.then_inc(dve_step, 1)
                d.n += 1

            def settle():
                dve.wait_ge(dve_step, d.at)

            def square(src, n=S):
                step(V.tensor_tensor(sqt[:, 0:n], src, src, ALU.mult))
                settle()
                V.tensor_tensor(acc[:, 0:n], acc[:, 0:n], sqt[:, 0:n], ALU.add).then_inc(squares, 1)
                sq.n += 1
                dve.wait_ge(squares, sq.at)

            def clear_acc():
                step(V.memset(acc[:, :], 0.0))
                settle()

            rx, ns, sp_ = Count(raw_x), Count(normed), Count(split_done)

            def scale_of(m, n=S):
                dve.wait_ge(std_done, m + 1)
                step(V.reciprocal(rstd[:, 0:n], rstd[:, 0:n]))
                settle()

            def norm(m, name, src, hi_buf, lo_buf, n=S):
                scale_of(m, n)

                def low(c):
                    dve.wait_ge(hi_x, ns.n + 1)
                    V.tensor_tensor(lo_buf[:, c * n:(c + 1) * n], tmp[:, (c % 2) * S:(c % 2) * S + n],
                                    plain(hi_buf[:, c * n:(c + 1) * n]), ALU.subtract).then_inc(normed, 1)
                    ns.n += 1

                for c in range(KD):
                    g0 = COL[name] + c
                    if ns.n >= 1:
                        dve.wait_ge(normed, ns.n)
                    V.scalar_tensor_tensor(out=tmp[:, (c % 2) * S:(c % 2) * S + n], in0=src(c),
                                           scalar=params[:, g0:g0 + 1], in1=rstd[:, 0:n], op0=ALU.mult,
                                           op1=ALU.mult).then_inc(raw_x, 1)
                    if c:
                        low(c - 1)
                low(KD - 1)

            def split(src, hi_, lo_):
                step(V.tensor_scalar(hi_, src, 1.0, None, ALU.mult))
                settle()
                V.tensor_tensor(lo_, src, plain(hi_), ALU.subtract).then_inc(split_done, 1)
                sp_.n += 1

            xc = lambda c: xt[:, c * S:(c + 1) * S]

            def residual(name, steps, per, squares_=True):
                if squares_:
                    clear_acc()
                with dve.Fori(0, steps) as i:
                    if squares_:
                        d.enter(i, per)
                        sq.enter(i, per)
                    for k in range(per):
                        b = k % 2
                        x = cols(xt, per * S * i + k * S)
                        dve.wait_ge(tile_done, TILE0[name] + k + 1 + per * i)
                        V.tensor_tensor(x, bank(b), x, ALU.add).then_inc(evac[b], 1)
                        if squares_:
                            dve.wait_ge(evac[b], TILE0[name] // 2 + k // 2 + 1 + (per // 2) * i)
                            square(x)
                if squares_:
                    d.leave(steps)
                    sq.leave(steps)

            def convolve(name, taps, col, n_ch, i, k, ch, bank_):
                t0 = (k % 2) * S
                for m in range(taps):
                    w = params[:, bass.ds(ch + (col + (taps - 1 - m) * n_ch), 1)]
                    src = psum[:, bank_, 0:S - m]
                    o = tmp[:, t0 + m:t0 + S]
                    if m == 0:
                        ins = V.tensor_scalar(o, src, w, None, ALU.mult)
                    else:
                        ins = V.scalar_tensor_tensor(out=o, in0=src, scalar=w, in1=o, op0=ALU.mult, op1=ALU.add)
                    if m < taps - 1:
                        step(ins)
                        settle()
                    else:
                        ins.then_inc(evac[bank_], 1)

            def attention(name, units, per_step, hi_of, lo_of, gate=None, sinks=False):
                s = att[name]
                steps, groups, per = att_dims(name)
                flat = [u for _ in range(groups) for u in units] if name != "ca" else units
                n_units = len(flat)
                width = 256 if name == "ca" else HD
                with loop(dve, steps) as i:
                    if steps > 1:
                        d.enter(i, per_step)
                    u0 = n_units * i

                    def maxima(u):
                        par, nk = u % 2, flat[u]["nk"]
                        dve.wait_ge(s["scores"], u0 + (u + 1))
                        nm_ = negmax[:, 2 * par:2 * par + 2]
                        ins = V.tensor_reduce(nm_, psum[:, 2 + 2 * par:4 + 2 * par, 0:nk], axis=AX_X, op=ALU.max,
                                              negate=True)
                        if sinks:
                            g = u // per
                            step(ins)
                            settle()
                            sink = bass.ds(8 * g + 2 * i, 2)
                            step(V.tensor_tensor(nm_, nm_, neg_sink[:, sink], ALU.min))
                            settle()
                            ins = V.tensor_tensor(sink_arg[:, 2 * par:2 * par + 2], nm_, neg_sink[:, sink],
                                                  ALU.subtract)
                        ins.then_inc(s["negmax"], 1)

                    def copy(u):
                        par, nk = u % 2, flat[u]["nk"]
                        dve.wait_ge(s["transposed"], u0 + (u + 1))
                        if u >= 2:
                            dve.wait_ge(s["summed"], u0 + (u - 1))
                        h, w = min(nk, P), max(nk, P)
                        V.tensor_copy(probs_t[0:h, (2 * par + 1) * S:(2 * par + 1) * S + w], psum[0:h, 7, 0:w]) \
                            .then_inc(s["copied_d"], 1)

                    def weights(u):
                        par, g = u % 2, u // per
                        t, c = total[:, 2 * par:2 * par + 2], coef[:, 2 * par:2 * par + 2]
                        if sinks:
                            step(V.tensor_tensor(t, t, sink_e[:, 2 * par:2 * par + 2], ALU.add))
                            settle()
                        step(V.reciprocal(c, t))
                        if gate is not None:
                            settle()
                            gt = gates[:, :].rearrange("p (x b) -> p x b", b=3)[
                                :, bass.ds(flat[u]["qt"] * 16 + 8 * g + 2 * i, 2), flat[u]["br"]]
                            if flat[u]["br"] == 0:
                                ins = V.scalar_tensor_tensor(out=c, in0=c, scalar=cmp_any[:, flat[u]["qt"]:flat[u]["qt"] + 1],
                                                             in1=gt, op0=ALU.mult, op1=ALU.mult)
                            else:
                                ins = V.tensor_tensor(c, c, gt, ALU.mult)
                            step(ins)

                    def combine(u):
                        par, g = u % 2, u // per
                        settle()
                        dve.wait_ge(s["summed"], u0 + (u + 1))
                        if not flat[u]["first"]:
                            dve.wait_ge(s["combined"], u0 + u)
                        for hd in range(2):
                            o0 = (g % 2) * S + hd * width + (0 if name == "ca" else flat[u]["qt"] * P)
                            o, c = o_acc[:, o0:o0 + width], coef[:, 2 * par + hd:2 * par + hd + 1]
                            s0 = hd * width if name == "ca" else hd * (P + HD)
                            src = psum[:, 0, s0:s0 + width]
                            if flat[u]["first"]:
                                last = V.tensor_scalar(o, src, c, None, ALU.mult)
                            else:
                                last = V.scalar_tensor_tensor(out=o, in0=src, scalar=c, in1=o, op0=ALU.mult,
                                                              op1=ALU.add)
                        last.then_inc(s["combined"], 1)

                    def low(g):
                        dve.wait_ge(s["stored"], groups * i + (g + 1))
                        src = psum[:, 1, :] if name != "ca" else psum[:, 1, :].rearrange("p (c t) -> p c t", c=4)
                        V.tensor_tensor(lo_of(i, g), src, plain(hi_of(i, g)), ALU.subtract).then_inc(s["split"], 1)

                    maxima(0)
                    for u in range(n_units):
                        if u + 1 < n_units:
                            maxima(u + 1)
                        if u >= 1:
                            combine(u - 1)
                        if u >= 2 and flat[u - 2]["last"]:
                            low((u - 2) // per)
                        copy(u)
                        weights(u)
                    combine(n_units - 1)
                    if n_units > 1 and flat[n_units - 2]["last"]:
                        low((n_units - 2) // per)
                    low(groups - 1)
                if steps > 1:
                    d.leave(steps)

            clear_acc()
            dve.wait_ge(x_in, 32)
            for c in range(KD):
                square(xc(c))
            dve.wait_ge(par_in, 16)
            step(V.tensor_scalar(neg_sink[:, :], params[:, COL["sink"]:COL["sink"] + 16], -1.0, None, ALU.mult))
            norm(0, "mix", xc, h_hi, h_lo)
            dve.wait_ge(small_in, 64)
            V.tensor_copy(wg_hi, w_gate).then_inc(small_split, 1)
            V.tensor_copy(wi_hi[:, :], w_if).then_inc(small_split, 1)
            dve.wait_ge(small_split, 2)
            V.tensor_tensor(wg_lo, w_gate, plain(wg_hi), ALU.subtract).then_inc(small_split, 1)
            V.tensor_tensor(wi_lo[:, :], w_if, plain(wi_hi[:, :]), ALU.subtract).then_inc(small_split, 1)
            clear_acc()
            dve.wait_ge(mem_in, 16)
            for c in range(KD):
                square(mem_raw[:, c * MEM:(c + 1) * MEM], MEM)
            norm(1, "mem", lambda c: mem_raw[:, c * MEM:(c + 1) * MEM], mem_hi, mem_lo, MEM)
            attention("nsa", nsa_units(), 2 * NU * 2, lambda i, g: cols(h_hi, 4 * g * S + S * i),
                      lambda i, g: cols(h_lo, 4 * g * S + S * i), gate=True)
            residual("nsa_out", 2, 4)
            norm(2, "cross", xc, h_hi, h_lo)

            def by_unit(buf):
                return lambda i, g: buf[:, :].rearrange("p (c t) -> p c t", c=KD)[
                    :, 4 * (g // NT):4 * (g // NT) + 4, (g % NT) * P:(g % NT + 1) * P]

            attention("ca", ca_units(), 0, by_unit(h_hi), by_unit(h_lo))
            residual("ca_out", 2, 4)
            norm(3, "ffn", xc, h_hi, h_lo)

            def ffn_hidden(part, steps, ch0):
                with dve.Fori(0, steps) as i:
                    d.enter(i, 6)
                    sp_.enter(i, 2)
                    for j in range(2):
                        dve.wait_ge(tile_done, TILE0[part] + 2 * j + 1 + 4 * i)
                        convolve(part, 3, COL["ffn_conv"] + ch0, FC, i, j, 2 * i + j, 0)
                        dve.wait_ge(tile_done, TILE0[part] + 2 * j + 2 + 4 * i)
                        dve.wait_ge(gated, ch0 + j + 1 + 2 * i)
                        if ch0 or j:
                            dve.wait_ge(split_done, sp_.at)
                        V.tensor_tensor(sqt[:, :], bank(1), act_o[:, j * S:(j + 1) * S], ALU.mult).then_inc(evac[1], 1)
                        dve.wait_ge(evac[1], TILE0[part] // 2 + j + 1 + 2 * i)
                        split(sqt[:, :], cols(big_r, 2 * S * i + j * S), cols(big_r, 2 * S * i + (16 + j) * S))
                d.leave(steps)
                sp_.leave(steps)

            ffn_hidden("ffn_up_a", HALF["ffn_a"] // 2, 0)
            residual("ffn_down_a", 4, 2, False)
            ffn_hidden("ffn_up_b", HALF["ffn_b"] // 2, HALF["ffn_a"])
            residual("ffn_down_b", 4, 2)
            scale_of(4)
            clear_acc()
            for c in range(KD):
                g0 = COL["final"] + c
                step(V.scalar_tensor_tensor(out=xc(c), in0=xc(c), scalar=params[:, g0:g0 + 1], in1=rstd[:, :],
                                            op0=ALU.mult, op1=ALU.mult))
                settle()
                square(xc(c))
            norm(5, "mix2", xc, h_hi, h_lo)
            with dve.Fori(0, 2) as i:
                d.enter(i, 12)
                for k in range(4):
                    dve.wait_ge(tile_done, TILE0["ml_qk"] + k + 1 + 4 * i)
                    dve.wait_ge(gated, FC + k - 1 + 4 * i)
                    convolve("ml_qk", 4, COL["ml_conv"], 8, i, k, 4 * i + k, k % 2)
            d.leave(2)
            ml = ml_step
            dve.wait_ge(tile_done, TILE0["ml_if"] + 2)
            V.tensor_scalar(fz[:, :], psum[0:MLH, 1, :], params[0:MLH, COL["b_f"]:COL["b_f"] + 1], None, ALU.add) \
                .then_inc(evac[1], 1)
            dve.wait_ge(evac[1], TILE0["merge_a"] // 2)
            V.tensor_scalar(fe[:, :], fz[:, :], -1.0, None, ALU.mult).then_inc(ml["z"], 1)
            dve.wait_ge(ml["z"], 1)
            V.tensor_tensor(fe[:, :], fe[:, :], fz[:, :], ALU.max).then_inc(ml["z"], 1)
            step(V.memset(sqt[:, :], 1.0))
            dve.wait_ge(ml["l"], 1)
            V.scalar_tensor_tensor(out=fz[:, :], in0=fz[:, :], scalar=0.0, in1=fe[:, :], op0=ALU.min,
                                   op1=ALU.subtract).then_inc(ml["rows"], 1)
            settle()
            dve.wait_ge(ml["rows"], 1)
            V.tensor_tensor_scan(fcum[:, :], sqt[0:MLH, :], fz[:, :], 0.0, ALU.mult, ALU.add).then_inc(ml["rows"], 1)
            dve.wait_ge(ml["rows"], 2)
            dve.wait_ge(evac[0], TILE0["merge_a"] // 2)
            V.tensor_tensor(u_row[:, :], ig[:, :], fcum[:, :], ALU.subtract).then_inc(ml["rows"], 1)
            dve.wait_ge(ml["rows"], 3)
            V.tensor_tensor_scan(m_row[:, :], u_row[:, :], u_row[:, :], 0.0, ALU.max, ALU.max).then_inc(ml["rows"], 1)
            dve.wait_ge(ml["rows"], 4)
            V.scalar_tensor_tensor(out=nm_row[:, :], in0=fcum[:, :], scalar=-1.0, in1=m_row[:, :], op0=ALU.mult,
                                   op1=ALU.subtract).then_inc(ml["rows"], 1)
            for h in range(MLH):
                dve.wait_ge(ml["bc_used"], 2 * h + 1)
                V.tensor_tensor(q_st[:, S:2 * S].rearrange("p (c t) -> p c t", c=NT),
                                q_st[:, 0:S].rearrange("p (c t) -> p c t", c=NT),
                                ml_mask[:, :].unsqueeze(1).to_broadcast([P, NT, P]), ALU.add).then_inc(ml["decay"], 1)
                for st in range(NT):
                    dve.wait_ge(ml["scores"], NT * h + st + 1)
                    dve.wait_ge(ml["decay"], (NT + 1) * h + st + 2)
                    if h:
                        dve.wait_ge(ml["sums"], h)
                    w = S - st * P
                    e0 = 24 * S + ML_AT[st]
                    V.scalar_tensor_tensor(out=probs_t[:, ML_AT[st]:ML_AT[st] + w], in0=psum[:, 2 + st, 0:w],
                                           scalar=float(P) ** -0.5, in1=big[:, e0:e0 + w], op0=ALU.mult,
                                           op1=ALU.mult).then_inc(ml["weighted"], 1)
                dve.wait_ge(ml["sums"], h + 1)
                dve.wait_ge(ml["bc_used"], 2 * h + 2)
                V.scalar_tensor_tensor(out=tmp[:, S:2 * S], in0=bank(6), scalar=-1.0, in1=tmp[:, 0:S], op0=ALU.mult,
                                       op1=ALU.max).then_inc(ml["recip"], 1)
                dve.wait_ge(ml["recip"], 3 * h + 1)
                V.tensor_tensor(tmp[:, S:2 * S], bank(6), tmp[:, S:2 * S], ALU.max).then_inc(ml["recip"], 1)
                dve.wait_ge(ml["recip"], 3 * h + 2)
                V.reciprocal(sqt[:, :], tmp[:, S:2 * S]).then_inc(ml["recip"], 1)
                dve.wait_ge(ml["recip"], 3 * h + 3)
                for dv in range(2):
                    V.tensor_tensor(o_acc[:, dv * S:(dv + 1) * S], bank(dv), sqt[:, :], ALU.mult).then_inc(ml["h"], 1)
                dve.wait_ge(ml["std"], h + 1)
                step(V.reciprocal(rstd[:, :], rstd[:, :]))
                settle()
                for dv in range(2):
                    c = 2 * h + dv
                    w = COL["mlstm"] + c
                    step(V.scalar_tensor_tensor(out=o_acc[:, dv * S:(dv + 1) * S], in0=o_acc[:, dv * S:(dv + 1) * S],
                                                scalar=params[:, w:w + 1], in1=rstd[:, :], op0=ALU.mult, op1=ALU.mult))
                    settle()
                    y = o_acc[:, dv * S:(dv + 1) * S]
                    step(V.tensor_tensor(y, chunk(16 + c), y, ALU.mult))
                    settle()
                    step(V.tensor_copy(chunk_r(16 + c), y))
                    settle()
                    V.tensor_tensor(chunk_r(h + 4 * dv), y, plain(chunk_r(16 + c)), ALU.subtract).then_inc(ml["y"], 1)
                dve.wait_ge(ml["y"], 2 * h + 2)
            with dve.Fori(0, 4) as i:
                for j in range(2):
                    dve.wait_ge(tile_done, TILE0["merge_a"] + 2 * j + 2 + 4 * i)
                    dve.wait_ge(evac[0], TILE0["merge_a"] // 2 + j + 1 + 2 * i)
                    V.tensor_tensor(cols(big, 2 * S * i + (8 + j) * S), bank(1), act_o[:, j * S:(j + 1) * S], ALU.mult) \
                        .then_inc(evac[1], 1)
            attention("sw", sw_units(), 2 * NT * 4, lambda i, g: cols(big_r, 4 * g * S + S * i),
                      lambda i, g: cols(big_r, (16 + 4 * g) * S + S * i), sinks=True)
            with dve.Fori(0, 4) as i:
                d.enter(i, 4)
                sp_.enter(i, 2)
                for j in range(2):
                    y = tmp[:, j * S:(j + 1) * S]
                    n0 = 2 * S * i + j * S
                    dve.wait_ge(tile_done, TILE0["merge_b"] + 2 * j + 2 + 4 * i)
                    dve.wait_ge(evac[0], TILE0["merge_b"] // 2 + j + 1 + 2 * i)
                    dve.wait_ge(split_done, sp_.at)
                    V.tensor_tensor(y, bank(1), act_o[:, j * S:(j + 1) * S], ALU.mult).then_inc(evac[1], 1)
                    dve.wait_ge(evac[1], TILE0["merge_b"] // 2 + j + 1 + 2 * i)
                    step(V.tensor_tensor(y, cols(big, n0 + 8 * S), y, ALU.add))
                    settle()
                    split(y, cols(big_r, n0 + 8 * S), cols(big_r, n0 + 24 * S))
            d.leave(4)
            sp_.leave(4)
            dve.wait_ge(ple_in, 16)
            V.tensor_copy(ple_hi, ple_raw).then_inc(small_split, 1)
            dve.wait_ge(small_split, 5)
            V.tensor_tensor(ple_lo, ple_raw, plain(ple_hi), ALU.subtract).then_inc(small_split, 1)
            residual("mix_out", 2, 4)
            norm(6, "mlp2", xc, h_hi, h_lo)

            def mlp_hidden(n0):
                with dve.Fori(0, 4) as i:
                    d.enter(i, 4)
                    sp_.enter(i, 4)
                    for k in range(4):
                        dve.wait_ge(squared, n0 + k + 1 + 4 * i)
                        n = 4 * S * i + k * S
                        split(tmp[:, (k % 2) * S:(k % 2 + 1) * S], cols(big_r, n), cols(big_r, n + 16 * S))
                d.leave(4)
                sp_.leave(4)

            mlp_hidden(0)
            residual("mlp_down_a", 4, 2, False)
            mlp_hidden(F2C // 2)
            residual("mlp_down_b", 4, 2)
            norm(7, "ple2", xc, h_hi, h_lo)
            clear_acc()
            with dve.Fori(0, 4) as i:
                d.enter(i, 4)
                sq.enter(i, 2)
                for j in range(2):
                    y = tmp[:, j * S:(j + 1) * S]
                    x = cols(xt, 2 * S * i + j * S)
                    dve.wait_ge(tile_done, TILE0["ple"] + 2 * j + 2 + 4 * i)
                    dve.wait_ge(evac[0], TILE0["ple"] // 2 + j + 1 + 2 * i)
                    V.tensor_tensor(y, bank(1), act_o[:, j * S:(j + 1) * S], ALU.mult).then_inc(evac[1], 1)
                    dve.wait_ge(evac[1], TILE0["ple"] // 2 + j + 1 + 2 * i)
                    step(V.tensor_tensor(x, x, y, ALU.add))
                    settle()
                    square(x)
            d.leave(4)
            sq.leave(4)
            scale_of(8)
            for c in range(KD):
                g0 = COL["final2"] + c
                V.scalar_tensor_tensor(out=chunk(c), in0=xc(c), scalar=params[:, g0:g0 + 1], in1=rstd[:, :],
                                       op0=ALU.mult, op1=ALU.mult).then_inc(final_out, 1)

        @block.gpsimd
        def _(pool):
            g = nc.gpsimd
            for buf, value in ((ident, 0.0), (ones, 1.0), (causal, 0.0), (band, 0.0), (cmp_mask, 0.0), (cmp_any, 1.0),
                               (ml_mask, 0.0), (eps, EPS)):
                last = g.memset(buf[:, :], value)
            last.then_inc(pool_step, 1)
            g.memset(start[:, 0:1], 0.0).then_inc(tile_done, 2)
            g.memset(start[:, 1:2], 0.0).then_inc(evac[0], 1)
            g.memset(start[:, 2:3], 0.0).then_inc(evac[1], 1)
            pool.wait_ge(pool_step, 1)

            def keep(buf, pattern, base, per_row, fill, compare=ALU.is_ge):
                return g.affine_select(out=buf, in_=buf, pattern=pattern, compare_op=compare, fill=fill, base=base,
                                       channel_multiplier=per_row)

            keep(ident[:, :], [[-1, P]], 0, 1, 1.0, ALU.not_equal).then_inc(pool_step, 1)
            keep(causal[:, :], [[-1, P]], 0, 1, NEG)
            keep(band[:, 0:P], [[1, P]], -1, -1, NEG)
            keep(band[:, P:2 * P], [[-1, P]], 0, 1, NEG)
            keep(cmp_mask[:, :], [[P, NT], [-16, NCMP]], -31, 1, NEG)
            keep(cmp_any[:, :], [[P, NT]], -31, 1, 0.0)
            keep(ml_mask[:, :], [[1, P]], 0, -1, -NEG)
            pool.wait_ge(pool_step, 2)
            g.tensor_copy(ident_bf[:, :], ident[:, :]).then_inc(consts, 1)

            def low(first, count, hi_=w_hi.bitcast(F32)):
                with loop(pool, count) as i:
                    for j in range(2):
                        p = slice(j * PANEL, (j + 1) * PANEL)
                        pool.wait_ge(hi_done[j], first + 1 + i)
                        g.tensor_tensor(w_lo[:, p], ring[:, p], hi_[:, p], ALU.subtract).then_inc(lo_done[j], 1)

            low(0, PAIR0["nsa_k"] + 1)
            pool.wait_ge(par_in, 16)
            for kind in range(2):
                for b in range(2):
                    pool.wait_ge(evac[b], TILE0["cmp_kv"] // 2 + kind + 1)
                src = big[:, (16 + 4 * kind) * S:(20 + 4 * kind) * S].rearrange("p (g t) -> p g t", g=G)
                for j in range(16):
                    d0 = (24 + 4 * kind) * S + j * CMPW
                    c = COL["pe_k" if kind == 0 else "pe_v"] + j
                    g.tensor_scalar(big[:, d0:d0 + CMPW].rearrange("p (g n) -> p g n", g=G),
                                    src[:, :, 2 * j:2 * j + 16 * (NCMP - 1) + 1:16], params[:, c:c + 1], None,
                                    ALU.add).then_inc(blocks, 1)

            def stage(name, done):
                s = att[name]
                g.memset(q_st[:, :], 0.0).then_inc(zeroed, 1)
                pool.wait_ge(zeroed, 1 if name == "nsa" else 2)

                def copy(half_, src):
                    for hd in range(2):
                        rows = slice(64 * hd, 64 * hd + 64)
                        q0 = (2 * half_ + hd) * S
                        last = g.tensor_copy(q_st[rows, q0:q0 + S], src[rows])
                    last.then_inc(s["staged"], 1)

                for b in range(2):
                    pool.wait_ge(evac[b], TILE0[done] // 2)
                for half_ in range(2):
                    copy(half_, chunk(4 * half_))
                with pool.Fori(1, PAIRS // 2) as i:
                    for half_ in range(2):
                        pool.wait_ge(s["turned"], 2 * i + half_ - 1)
                        pool.wait_ge(evac[0], TILE0[done] // 2)
                        copy(half_, cols(big, 4 * half_ * S + S * i))

            low(PAIR0["cmp_w1"], 2, w_hi32)
            low(PAIR0["nsa_q"], PAIR0["nsa_out"] + 1 - PAIR0["nsa_q"])
            stage("nsa", "nsa_out")
            low(PAIR0["nsa_out"] + 1, PAIR0["merge_b"] - PAIR0["nsa_out"])
            stage("sw", "merge_b")
            low(PAIR0["merge_b"] + 1, NPAIRS - PAIR0["merge_b"] - 1)


def lay_out(x):
    def tiles(w):
        k, n = w.shape
        return w.reshape(k // P, P, n // P, P).transpose(0, 2, 1, 3)

    def by_output(w):
        t = tiles(w)
        k, n = t.shape[:2]
        return t.reshape(k, n // 2, 2, P, P).transpose(1, 3, 2, 0, 4).reshape(n // 2, P, 2 * k * P)

    def by_token(w):
        k, n = w.shape
        return w.reshape(2, 4, P, n // S, S).transpose(3, 0, 2, 1, 4).reshape(-1, P, PANEL)

    def in_pairs(v, w):
        tv, tw = tiles(v), tiles(w)
        n = tv.shape[1]
        p = [np.concatenate([t.transpose(1, 2, 0, 3).reshape(n, P, -1) for t in (tv, tw)], axis=2)]
        return pad(p[0])

    def down(w, k0, k1):
        t = tiles(w)[k0:k1]
        return pad(t.transpose(1, 2, 0, 3).reshape(t.shape[1], P, (k1 - k0) * P))

    def pad(p):
        return np.concatenate([p, np.zeros((*p.shape[:2], PANEL - p.shape[2]), p.dtype)], axis=2)

    def heads(w):
        return w.reshape(-1, 2, 2, 4, HD).transpose(0, 1, 3, 2, 4).reshape(w.shape)

    def feature_rows(w):
        return heads(w.T).T

    def column(v):
        return v.reshape(-1, P).T

    ws = x["nsa_w_in"][0]
    q, kc, vc, ks, vs, kw, vw, gl = np.split(ws, [D + 256 * i for i in range(7)], axis=1)
    w1 = [x[n][0].reshape(2, 8, P, 256).transpose(0, 2, 1, 3).reshape(2, P, PANEL) for n in ("nsa_ck_w1", "nsa_cv_w1")]
    w = x["w_in_2"][0]
    qk, v_ml, o_ml, if_, q_sw, k_sw, v_sw, g_a, g_b = np.split(w, np.cumsum([D, D, D, 8, D, 256, 256, D]), axis=1)
    up = x["ffn_w_up"][0]
    wkv = x["ca_wkv"][0]
    parts = {
        "mem_k": by_output(wkv[:, :D]), "mem_v": by_token(wkv[:, D:]),
        "nsa_v": by_token(np.concatenate([vs, vw], axis=1)), "cmp_kv": by_output(np.concatenate([kc, vc], axis=1)),
        "nsa_k": by_output(np.concatenate([ks, kw], axis=1)), "cmp_w1": np.concatenate(w1),
        "nsa_q": by_output(heads(q)), "nsa_out": by_output(feature_rows(x["nsa_w_out"][0])),
        "ca_q": by_output(x["ca_wq"][0]), "ca_out": by_output(x["ca_wo"][0]),
        "ffn_up_a": in_pairs(up[:, :FF], up[:, FF:])[:HALF["ffn_a"]], "ffn_down_a": down(x["ffn_w_down"][0], 0, HALF["ffn_a"]),
        "ffn_up_b": in_pairs(up[:, :FF], up[:, FF:])[HALF["ffn_a"]:], "ffn_down_b": down(x["ffn_w_down"][0], HALF["ffn_a"], FC),
        "ml_qk": by_output(qk), "ml_v": by_token(v_ml), "ml_o": by_output(o_ml),
        "merge_a": in_pairs(g_a, x["w_branch_a_2"][0]), "sw_q": by_output(heads(q_sw)),
        "sw_kv": np.concatenate([by_output(k_sw), v_sw.reshape(KD, P, 256).transpose(1, 0, 2).reshape(1, P, PANEL)]),
        "merge_b": in_pairs(g_b, feature_rows(x["w_branch_b_2"][0])), "mix_out": by_output(x["w_out_2"][0]),
        "mlp_up_a": by_output(x["w_up_2"][0])[:F2C // 4], "mlp_down_a": down(x["w_down_2"][0], 0, F2C // 2),
        "mlp_up_b": by_output(x["w_up_2"][0])[F2C // 4:], "mlp_down_b": down(x["w_down_2"][0], F2C // 2, F2C),
        "ple": in_pairs(x["w_ple_gate_2"][0], x["w_ple_proj_2"][0]),
    }
    for name, pairs, _ in PHASES:
        assert not pairs or len(parts[name]) == 2 * pairs, name
    gl = gl.reshape(D, 2, 2, 4, 3).transpose(0, 1, 3, 2, 4).reshape(D, 48)
    sinks = x["sinks_2"][0].reshape(2, 2, 4).transpose(0, 2, 1).reshape(1, 16)
    norms = [x["mem_norm_w"], x["norm_mix_w"][0], x["norm_cross_w"][0], x["norm_ffn_w"][0], x["final_norm_w"],
             x["norm_mix_g_2"][0], x["norm_mlp_g_2"][0], x["norm_ple_g_2"][0], x["final_norm_g_2"],
             x["mlstm_norm_g_2"][0]]
    b_if = np.zeros((P, 2), np.float32)
    b_if[0:MLH] = x["b_if_2"][0].reshape(2, MLH).T
    params = np.concatenate(
        [column(v) for v in norms] + [column(v) for v in x["ffn_conv_w"][0]] + [column(v) for v in x["conv_qk_2"][0]]
        + [column(x["nsa_pe_k"][0].reshape(-1)), column(x["nsa_pe_v"][0].reshape(-1)), np.repeat(sinks, P, axis=0), b_if],
        axis=1)

    def chunks(v):
        return v.T.reshape(-1, P, v.shape[0]).transpose(1, 0, 2).reshape(P, -1)

    def rows(v):
        return v.reshape(-1, P, v.shape[1]).transpose(1, 0, 2).reshape(P, -1)

    ck2 = x["nsa_ck_w2"][0]
    return {
        "panels": np.concatenate([parts[n] for n, pairs, _ in PHASES if pairs]), "params": params,
        "x": chunks(x["x"][0]), "mem": chunks(x["mem"][0]), "ple": chunks(x["p_2"][0, 0]),
        "w_gate": rows(gl), "w_if": rows(if_), "w2_k": rows(np.concatenate([ck2, ck2], axis=1)),
        "w2_v": rows(x["nsa_cv_w2"][0]),
    }


def kernel(**inputs):
    import concourse.bacc as _bacc
    from concourse.bass_utils import run_bass_kernel_spmd as _run

    nc = _bacc.Bacc("TRN2", target_bir_lowering=False, num_devices=1)
    arrays, args = {}, {}
    for name, v in lay_out({k: np.asarray(v) for k, v in inputs.items()}).items():
        v = np.ascontiguousarray(v)
        arrays[f"in_{name}"] = v
        args[name] = nc.dram_tensor(f"in_{name}", v.shape, mybir.dt.from_np(v.dtype), kind="ExternalInput").ap()
    out = nc.dram_tensor("out", (P, KD * S), F32, kind="ExternalOutput").ap()
    program(nc, args, out)
    r = _run(nc, [arrays], core_ids=[0])
    y = r.results[0]["out"]
    return np.ascontiguousarray(y.reshape(P, KD, S).transpose(2, 1, 0).reshape(1, S, D))
```

```python
from contextlib import ExitStack

import concourse.bass as bass
from concourse import mybir
import numpy as np

F32 = mybir.dt.float32
F32R = mybir.dt.float32r
BF16 = mybir.dt.bfloat16
ALU = mybir.AluOpType
ACT = mybir.ActivationFunctionType
AX_X = mybir.AxisListType.X

P = 128
S = 512
D = 1024
KD = D // P
NT = S // P
MEM = 256
FF = 2816
FC = FF // P
F2 = 4096
F2C = F2 // P
PLE = 256
PANEL = 16 * P
EPS = 1e-6
TOKEN_BANK = (0, 1, 4, 5)
NEG = -1e30

HD = 64
G = 4
PAIRS = 8
NCMP = 31
CMPW = G * NCMP
MLH = 4
NSA_GROUPS_STEP = 4
SWK = 2 * P
SW_UNITS = 4 * NT

NORMS = ["mem", "mix", "cross", "ffn", "final", "mix2", "mlp2", "ple2", "final2", "mlstm"]
COL = {name: 8 * i for i, name in enumerate(NORMS)}
COL["ffn_conv"] = 80
COL["ml_conv"] = COL["ffn_conv"] + 3 * FC
COL["pe_k"] = COL["ml_conv"] + 4 * 8
COL["pe_v"] = COL["pe_k"] + 16
COL["sink"] = COL["pe_v"] + 16
COL["b_i"] = COL["sink"] + 16
COL["b_f"] = COL["b_i"] + 1
NPAR = COL["b_f"] + 1

PHASES = [
    ("cmp_kv", 1, 4), ("nsa_v", 1, 4), ("nsa_g", 0, 2), ("nsa_k", 1, 4), ("nsa_q", 2, 4),
    ("cmp_w1", 2, 2), ("cmp_w2", 0, 2), ("mem_k", 2, 4), ("nsa_out", 2, 4),
    ("mem_v", 2, 2), ("ca_q", 2, 4), ("ca_out", 2, 4),
    ("ffn_up_a", 6, 4), ("ffn_down_a", 4, 2), ("ffn_up_b", 5, 4), ("ffn_down_b", 4, 2),
    ("ml_qk", 2, 4), ("ml_if", 0, 2), ("ml_v", 2, 4), ("ml_o", 2, 4), ("merge_a", 4, 4),
    ("sw_q", 2, 4), ("sw_kv", 1, 6), ("merge_b", 4, 4), ("mix_out", 2, 4),
    ("mlp_up_a", 4, 4), ("mlp_down_a", 4, 2), ("mlp_up_b", 4, 4), ("mlp_down_b", 4, 2),
    ("ple_v", 1, 8), ("ple_g", 2, 4),
]
PER = {name: per for name, _, per in PHASES}
HALF = {"ffn_a": 12, "ffn_b": FC - 12, "mlp_a": F2C // 2, "mlp_b": F2C // 2}
SPLIT0 = {"ffn_a": 0, "ffn_b": 12, "merged": FC, "mlp_a": FC + 8, "mlp_b": FC + 8 + F2C // 2}
ML_AT = [0, 512, 896, 1152]
PAIR0, TILE0 = {}, {}
_r, _t = 0, 2
for _name, _pairs, _tiles in PHASES:
    PAIR0[_name], TILE0[_name] = _r, _t
    _r += _pairs
    _t += max(_pairs, 1) * _tiles
NPAIRS, NTILES = _r, _t


def loop(engine, n, first=0):
    from contextlib import nullcontext
    return engine.Fori(first, n) if n - first > 1 else nullcontext(first)


def cols(buf, first, n=S):
    return buf[:, bass.ds(first, n)]


class Count:

    def __init__(self, sem):
        self.sem, self.n, self.i, self.per = sem, 0, 0, 0

    def enter(self, i, per):
        self.i, self.per, self.start = i, per, self.n

    def leave(self, steps):
        assert self.n - self.start == self.per, (self.n - self.start, self.per)
        self.n = self.start + steps * self.per
        self.i, self.per = 0, 0

    @property
    def at(self):
        return self.n + self.per * self.i if self.per else self.n


def nsa_units():
    order = [(0, 0), (3, 1), (0, 1), (2, 1), (1, 0), (3, 2), (0, 2), (2, 2), (2, 0), (1, 1), (3, 0), (1, 2)]
    seen, units = set(), []
    for n, (qt, br) in enumerate(order):
        units.append(dict(qt=qt, br=br, k0=0, nk=(qt + 1) * P if br else NCMP, first=qt not in seen,
                          last=n == len(order) - 1))
        seen.add(qt)
    return units


def nsa_chunk(i, g):
    return i * (NSA_GROUPS_STEP // 2) + (4 * (g % 2) + g // 2)


def sw_keys(qt):
    return (0, P) if qt == 0 else ((qt - 1) * P, 2 * P)


def ca_units():
    return [dict(qt=qt, hp=hp, nk=MEM, first=True, last=True) for hp in range(2) for qt in range(NT)]


def program(nc, a, out):
    with ExitStack() as ctx:
        def sem(name):
            return ctx.enter_context(nc.semaphore(name))

        at = [-(-nc.sbuf_base // 32) * 8]

        def sb(name, shape, dt=F32, twin=False):
            rows, n = shape
            size = 2 if dt == BF16 else 4
            words = -(-n * size // 32) * 8
            base = at[0] * 4
            at[0] += words
            t = nc.alloc_sbuf_tensor_at(name, [rows, n], dt, offset=base)
            if twin:
                return t, nc.alloc_sbuf_tensor_at(name + "_r", [rows, n], F32R, offset=base)
            return t

        def view(name, shape, on, first=0):
            return on[0:shape[0], first:first + shape[1]]

        xt = sb("xt", [P, KD * S])
        h_hi = sb("h_hi", [P, KD * S], F32R)
        h_lo = sb("h_lo", [P, KD * S], F32R)
        ring = sb("ring", [P, 2 * PANEL])
        w_hi32, w_hi = sb("w_hi", [P, 2 * PANEL], twin=True)
        w_lo = sb("w_lo", [P, 2 * PANEL], F32R)
        big, big_r = sb("big", [P, 32 * S], twin=True)
        params = sb("params", [P, NPAR])
        wi_hi = sb("wi_hi", [P, KD * 8], F32R)
        wi_lo = sb("wi_lo", [P, KD * 8], F32R)
        ident = sb("ident", [P, P])
        ones = sb("ones", [P, P])
        ident_bf = sb("ident_bf", [P, P], BF16)
        causal = sb("causal", [P, P], BF16)
        band = sb("band", [P, 2 * P], BF16)
        cmp_mask = sb("cmp_mask", [P, NT * NCMP], BF16)
        cmp_any = sb("cmp_any", [P, NT])
        ml_mask = sb("ml_mask", [P, P])
        eps = sb("eps", [P, 1])
        start = sb("start", [P, 7])
        acc = sb("acc", [P, S])
        sqt = sb("sqt", [P, S])
        rstd = sb("rstd", [P, S])
        gains = sb("gains", [P, 2 * KD])
        tmp = sb("tmp", [P, 2 * S])
        o_acc = sb("o_acc", [P, 2 * S])
        act_o = o_acc
        gates = sb("gates", [P, NT * 48])
        hid = sb("hid", [P, 2 * 2 * CMPW])
        kcmp = sb("kcmp", [P, CMPW])
        vcmp = sb("vcmp", [NCMP, G * HD])
        probs, probs_r = sb("probs", [P, 2 * 2 * S], twin=True)
        probs_t, probs_tr = sb("probs_t", [P, 2 * 2 * S], twin=True)
        q_st = sb("q_st", [P, 4 * S])
        negmax = sb("negmax", [P, 8])
        total = sb("total", [P, 8])
        coef = sb("coef", [P, 8])
        sink_arg = sb("sink_arg", [P, 8])
        sink_e = sb("sink_e", [P, 8])
        neg_sink = sb("neg_sink", [P, 16])
        u_col = sb("u_col", [P, NT * MLH])
        assert at[0] * 4 <= nc.sbuf_usable_end, (at[0] * 4, nc.sbuf_usable_end)

        w2_k = view("w2_k", [P, 2 * P], probs)
        w2_v = view("w2_v", [P, 2 * HD], probs, 2 * P)
        w_gate = view("w_gate", [P, KD * 48], probs_t)
        wg_hi = view("wg_hi", [P, KD * 48], probs_tr, S)
        wg_lo = view("wg_lo", [P, KD * 48], probs_tr, 2 * S)
        gate_rows = view("gate_rows", [48, S], o_acc)
        w_if = view("w_if", [P, KD * 8], probs_t, 3 * S)
        ig, fz, fe, fcum = (view(n, [MLH, S], probs, i * S) for i, n in enumerate(("ig", "fz", "fe", "fcum")))
        u_row, m_row, nm_row = (view(n, [MLH, S], q_st, (1 + i) * S) for i, n in enumerate(("u", "m", "nm")))
        acc2, rstd2 = view("acc2", [P, S], o_acc), view("rstd2", [P, S], o_acc, S)
        sw_o = (o_acc, tmp)
        sw_q = (view("sw_q0", [P, 4 * S], q_st), view("sw_q1", [P, 4 * S], big, 28 * S))
        ml_h = ((view("ml_h00", [P, S], o_acc), view("ml_h01", [P, S], o_acc, S)),
                (view("ml_h10", [P, S], probs_t, ML_AT[-1] + P), view("ml_h11", [P, S], probs, ML_AT[-1] + P)))
        ml_y = (view("ml_y0", [P, S], big, 27 * S), view("ml_y1", [P, S], tmp))
        ml_weights = (probs_t, probs)
        mem_raw = view("mem_raw", [P, KD * MEM], big, 16 * S)
        mem_hi = view("mem_hi", [P, KD * MEM], big_r, 20 * S)
        mem_lo = view("mem_lo", [P, KD * MEM], big_r, 16 * S)
        memk = view("memk", [P, KD * MEM], big, 28 * S)
        memv = view("memv", [P, 2 * D], big, 24 * S)
        ple_raw = view("ple_raw", [P, 2 * S], q_st)
        ple_hi = view("ple_hi", [P, 2 * S], probs_r)
        ple_lo = view("ple_lo", [P, 2 * S], probs_r, 2 * S)

        psum = ctx.enter_context(nc.psum_tensor("psum", [P, 8, S], F32))

        def bank(b, n=S):
            return psum[:, b, 0:n]

        def sw_score(par, x, nk):
            return psum[:, 2 + 2 * par + x // 2, (x % 2) * SWK:(x % 2) * SWK + nk]

        def sw_pairs(buf, nk):
            return buf.rearrange("p (x k) -> p x k", k=SWK)[:, :, 0:nk]

        def chunk(i):
            return big[:, i * S:(i + 1) * S]

        def chunk_r(i):
            return big_r[:, i * S:(i + 1) * S]

        def plain(x):
            return x.bitcast(F32)

        w_full = [sem("w_full0"), sem("w_full1")]
        hi_done = [sem("hi_done0"), sem("hi_done1")]
        lo_done = [sem("lo_done0"), sem("lo_done1")]
        slot0_free = sem("slot0_free")
        tile_done = sem("tile_done")
        evac = [sem("evac0"), sem("evac1")]
        x_in = [sem(f"x_in{part}") for part in range(4)]
        mem_in, par_in, small_in, ple_in = (sem(n) for n in ("mem_in", "par_in", "small_in", "ple_in"))
        x_squared = sem("x_squared")
        gate_used = sem("gate_used")
        product_sum = sem("product_sum")
        consts, zeroed = sem("consts"), sem("zeroed")
        dve_step, pool_step = sem("dve_step"), sem("pool_step")
        squares = sem("squares")
        stat = sem("stat")
        std_done = sem("std_done")
        raw_x, hi_x = sem("raw_x"), sem("hi_x")
        normed = sem("normed")
        split_done = sem("split_done")
        squared = sem("squared")
        small_split = sem("small_split")
        blocks = sem("blocks")
        gated = sem("gated")
        ml_step = {n: sem("ml_" + n) for n in (
            "u_col", "z", "e", "l", "rows", "bc", "bc_used", "scores", "decay", "weighted", "sums", "recip", "h",
            "sq", "ssq", "std", "scaled", "gate", "y_hi", "y")}
        att = {}
        for name in ("nsa", "ca", "sw"):
            att[name] = {n: sem(f"{name}_{n}") for n in (
                "staged", "scores", "negmax", "probs", "transposed", "copied_a", "copied_d", "summed",
                "combined", "turned", "stored", "split")}
        final_out = sem("final_out")
        stored = sem("stored")

        def half(name, i, k):
            per = PER[name]
            return TILE0[name] // 2 + (per // 2) * i + k // 2

        block = ctx.enter_context(nc.Block())

        NU = len(nsa_units())
        def att_dims(name):
            return {"nsa": (PAIRS // NSA_GROUPS_STEP, NSA_GROUPS_STEP, NU), "ca": (1, 2 * NT, 1)}[name]

        @block.sync
        def _(sp):
            def load(r, j):
                sp.dma_start(ring[:, j * PANEL:(j + 1) * PANEL], a["panels"][2 * r + j]).then_inc(w_full[j], 16)

            for part in range(4):
                cs = slice(2 * part * S, 2 * (part + 1) * S)
                sp.dma_start(xt[:, cs], a["x"][:, cs]).then_inc(x_in[part], 16)
            for j in range(2):
                load(0, j)
            with sp.Fori(1, NPAIRS) as r:
                for j in range(2):
                    sp.wait_ge(lo_done[j], r)
                    load(r, j)
            for c in range(KD):
                sp.wait_ge(final_out, c + 1)
                sp.dma_start(out[:, c * S:(c + 1) * S], chunk(c)).then_inc(stored, 16)
            sp.wait_ge(stored, 16 * KD)

        @block.tensor
        def _(pe):
            def mm(o, l, r, start, stop, **kw):
                return nc.tensor.matmul(o, l, r, start=start, stop=stop, **kw)

            def weights_here(name, i, j):
                pe.wait_ge(lo_done[j], PAIR0[name] + 1 + i)

            def bank_free(name, i, k):
                pe.wait_ge(evac[k % 2], half(name, i, k))

            def mm3(o, l, r, first, last):
                mm(o, l[0], r[0], first, False)
                mm(o, l[0], r[1], False, False)
                return mm(o, l[1], r[0], False, last)

            def w(at_, n=P):
                return w_hi[:, at_:at_ + n], w_lo[:, at_:at_ + n]

            def product(name, pairs, rhs, n=S, fresh=None, bank1=None):
                def pair(i, fresh=None, peeled=False):
                    for j in range(2):
                        weights_here(name, i, j)
                        for t in range(2):
                            bank_free(name, i, 2 * j + t)
                            if peeled and bank1 is not None and (j, t) == (0, 1):
                                pe.wait_ge(*bank1)
                            if fresh is not None and j == 0:
                                continue
                            for k in range(KD):
                                last = mm3(bank(t, n), w(j * PANEL + (t * KD + k) * P), rhs(k), k == 0, k == KD - 1)
                            last.then_inc(tile_done, 1)
                        for k in range(KD if fresh is not None and j == 0 else 0):
                            pe.wait_ge(normed, KD * fresh + k + 1)
                            for t in range(2):
                                last = mm3(bank(t, n), w(j * PANEL + (t * KD + k) * P), rhs(k), k == 0, k == KD - 1)
                                if k == KD - 1:
                                    last.then_inc(tile_done, 1)

                peeled = fresh is not None or bank1 is not None
                if peeled:
                    pair(0, fresh, True)
                if pairs > int(peeled):
                    with loop(pe, pairs, int(peeled)) as i:
                        pair(i)

            def product_tokens(name, pairs, lhs, tiles_):
                with loop(pe, pairs) as i:
                    for b in range(2):
                        pe.wait_ge(evac[b], half(name, i, 0))
                    for j in range(2):
                        weights_here(name, i, j)
                        for k in range(4):
                            for t in range(tiles_):
                                last = mm3(bank(TOKEN_BANK[t]), lhs(4 * j + k, t), w(j * PANEL + k * S, S),
                                           j == 0 and k == 0, j == 1 and k == 3)
                                if j == 1 and k == 3:
                                    last.then_inc(tile_done, 1)
                        if j == 0:
                            last.then_inc(slot0_free, 1)

            def product_down(name, n_k, done):
                with pe.Fori(0, 4) as i:
                    for j in range(2):
                        weights_here(name, i, j)
                        bank_free(name, i, j)
                        for k in range(n_k):
                            if j == 0:
                                pe.wait_ge(split_done, done + k + 1)
                            last = mm3(bank(j), w(j * PANEL + k * P), (chunk_r(k), chunk_r(16 + k)), k == 0,
                                       k == n_k - 1)
                        last.then_inc(tile_done, 1)

            def partition_sum(m, b, n=S):
                pe.wait_ge(squares, KD * (m + 1))
                mm(bank(b, n), ones[:, :], acc[:, 0:n], True, True).then_inc(stat, 1)

            def attention(name, qk, mask, pv, units):
                s = att[name]
                steps, groups, per = att_dims(name)
                flat = [u for _ in range(groups) for u in units] if name != "ca" else units
                n_units = len(flat)
                with loop(pe, steps) as i:
                    u0 = n_units * i

                    def scores(u):
                        g = u // per
                        if u % per == 0 and name != "ca":
                            pe.wait_ge(s["staged"], groups * i + g + 1)
                        if u >= 2:
                            pe.wait_ge(s["probs"], u0 + (u - 1))
                        for hd in range(2):
                            ops = qk(flat[u], g % 2, hd)
                            b = 2 + 2 * (u % 2) + hd
                            m = mask(flat[u])
                            for n, (l, r) in enumerate(ops):
                                last = mm(bank(b, flat[u]["nk"]), l, r, n == 0, m is None and n == len(ops) - 1)
                            if m is not None:
                                c0 = flat[u]["nk"] - m.shape[1]
                                last = mm(psum[:, b, c0:flat[u]["nk"]], ident_bf[:, :], m, False, True)
                        last.then_inc(s["scores"], 1)

                    def transposes(u):
                        pe.wait_ge(s["probs"], u0 + (u + 1))
                        if u >= 1:
                            pe.wait_ge(s["copied_a"], u0 + u)
                            pe.wait_ge(s["copied_d"], u0 + u)
                        nk = flat[u]["nk"]
                        for hd in range(2):
                            for k in range(0, nk, P):
                                w = min(P, nk - k)
                                p0 = (2 * (u % 2) + hd) * S + k
                                last = nc.tensor.transpose(psum[0:w, 6 + hd, k:k + P], probs[:, p0:p0 + w], ident[:, :])
                        last.then_inc(s["transposed"], 1)

                    def values(u):
                        g = u // per
                        pe.wait_ge(s["copied_a"], u0 + (u + 1))
                        pe.wait_ge(s["copied_d"], u0 + (u + 1))
                        halves = 1 if name == "ca" else 2
                        if u >= halves:
                            pe.wait_ge(s["combined"], u0 + (u + 1 - halves))
                        for hd in range(2):
                            ops, o0, ow = pv(flat[u], g % 2, hd, u % 2)
                            for n, (l, r) in enumerate(ops):
                                last = mm(psum[:, 0, o0:o0 + ow], l, r, n == 0, n == len(ops) - 1)
                        last.then_inc(s["summed"], 1)

                    def turn(g):
                        pe.wait_ge(s["combined"], u0 + per * (g + 1))
                        if g:
                            pe.wait_ge(s["split"], groups * i + g)
                        for t in range(NT):
                            o0 = (g % 2) * S + t * P
                            last = nc.tensor.transpose(psum[:, 1, t * P:(t + 1) * P], o_acc[:, o0:o0 + P], ident[:, :])
                        last.then_inc(s["turned"], 1)

                    scores(0)
                    for u in range(n_units):
                        if u + 1 < n_units:
                            scores(u + 1)
                        if u >= 1:
                            values(u - 1)
                        if u >= 2 and flat[u - 2]["last"]:
                            turn((u - 2) // per)
                        transposes(u)
                    values(n_units - 1)
                    if n_units > 1 and flat[n_units - 2]["last"]:
                        turn((n_units - 2) // per)
                    turn(groups - 1)

            pe.wait_ge(consts, 1)
            hk = lambda k: (h_hi[:, k * S:(k + 1) * S], h_lo[:, k * S:(k + 1) * S])
            htok = lambda k, t: tuple(x[:, k * S + t * P:k * S + (t + 1) * P] for x in (h_hi, h_lo))
            partition_sum(0, 2)
            product("cmp_kv", 1, hk, fresh=0)
            product_tokens("nsa_v", 1, htok, 4)
            pe.wait_ge(small_split, 4)
            bank_free("nsa_g", 0, 0)
            for k in range(KD):
                last = mm3(psum[0:48, 0, :], (wg_hi[:, k * 48:(k + 1) * 48], wg_lo[:, k * 48:(k + 1) * 48]), hk(k),
                           k == 0, k == KD - 1)
            last.then_inc(tile_done, 1)
            bank_free("nsa_g", 0, 1)
            pe.wait_ge(evac[0], TILE0["nsa_g"] // 2 + 1)
            for t in range(NT):
                last = nc.tensor.transpose(psum[:, 1, t * 48:(t + 1) * 48], gate_rows[:, t * P:(t + 1) * P],
                                           ident[0:48, 0:48])
            last.then_inc(tile_done, 1)
            product("nsa_k", 1, hk)
            product("nsa_q", 2, hk)
            partition_sum(1, 2, MEM)
            with pe.Fori(0, 2) as i:
                pe.wait_ge(blocks, 16 * i + 16)
                for b in range(2):
                    pe.wait_ge(evac[b], half("cmp_w1", i, 0))
                for j in range(2):
                    weights_here("cmp_w1", i, j)
                    for t in range(2):
                        for k in range(8):
                            w0 = j * PANEL + k * 2 * P + t * P
                            last = mm(bank(t, CMPW), w_hi32[:, w0:w0 + P],
                                      cols(big, i * (4 * S) + 24 * S + (8 * j + k) * CMPW, CMPW),
                                      j == 0 and k == 0, j == 1 and k == 7)
                        if j == 1:
                            last.then_inc(tile_done, 1)
                    if j == 0:
                        last.then_inc(slot0_free, 1)
            for b in range(2):
                pe.wait_ge(evac[b], half("cmp_w2", 0, 0))
            pe.wait_ge(small_in, 64)
            for k in range(2):
                last = mm(bank(0, CMPW), w2_k[:, k * P:(k + 1) * P], hid[:, k * CMPW:(k + 1) * CMPW], k == 0, k == 1)
            last.then_inc(tile_done, 1)
            for g in range(G):
                for k in range(2):
                    h0 = (2 + k) * CMPW + g * NCMP
                    last = mm(psum[0:NCMP, 1, g * HD:(g + 1) * HD], hid[:, h0:h0 + NCMP],
                              w2_v[:, k * HD:(k + 1) * HD], k == 0, k == 1)
            last.then_inc(tile_done, 1)

            def nsa_qk(u, par, hd):
                q0 = (2 * par + hd) * S + u["qt"] * P
                q = q_st[:, q0:q0 + P]
                if u["br"] == 0:
                    k0 = (2 * par + hd) * NCMP
                    return [(q, kcmp[:, k0:k0 + NCMP])]
                k0 = (8 + 2 * (u["br"] - 1) + par) * S
                return [(q, big[:, k0:k0 + u["nk"]])]

            def nsa_mask(u):
                return cmp_mask[:, u["qt"] * NCMP:(u["qt"] + 1) * NCMP] if u["br"] == 0 else causal[:, :]

            def nsa_pv(u, par, hd, up):
                p0 = (2 * up + hd) * S
                if u["br"] == 0:
                    v0 = 2 * par * HD
                    return [(probs_t[0:NCMP, p0:p0 + P], vcmp[:, v0:v0 + P])], (2 * up + hd) * P, P
                ops = []
                for kt in range(u["nk"] // P):
                    v0 = (12 + kt) * S + (u["br"] - 1) * 256 + 2 * par * HD
                    ops.append((probs_t[:, p0 + kt * P:p0 + (kt + 1) * P], big[:, v0:v0 + P]))
                return ops, (2 * up + hd) * P, P

            for b in range(2):
                pe.wait_ge(evac[b], half("mem_k", 0, 0))
            attention("nsa", nsa_qk, nsa_mask, nsa_pv, nsa_units())
            pe.wait_ge(normed, KD * 2)
            product("mem_k", 2, lambda k: (mem_hi[:, k * MEM:(k + 1) * MEM], mem_lo[:, k * MEM:(k + 1) * MEM]), MEM,
                    bank1=(att["nsa"]["split"], PAIRS))
            product("nsa_out", 2, hk)
            partition_sum(2, 2)
            product_tokens("mem_v", 2, lambda k, t: tuple(x[:, k * MEM + t * P:k * MEM + (t + 1) * P]
                                                          for x in (mem_hi, mem_lo)), 2)
            product("ca_q", 2, hk, fresh=2)

            def ca_qk(u, par, hd):
                h = 2 * u["hp"] + hd
                return [(big[:, (2 * h + c) * S + u["qt"] * P:(2 * h + c) * S + (u["qt"] + 1) * P],
                         memk[:, (2 * h + c) * MEM:(2 * h + c + 1) * MEM]) for c in range(2)]

            def ca_pv(u, par, hd, up):
                h = 2 * u["hp"] + hd
                p0 = (2 * up + hd) * S
                return [(probs_t[:, p0 + kt * P:p0 + (kt + 1) * P],
                         memv[:, kt * D + h * 256:kt * D + (h + 1) * 256]) for kt in range(2)], hd * 256, 256

            pe.wait_ge(evac[0], half("ca_out", 0, 0))
            pe.wait_ge(evac[1], half("ca_out", 0, 0))
            attention("ca", ca_qk, lambda u: None, ca_pv, ca_units())
            pe.wait_ge(att["ca"]["split"], 2 * NT)
            product("ca_out", 2, hk)
            partition_sum(3, 2)
            product("ffn_up_a", HALF["ffn_a"] // 2, hk, fresh=3)
            product_down("ffn_down_a", HALF["ffn_a"], SPLIT0["ffn_a"])
            product("ffn_up_b", HALF["ffn_b"] // 2, hk)
            product_down("ffn_down_b", HALF["ffn_b"], SPLIT0["ffn_b"])
            pe.wait_ge(squares, KD * 6)
            mm(bank(2), ones[:, :], acc[:, :], True, True).then_inc(stat, 1)
            mm(bank(3), ones[:, :], acc2, True, True).then_inc(stat, 1)
            product("ml_qk", 2, hk, fresh=4)
            for t in range(2):
                bank_free("ml_if", 0, t)
                for k in range(KD):
                    g0 = k * 8 + 4 * t
                    last = mm3(psum[0:MLH, t, :], (wi_hi[:, g0:g0 + 4], wi_lo[:, g0:g0 + 4]), hk(k), k == 0, k == KD - 1)
                last.then_inc(tile_done, 1)
            product_tokens("ml_v", 2, htok, 4)
            product("ml_o", 2, hk)
            ml = ml_step
            pe.wait_ge(ml["rows"], 5)
            for st in range(NT):
                last = mm(psum[:, 2, st * MLH:(st + 1) * MLH], u_row[:, st * P:(st + 1) * P], ident[0:MLH, 0:MLH],
                          True, True)
            last.then_inc(ml["u_col"], 1)
            pe.wait_ge(ml["u_col"], 2)
            for t in range(2):
                pe.wait_ge(evac[t], TILE0["merge_a"] // 2)

            def ahead(h):
                if h:
                    pe.wait_ge(ml["bc_used"], 2 * h)
                if h >= 3:
                    pe.wait_ge(ml["std"], h - 2)
                mm(bank(7), ident[0:MLH, h:h + 1].to_broadcast([MLH, P]), m_row[:, :], True, True).then_inc(ml["bc"], 1)
                if h:
                    pe.wait_ge(ml["weighted"], NT * h)
                for st in range(NT):
                    mm(psum[:, 2 + st, 0:S - st * P], big[:, (4 + h) * S + st * P:(4 + h) * S + (st + 1) * P],
                       big[:, h * S + st * P:(h + 1) * S], True, True).then_inc(ml["scores"], 1)
                pe.wait_ge(ml["bc_used"], 2 * h + 1)
                mm(bank(7), ident[0:MLH, h:h + 1].to_broadcast([MLH, P]), nm_row[:, :], True, True).then_inc(ml["bc"], 1)

            def squares_sum(h):
                pe.wait_ge(ml["sq"], 2 * h + 2)
                pe.wait_ge(ml["bc_used"], 2 * min(h + 3, MLH))
                for dv in range(2):
                    last = mm(bank(7), ones[:, :], chunk(28 + dv), dv == 0, dv == 1)
                last.then_inc(ml["ssq"], 1)

            ahead(0)
            for h in range(MLH):
                if h + 1 < MLH:
                    ahead(h + 1)
                if h:
                    pe.wait_ge(ml["h"], 2 * h)
                for st in range(NT):
                    pe.wait_ge(ml["weighted"], NT * h + st + 1)
                    p0 = ML_AT[st]
                    pt = ml_weights[h % 2][:, p0:p0 + S - st * P]
                    for dv in range(2):
                        v0 = (8 * S) + st * D + h * 256 + dv * P
                        mm(psum[:, dv, st * P:S], big[:, v0:v0 + P], pt, st == 0, st == NT - 1)
                    last = mm(psum[:, 6, st * P:S], ones[:, :], pt, st == 0, st == NT - 1)
                last.then_inc(ml["sums"], 1)
                if h:
                    squares_sum(h - 1)
            squares_sum(MLH - 1)
            pe.wait_ge(ml["h"], 2 * MLH)

            def merge(name, rhs, ready):
                def pair(i, peeled=False):
                    for j in range(2):
                        weights_here(name, i, j)
                        for t in range(2):
                            bank_free(name, i, 2 * j + t)
                            if peeled and (j, t) == (0, 1):
                                pe.wait_ge(*ready)
                            for k in range(KD):
                                last = mm3(bank(t), w(j * PANEL + (t * KD + k) * P), hk(k) if t == 0 else rhs(k),
                                           k == 0, k == KD - 1)
                            last.then_inc(tile_done, 1)

                pair(0, True)
                with pe.Fori(1, 4) as i:
                    pair(i)

            merge("merge_a", lambda k: (chunk_r(16 + k), chunk_r(k // 2 + 4 * (k % 2))), ready=(ml["y"], 2 * MLH))
            product("sw_q", 2, hk)
            for j in range(2):
                weights_here("sw_kv", 0, j)
                for t in range(2 if j == 0 else NT):
                    bank_free("sw_kv", 0, t + 2 * j)
                    for k in range(KD):
                        if j == 0:
                            last = mm3(bank(t), w((t * KD + k) * P), hk(k), k == 0, k == KD - 1)
                        else:
                            last = mm3(bank(t % 2, 256), htok(k, t), w(PANEL + k * 256, 256), k == 0, k == KD - 1)
                    last.then_inc(tile_done, 1)

            for b in range(2):
                pe.wait_ge(evac[b], half("merge_b", 0, 0))
            s = att["sw"]
            def scores(u):
                qt, par, quad = u % NT, u % 2, u // NT
                if qt == 0:
                    pe.wait_ge(s["staged"], 2 * quad + 2)
                if u >= 2:
                    pe.wait_ge(s["probs"], u - 1)
                k0, nk = sw_keys(qt)
                m = causal[:, :] if qt == 0 else band[:, :]
                for x in range(4):
                    o = sw_score(par, x, nk)
                    q0 = x * S + qt * P
                    key0 = (24 + x // 2) * S + k0
                    mm(o, sw_q[quad % 2][:, q0:q0 + P], big[:, key0:key0 + nk], True, False)
                    last = mm(o, ident_bf[:, :], m, False, True)
                last.then_inc(s["scores"], 1)

            def transposes(u):
                par, (_, nk) = u % 2, sw_keys(u % NT)
                pe.wait_ge(s["probs"], u + 1)
                if u >= 1:
                    pe.wait_ge(s["copied_a"], u)
                    pe.wait_ge(s["copied_d"], u)
                for x in range(4):
                    for k in range(0, nk, P):
                        p0 = par * 2 * S + x * SWK + k
                        c0 = (x % 2) * SWK + k
                        last = nc.tensor.transpose(psum[:, 6 + x // 2, c0:c0 + P], probs[:, p0:p0 + P], ident[:, :])
                last.then_inc(s["transposed"], 1)

            def values(u):
                par, (k0, nk) = u % 2, sw_keys(u % NT)
                pe.wait_ge(s["copied_a"], u + 1)
                pe.wait_ge(s["copied_d"], u + 1)
                if u >= 1:
                    pe.wait_ge(s["combined"], u)
                for x in range(4):
                    for k in range(0, nk, P):
                        p0 = par * 2 * S + x * SWK + k
                        v0 = 26 * S + (k0 + k) // P * 256 + x // 2 * 2 * HD
                        last = mm(psum[:, 0, x * P:(x + 1) * P], probs_t[:, p0:p0 + P], big[:, v0:v0 + P], k == 0,
                                  k == nk - P)
                last.then_inc(s["summed"], 1)

            def turn(quad, g):
                pe.wait_ge(s["combined"], NT * (quad + 1))
                if quad or g:
                    pe.wait_ge(s["split"], 2 * quad + g)
                for t in range(NT):
                    o0 = g * S + t * P
                    last = nc.tensor.transpose(psum[:, 1, t * P:(t + 1) * P], sw_o[quad % 2][:, o0:o0 + P], ident[:, :])
                last.then_inc(s["turned"], 1)

            scores(0)
            for u in range(SW_UNITS):
                if u + 1 < SW_UNITS:
                    scores(u + 1)
                if u >= 1:
                    values(u - 1)
                    if u >= NT and u % NT in (1, 2):
                        turn(u // NT - 1, u % NT - 1)
                transposes(u)
            values(SW_UNITS - 1)
            for g in range(2):
                turn(SW_UNITS // NT - 1, g)
            merge("merge_b", lambda k: (chunk_r(k), chunk_r(16 + k)), ready=(att["sw"]["split"], PAIRS))
            pe.wait_ge(split_done, SPLIT0["mlp_a"])
            product("mix_out", 2, lambda k: (chunk_r(8 + k), chunk_r(24 + k)))
            partition_sum(6, 2)
            product("mlp_up_a", F2C // 8, hk, fresh=5)
            product_down("mlp_down_a", HALF["mlp_a"], SPLIT0["mlp_a"])
            product("mlp_up_b", F2C // 8, hk)
            product_down("mlp_down_b", HALF["mlp_b"], SPLIT0["mlp_b"])
            partition_sum(7, 2)
            pe.wait_ge(small_split, 6)
            weights_here("ple_v", 0, 1)
            for t in range(KD):
                bank_free("ple_v", 0, t)
                for k in range(PLE // P):
                    last = mm3(bank(t % 2), w(PANEL + (t * 2 + k) * P),
                               (ple_hi[:, k * S:(k + 1) * S], ple_lo[:, k * S:(k + 1) * S]), k == 0, k == 1)
                last.then_inc(tile_done, 1)
            product("ple_g", 2, hk, fresh=6)
            partition_sum(8, 2)

        @block.scalar
        def _(act):
            act.dma_start(params[:, :], a["params"]).then_inc(par_in, 16)
            for dst, src in ((w_gate, "w_gate"), (w_if, "w_if"), (w2_k, "w2_k"), (w2_v, "w2_v")):
                act.dma_start(dst, a[src]).then_inc(small_in, 16)

            def hi(r, j, whole=False):
                act.wait_ge(w_full[j], 16 * r + 16)
                dst = w_hi32 if whole else w_hi
                nc.scalar.copy(dst[:, j * PANEL:(j + 1) * PANEL], ring[:, j * PANEL:(j + 1) * PANEL]) \
                    .then_inc(hi_done[j], 1)

            def norm(m, b, n=S):
                act.wait_ge(stat, m + 1)
                nc.scalar.activation(rstd[:, 0:n], bank(b, n), ACT.Sqrt, bias=eps[:, 0:1], scale=1.0 / D) \
                    .then_inc(std_done, 1)

            def norm_hi(m, hi_buf, n=S, chunks=range(KD)):
                for c in chunks:
                    act.wait_ge(raw_x, KD * m + c + 1)
                    nc.scalar.copy(hi_buf[:, c * n:(c + 1) * n], tmp[:, (c % 2) * S:(c % 2) * S + n]) \
                        .then_inc(hi_x, 1)

            def phase(name, pairs, slot, last=False, tokens=None):
                def pair(i, next_):
                    for j in range(2):
                        if tokens is not None and j == 0:
                            if next_:
                                act.wait_ge(slot0_free, tokens + i + 1)
                                hi(PAIR0[name] + 1 + i, 0)
                            continue
                        slot(i, j)
                        if next_:
                            hi(PAIR0[name] + 1 + i, j)

                with loop(act, pairs - 1 if last else pairs) as i:
                    pair(i, True)
                if last:
                    pair(pairs - 1, False)

            def wait_tile(name, i, k):
                act.wait_ge(tile_done, TILE0[name] + k + 1 + PER[name] * i)

            def take(name, pairs, dst, n=S, func=ACT.Copy, scale=1.0, tokens=None, banks=(0, 1, 0, 1)):
                def slot(i, j):
                    ks = range(PER[name]) if tokens is not None else range(2 * j, 2 * j + 2)
                    for k in ks:
                        wait_tile(name, i, k)
                        nc.scalar.activation(dst(i, k), bank(banks[k], n), func, scale=scale).then_inc(evac[k % 2], 1)
                phase(name, pairs, slot, tokens=tokens)

            def through(name, pairs):
                def slot(i, j):
                    per = PER[name] // 2
                    wait_tile(name, i, per * j + per - 1)
                phase(name, pairs, slot)

            def attention(name, units, dst):
                s = att[name]
                steps, groups, per = att_dims(name)
                flat = [u for _ in range(groups) for u in units] if name != "ca" else units
                n_units = len(flat)
                with loop(act, steps) as i:
                    u0 = n_units * i

                    def exps(u):
                        par, nk = u % 2, flat[u]["nk"]
                        act.wait_ge(s["negmax"], u0 + (u + 1))
                        if u >= 2:
                            act.wait_ge(s["transposed"], u0 + (u - 1))
                        for hd in range(2):
                            x = 2 * par + hd
                            last = nc.scalar.activation(probs[:, x * S:x * S + nk], bank(2 + x, nk), ACT.Exp,
                                                        bias=negmax[:, x:x + 1], accum_out=total[:, x:x + 1])
                        last.then_inc(s["probs"], 1)

                    def copy(u):
                        par, nk = u % 2, flat[u]["nk"]
                        act.wait_ge(s["transposed"], u0 + (u + 1))
                        if u >= 2:
                            act.wait_ge(s["summed"], u0 + (u - 1))
                        h, w = min(nk, P), max(nk, P)
                        nc.scalar.copy(probs_t[0:h, 2 * par * S:2 * par * S + w], psum[0:h, 6, 0:w]) \
                            .then_inc(s["copied_a"], 1)

                    def store(g):
                        act.wait_ge(s["turned"], groups * i + (g + 1))
                        nc.scalar.copy(dst(i, g), psum[:, 1, :] if name != "ca" else
                                       psum[:, 1, :].rearrange("p (c t) -> p c t", c=4)).then_inc(s["stored"], 1)

                    exps(0)
                    for u in range(n_units):
                        if u + 1 < n_units:
                            exps(u + 1)
                        if u >= 2 and flat[u - 2]["last"]:
                            store((u - 2) // per)
                        copy(u)
                    if n_units > 1 and flat[n_units - 2]["last"]:
                        store((n_units - 2) // per)
                    store(groups - 1)

            for c in range(KD):
                act.wait_ge(x_in[c // 2], 16)
                nc.scalar.activation(chunk(c), xt[:, c * S:(c + 1) * S], ACT.Square).then_inc(x_squared, 1)
            hi(0, 0)
            act.wait_ge(consts, 1)
            norm(0, 2)
            norm_hi(0, h_hi)
            hi(0, 1)
            def cmp_input(i, j):
                for k in range(2 * j, 2 * j + 2):
                    wait_tile("cmp_kv", i, k)
                    for g in range(2):
                        src = psum[64 * g:64 * g + 64, k % 2, :]
                        dst = chunk(16 + 2 * k + g)
                        nc.scalar.copy(dst[0:64, :], src)
                        last = nc.scalar.copy(dst[64:P, 0:S - 1], src[:, 1:S])
                    last.then_inc(evac[k % 2], 1)

            phase("cmp_kv", 1, cmp_input)
            take("nsa_v", 1, lambda i, k: chunk(12 + k), tokens=0, banks=TOKEN_BANK)
            wait_tile("nsa_g", 0, 0)
            nc.scalar.activation(gate_rows, psum[0:48, 0, :], ACT.Sigmoid).then_inc(evac[0], 1)
            wait_tile("nsa_g", 0, 1)
            nc.scalar.copy(gates[:, :], bank(1, NT * 48)).then_inc(evac[1], 1)

            take("nsa_k", 1, lambda i, k: chunk(8 + k))
            act.wait_ge(blocks, 32)
            act.dma_start(mem_raw, a["mem"]).then_inc(mem_in, 16)
            for i in range(2):
                for j in range(2):
                    for k in range(2 * j, 2 * j + 2):
                        wait_tile("nsa_q", i, k)
                        nc.scalar.activation(chunk(4 * i + k), bank(k % 2), ACT.Copy, scale=HD ** -0.5) \
                            .then_inc(evac[k % 2], 1)
                    hi(PAIR0["nsa_q"] + 1 + i, j, whole=i == 1)
            norm(1, 2, MEM)
            for i in range(2):
                act.wait_ge(slot0_free, 2 + i)
                hi(PAIR0["cmp_w1"] + 1 + i, 0, whole=i == 0)
                for k in range(2):
                    wait_tile("cmp_w1", i, k)
                    h0 = (2 * i + k) * CMPW
                    nc.scalar.activation(hid[:, h0:h0 + CMPW], bank(k, CMPW), ACT.Gelu_apprx_tanh).then_inc(evac[k], 1)
                hi(PAIR0["cmp_w1"] + 1 + i, 1, whole=i == 0)
            wait_tile("cmp_w2", 0, 0)
            nc.scalar.copy(kcmp[:, :], bank(0, CMPW)).then_inc(evac[0], 1)
            wait_tile("cmp_w2", 0, 1)
            nc.scalar.copy(vcmp[:, :], psum[0:NCMP, 1, 0:G * HD]).then_inc(evac[1], 1)
            attention("nsa", nsa_units(), lambda i, g: cols(h_hi, nsa_chunk(i, g) * S))
            take("mem_k", 2, lambda i, k: cols(memk, 4 * MEM * i + k * MEM, MEM), MEM)
            through("nsa_out", 2)
            norm(2, 2)
            take("mem_v", 2, lambda i, k: cols(memv, S * i + k * D), tokens=3, banks=TOKEN_BANK)
            take("ca_q", 2, lambda i, k: cols(big, 4 * S * i + k * S), scale=256 ** -0.5)
            attention("ca", ca_units(), lambda i, g: h_hi[:, :].rearrange("p (c t) -> p c t", c=KD)
                      [:, 4 * (g // NT):4 * (g // NT) + 4, (g % NT) * P:(g % NT + 1) * P])
            through("ca_out", 2)
            norm(3, 2)
            norm_hi(3, h_hi)

            def ffn_gate(part, done):
                def slot(i, j):
                    act.wait_ge(evac[0], TILE0[part] // 2 + j + 1 + 2 * i)
                    nc.scalar.activation(act_o[:, j * S:(j + 1) * S], tmp[:, j * S:(j + 1) * S], ACT.Silu) \
                        .then_inc(gated, 1)
                    wait_tile(part, i, 2 * j + 1)
                return slot

            phase("ffn_up_a", HALF["ffn_a"] // 2, ffn_gate("ffn_up_a", 0))
            through("ffn_down_a", 4)
            phase("ffn_up_b", HALF["ffn_b"] // 2, ffn_gate("ffn_up_b", 12))
            through("ffn_down_b", 4)
            norm(4, 2)
            act.wait_ge(product_sum, 1)
            nc.scalar.activation(rstd2, acc[:, :], ACT.Sqrt, bias=eps[:, 0:1], scale=1.0 / D).then_inc(std_done, 1)
            norm_hi(4, h_hi)

            def ml_silu(i, j):
                for k in range(2 * j, 2 * j + 2):
                    b = k % 2
                    act.wait_ge(evac[b], TILE0["ml_qk"] // 2 + k // 2 + 1 + 2 * i)
                    nc.scalar.activation(cols(big, 4 * S * i + k * S), tmp[:, b * S:(b + 1) * S], ACT.Silu) \
                        .then_inc(gated, 1)

            phase("ml_qk", 2, ml_silu)
            ml = ml_step
            act.wait_ge(tile_done, TILE0["ml_if"] + 1)
            nc.scalar.activation(ig[:, :], psum[0:MLH, 0, :], ACT.Identity,
                                 bias=params[0:MLH, COL["b_i"]:COL["b_i"] + 1]).then_inc(evac[0], 1)
            act.wait_ge(ml["z"], 2)
            nc.scalar.activation(fe[:, :], fe[:, :], ACT.Exp, scale=-1.0).then_inc(ml["e"], 1)
            act.wait_ge(ml["e"], 1)
            nc.scalar.activation(fe[:, :], fe[:, :], ACT.Ln, bias=ones[0:MLH, 0:1]).then_inc(ml["l"], 1)
            take("ml_v", 2, lambda i, k: cols(big, S * i + 8 * S + k * D), tokens=5, banks=TOKEN_BANK)
            take("ml_o", 2, lambda i, k: cols(big, 4 * S * i + (16 + k) * S), func=ACT.Sigmoid)
            act.wait_ge(ml["u_col"], 1)
            nc.scalar.copy(u_col[:, :], bank(2, NT * MLH)).then_inc(ml["u_col"], 1)
            act.wait_ge(ml["u_col"], 2)

            def spread(h):
                if h:
                    act.wait_ge(ml["decay"], (NT + 1) * h)
                act.wait_ge(ml["bc"], 2 * h + 1)
                nc.scalar.copy(q_st[:, 0:S], bank(7)).then_inc(ml["bc_used"], 1)
                act.wait_ge(ml["bc"], 2 * h + 2)
                if h >= 2:
                    act.wait_ge(ml["recip"], 3 * (h - 1))
                nc.scalar.activation(chunk(30 + h % 2), bank(7), ACT.Exp).then_inc(ml["bc_used"], 1)

            def decays(h):
                act.wait_ge(ml["decay"], (NT + 1) * h + 1)
                if h:
                    act.wait_ge(ml["weighted"], NT * h)
                for st in range(NT):
                    e0 = 24 * S + ML_AT[st]
                    w = S - (st + 1) * P
                    uc = u_col[:, st * MLH + h:st * MLH + h + 1]
                    last = nc.scalar.activation(big[:, e0:e0 + P], q_st[:, S + st * P:S + (st + 1) * P], ACT.Exp,
                                                bias=uc, scale=-1.0)
                    if w:
                        last = nc.scalar.activation(big[:, e0 + P:e0 + P + w], q_st[:, (st + 1) * P:S], ACT.Exp,
                                                    bias=uc, scale=-1.0)
                    last.then_inc(ml["decay"], 1)

            def head_squares(h):
                if h:
                    act.wait_ge(ml["ssq"], h)
                for dv in range(2):
                    act.wait_ge(ml["h"], 2 * h + dv + 1)
                    nc.scalar.activation(chunk(28 + dv), ml_h[h % 2][dv], ACT.Square) \
                        .then_inc(ml["sq"], 1)

            def head_std(h):
                act.wait_ge(ml["ssq"], h + 1)
                if h:
                    act.wait_ge(ml["scaled"], 2 * h)
                nc.scalar.activation(rstd[:, :], bank(7), ACT.Sqrt, bias=eps[:, 0:1], scale=1.0 / 256) \
                    .then_inc(ml["std"], 1)

            def y_hi(h):
                for dv in range(2):
                    act.wait_ge(ml["gate"], 2 * h + dv + 1)
                    nc.scalar.copy(chunk_r(16 + 2 * h + dv), ml_y[dv]).then_inc(ml["y_hi"], 1)

            spread(0)
            decays(0)
            for h in range(MLH):
                if h + 1 < MLH:
                    spread(h + 1)
                    decays(h + 1)
                if h:
                    head_squares(h - 1)
                if h >= 2:
                    y_hi(h - 2)
                if h:
                    head_std(h - 1)
            head_squares(MLH - 1)
            y_hi(MLH - 2)
            head_std(MLH - 1)
            y_hi(MLH - 1)

            def gate(name):
                def slot(i, j):
                    wait_tile(name, i, 2 * j)
                    act.wait_ge(evac[1], TILE0[name] // 2 + j - 1 + 2 * i)
                    nc.scalar.activation(act_o[:, j * S:(j + 1) * S], bank(0), ACT.Sigmoid).then_inc(evac[0], 1)
                    wait_tile(name, i, 2 * j + 1)
                phase(name, 4, slot)

            act.wait_ge(ml["y"], 2 * MLH)
            gate("merge_a")
            take("sw_q", 2, lambda i, k: cols(big, 4 * S * i + k * S), scale=HD ** -0.5)

            def sw_kv(i, j):
                for k in ((0, 1), (2, 3, 4, 5))[j]:
                    wait_tile("sw_kv", 0, k)
                    src = bank(k % 2) if k < 2 else bank(k % 2, 256)
                    dst = chunk(24 + k) if k < 2 else big[:, 26 * S + (k - 2) * 256:26 * S + (k - 1) * 256]
                    nc.scalar.copy(dst, src).then_inc(evac[k % 2], 1)

            phase("sw_kv", 1, sw_kv)
            s = att["sw"]

            def exps(u):
                par, (_, nk) = u % 2, sw_keys(u % NT)
                act.wait_ge(s["negmax"], u + 1)
                if u >= 2:
                    act.wait_ge(s["transposed"], u - 1)
                for x in range(4):
                    p0, c = par * 2 * S + x * SWK, 4 * par + x
                    nc.scalar.activation(probs[:, p0:p0 + nk], sw_score(par, x, nk), ACT.Exp,
                                         bias=negmax[:, c:c + 1], accum_out=total[:, c:c + 1])
                nc.scalar.activation(sink_e[:, 4 * par:4 * par + 4], sink_arg[:, 4 * par:4 * par + 4], ACT.Exp) \
                    .then_inc(s["probs"], 1)

            def copy(u):
                par, (_, nk) = u % 2, sw_keys(u % NT)
                act.wait_ge(s["transposed"], u + 1)
                if u >= 2:
                    act.wait_ge(s["summed"], u - 1)
                nc.scalar.copy(sw_pairs(probs_t[:, par * 2 * S:par * 2 * S + S], nk), sw_pairs(bank(6), nk)) \
                    .then_inc(s["copied_a"], 1)

            def store(quad, g):
                act.wait_ge(s["turned"], 2 * quad + g + 1)
                nc.scalar.copy(chunk_r(4 * g + quad), bank(1)).then_inc(s["stored"], 1)

            exps(0)
            for u in range(SW_UNITS):
                if u + 1 < SW_UNITS:
                    exps(u + 1)
                if u >= NT and u % NT in (1, 2):
                    store(u // NT - 1, u % NT - 1)
                copy(u)
            for g in range(2):
                store(SW_UNITS // NT - 1, g)
            act.wait_ge(att["sw"]["split"], PAIRS)
            act.dma_start(ple_raw, a["ple"]).then_inc(ple_in, 16)
            gate("merge_b")
            through("mix_out", 2)
            norm(6, 2)
            norm_hi(5, h_hi)

            def squared_relu(part, done):
                def slot(i, j):
                    for k in range(2 * j, 2 * j + 2):
                        b = k % 2
                        wait_tile(part, i, k)
                        nc.scalar.activation(act_o[:, b * S:(b + 1) * S], bank(b), ACT.Relu).then_inc(evac[b], 1)
                        act.wait_ge(evac[b], TILE0[part] // 2 + k // 2 + 1 + 2 * i)
                        act.wait_ge(split_done, done + k - 1 + 4 * i)
                        nc.scalar.activation(tmp[:, b * S:(b + 1) * S], act_o[:, b * S:(b + 1) * S], ACT.Square) \
                            .then_inc(squared, 1)
                return slot

            phase("mlp_up_a", 4, squared_relu("mlp_up_a", SPLIT0["mlp_a"]))
            through("mlp_down_a", 4)
            phase("mlp_up_b", 4, squared_relu("mlp_up_b", SPLIT0["mlp_b"]))
            through("mlp_down_b", 4)
            hi(PAIR0["ple_g"], 0)
            norm(7, 2)
            for c in range(KD):
                wait_tile("ple_v", 0, c)
                nc.scalar.copy(chunk(c), bank(c % 2)).then_inc(evac[c % 2], 1)
                norm_hi(6, h_hi, chunks=(c,))
            hi(PAIR0["ple_g"], 1)

            def ple_gate(i, j):
                for k in range(2 * j, 2 * j + 2):
                    wait_tile("ple_g", i, k)
                    if 4 * i + k >= 2:
                        act.wait_ge(gate_used, 4 * i + k - 1)
                    b = k % 2
                    nc.scalar.activation(act_o[:, b * S:(b + 1) * S], bank(b), ACT.Sigmoid).then_inc(evac[b], 1)

            phase("ple_g", 2, ple_gate, last=True)
            norm(8, 2)

        @block.vector
        def _(dve):
            V = nc.vector
            d = Count(dve_step)
            sq = Count(squares)
            nm = Count(normed)

            def step(ins):
                ins.then_inc(dve_step, 1)
                d.n += 1

            def settle():
                dve.wait_ge(dve_step, d.at)

            def square(src, n=S):
                step(V.tensor_tensor(sqt[:, 0:n], src, src, ALU.mult))
                settle()
                V.tensor_tensor(acc[:, 0:n], acc[:, 0:n], sqt[:, 0:n], ALU.add).then_inc(squares, 1)
                sq.n += 1
                dve.wait_ge(squares, sq.at)

            def clear_acc():
                step(V.memset(acc[:, :], 0.0))
                settle()

            rx, ns, sp_ = Count(raw_x), Count(normed), Count(split_done)

            def scale_of(m, n=S):
                dve.wait_ge(std_done, m + 1)
                step(V.reciprocal(rstd[:, 0:n], rstd[:, 0:n]))
                settle()

            def norm(m, name, src, hi_buf, lo_buf, n=S, own_hi=False, by=None):
                if by is None:
                    scale_of(m, n)
                gain, scale = by or (params[:, COL[name]:COL[name] + KD], rstd)

                def low(c):
                    if own_hi:
                        dve.wait_ge(raw_x, ns.n + 1)
                        V.tensor_scalar(hi_buf[:, c * n:(c + 1) * n], tmp[:, (c % 2) * S:(c % 2) * S + n], 1.0, None,
                                        ALU.mult).then_inc(hi_x, 1)
                    dve.wait_ge(hi_x, ns.n + 1)
                    V.tensor_tensor(lo_buf[:, c * n:(c + 1) * n], tmp[:, (c % 2) * S:(c % 2) * S + n],
                                    plain(hi_buf[:, c * n:(c + 1) * n]), ALU.subtract).then_inc(normed, 1)
                    ns.n += 1

                for c in range(KD):
                    if ns.n >= 1:
                        dve.wait_ge(normed, ns.n)
                    V.scalar_tensor_tensor(out=tmp[:, (c % 2) * S:(c % 2) * S + n], in0=src(c),
                                           scalar=gain[:, c:c + 1], in1=scale[:, 0:n], op0=ALU.mult,
                                           op1=ALU.mult).then_inc(raw_x, 1)
                    if c:
                        low(c - 1)
                low(KD - 1)

            def split(src, hi_, lo_):
                step(V.tensor_scalar(hi_, src, 1.0, None, ALU.mult))
                settle()
                V.tensor_tensor(lo_, src, plain(hi_), ALU.subtract).then_inc(split_done, 1)
                sp_.n += 1

            xc = lambda c: xt[:, c * S:(c + 1) * S]

            def residual(name, steps, per, sums=1):
                if sums:
                    clear_acc()
                if sums == 2:
                    step(V.memset(acc2, 0.0))
                with dve.Fori(0, steps) as i:
                    if sums:
                        d.enter(i, per)
                        sq.enter(i, per * sums)
                    for k in range(per):
                        b = k % 2
                        x = cols(xt, per * S * i + k * S)
                        dve.wait_ge(tile_done, TILE0[name] + k + 1 + per * i)
                        V.tensor_tensor(x, bank(b), x, ALU.add).then_inc(evac[b], 1)
                        if sums:
                            dve.wait_ge(evac[b], TILE0[name] // 2 + k // 2 + 1 + (per // 2) * i)
                            square(x)
                        if sums == 2:
                            V.scalar_tensor_tensor(out=acc2, in0=sqt[:, :], scalar=gains[:, bass.ds(per * i + k, 1)],
                                                   in1=acc2, op0=ALU.mult, op1=ALU.add).then_inc(squares, 1)
                            sq.n += 1
                            dve.wait_ge(squares, sq.at)
                if sums:
                    d.leave(steps)
                    sq.leave(steps)

            def convolve(name, taps, col, n_ch, i, k, ch, bank_):
                t0 = (k % 2) * S
                for m in range(taps):
                    w = params[:, bass.ds(ch + (col + (taps - 1 - m) * n_ch), 1)]
                    src = psum[:, bank_, 0:S - m]
                    o = tmp[:, t0 + m:t0 + S]
                    if m == 0:
                        ins = V.tensor_scalar(o, src, w, None, ALU.mult)
                    else:
                        ins = V.scalar_tensor_tensor(out=o, in0=src, scalar=w, in1=o, op0=ALU.mult, op1=ALU.add)
                    if m < taps - 1:
                        step(ins)
                        settle()
                    else:
                        ins.then_inc(evac[bank_], 1)

            def attention(name, units, per_step, hi_of, lo_of, gate=None):
                s = att[name]
                steps, groups, per = att_dims(name)
                flat = [u for _ in range(groups) for u in units] if name != "ca" else units
                n_units = len(flat)
                width = 256 if name == "ca" else HD
                with loop(dve, steps) as i:
                    if steps > 1:
                        d.enter(i, per_step)
                    u0 = n_units * i

                    def maxima(u):
                        par, nk = u % 2, flat[u]["nk"]
                        dve.wait_ge(s["scores"], u0 + (u + 1))
                        nm_ = negmax[:, 2 * par:2 * par + 2]
                        ins = V.tensor_reduce(nm_, psum[:, 2 + 2 * par:4 + 2 * par, 0:nk], axis=AX_X, op=ALU.max,
                                              negate=True)
                        ins.then_inc(s["negmax"], 1)

                    def copy(u):
                        par, nk = u % 2, flat[u]["nk"]
                        dve.wait_ge(s["transposed"], u0 + (u + 1))
                        if u >= 2:
                            dve.wait_ge(s["summed"], u0 + (u - 1))
                        h, w = min(nk, P), max(nk, P)
                        V.tensor_copy(probs_t[0:h, (2 * par + 1) * S:(2 * par + 1) * S + w], psum[0:h, 7, 0:w]) \
                            .then_inc(s["copied_d"], 1)

                    def weights(u):
                        par, g = u % 2, u // per
                        t, c = total[:, 2 * par:2 * par + 2], coef[:, 2 * par:2 * par + 2]
                        step(V.reciprocal(c, t))
                        if gate is not None:
                            settle()
                            gt = gates[:, :].rearrange("p (x b) -> p x b", b=3)[
                                :, bass.ds(nsa_chunk(i, g) * 2 + flat[u]["qt"] * 16, 2), flat[u]["br"]]
                            if flat[u]["br"] == 0:
                                ins = V.scalar_tensor_tensor(out=c, in0=c, scalar=cmp_any[:, flat[u]["qt"]:flat[u]["qt"] + 1],
                                                             in1=gt, op0=ALU.mult, op1=ALU.mult)
                            else:
                                ins = V.tensor_tensor(c, c, gt, ALU.mult)
                            step(ins)

                    def combine(u):
                        par, g = u % 2, u // per
                        settle()
                        dve.wait_ge(s["summed"], u0 + (u + 1))
                        if not flat[u]["first"]:
                            dve.wait_ge(s["combined"], u0 + u)
                        for hd in range(2):
                            o0 = (g % 2) * S + hd * width + (0 if name == "ca" else flat[u]["qt"] * P)
                            o, c = o_acc[:, o0:o0 + width], coef[:, 2 * par + hd:2 * par + hd + 1]
                            s0 = hd * width if name == "ca" else 2 * par * P + hd * (P + HD)
                            src = psum[:, 0, s0:s0 + width]
                            if flat[u]["first"]:
                                last = V.tensor_scalar(o, src, c, None, ALU.mult)
                            else:
                                last = V.scalar_tensor_tensor(out=o, in0=src, scalar=c, in1=o, op0=ALU.mult,
                                                              op1=ALU.add)
                        last.then_inc(s["combined"], 1)

                    def low(g):
                        dve.wait_ge(s["stored"], groups * i + (g + 1))
                        src = psum[:, 1, :] if name != "ca" else psum[:, 1, :].rearrange("p (c t) -> p c t", c=4)
                        V.tensor_tensor(lo_of(i, g), src, plain(hi_of(i, g)), ALU.subtract).then_inc(s["split"], 1)

                    maxima(0)
                    for u in range(n_units):
                        if u + 1 < n_units:
                            maxima(u + 1)
                        if u >= 1:
                            combine(u - 1)
                        if u >= 2 and flat[u - 2]["last"]:
                            low((u - 2) // per)
                        copy(u)
                        weights(u)
                    combine(n_units - 1)
                    if n_units > 1 and flat[n_units - 2]["last"]:
                        low((n_units - 2) // per)
                    low(groups - 1)
                if steps > 1:
                    d.leave(steps)

            clear_acc()
            for c in range(KD):
                dve.wait_ge(x_squared, c + 1)
                V.tensor_tensor(acc[:, :], acc[:, :], chunk(c), ALU.add).then_inc(squares, 1)
                sq.n += 1
                dve.wait_ge(squares, sq.at)
            dve.wait_ge(par_in, 16)
            step(V.tensor_scalar(neg_sink[:, :], params[:, COL["sink"]:COL["sink"] + 16], -1.0, None, ALU.mult))
            norm(0, "mix", xc, h_hi, h_lo)
            final, mix2 = (params[:, COL[n]:COL[n] + KD] for n in ("final", "mix2"))
            step(V.tensor_tensor(gains[:, 0:KD], final, final, ALU.mult))
            step(V.tensor_tensor(gains[:, KD:2 * KD], final, mix2, ALU.mult))
            dve.wait_ge(small_in, 64)
            V.tensor_copy(wg_hi, w_gate).then_inc(small_split, 1)
            V.tensor_copy(wi_hi[:, :], w_if).then_inc(small_split, 1)
            dve.wait_ge(small_split, 2)
            V.tensor_tensor(wg_lo, w_gate, plain(wg_hi), ALU.subtract).then_inc(small_split, 1)
            V.tensor_tensor(wi_lo[:, :], w_if, plain(wi_hi[:, :]), ALU.subtract).then_inc(small_split, 1)
            for kind in range(2):
                for b in range(2):
                    dve.wait_ge(evac[b], TILE0["cmp_kv"] // 2 + kind + 1)
                src = big[:, (16 + 4 * kind) * S:(20 + 4 * kind) * S].rearrange("p (g t) -> p g t", g=G)
                for j in range(16):
                    d0 = (24 + 4 * kind) * S + j * CMPW
                    c = COL["pe_k" if kind == 0 else "pe_v"] + j
                    V.tensor_scalar(big[:, d0:d0 + CMPW].rearrange("p (g n) -> p g n", g=G),
                                    src[:, :, 2 * j:2 * j + 16 * (NCMP - 1) + 1:16], params[:, c:c + 1], None,
                                    ALU.add).then_inc(blocks, 1)
            clear_acc()
            dve.wait_ge(mem_in, 16)
            for c in range(KD):
                square(mem_raw[:, c * MEM:(c + 1) * MEM], MEM)
            norm(1, "mem", lambda c: mem_raw[:, c * MEM:(c + 1) * MEM], mem_hi, mem_lo, MEM, own_hi=True)
            attention("nsa", nsa_units(), NSA_GROUPS_STEP * NU * 2, lambda i, g: cols(h_hi, nsa_chunk(i, g) * S),
                      lambda i, g: cols(h_lo, nsa_chunk(i, g) * S), gate=True)
            residual("nsa_out", 2, 4)
            norm(2, "cross", xc, h_hi, h_lo, own_hi=True)

            def by_unit(buf):
                return lambda i, g: buf[:, :].rearrange("p (c t) -> p c t", c=KD)[
                    :, 4 * (g // NT):4 * (g // NT) + 4, (g % NT) * P:(g % NT + 1) * P]

            attention("ca", ca_units(), 0, by_unit(h_hi), by_unit(h_lo))
            residual("ca_out", 2, 4)
            norm(3, "ffn", xc, h_hi, h_lo)

            def ffn_hidden(part, steps, ch0):
                with dve.Fori(0, steps) as i:
                    d.enter(i, 6)
                    sp_.enter(i, 2)
                    for j in range(2):
                        dve.wait_ge(tile_done, TILE0[part] + 2 * j + 1 + 4 * i)
                        convolve(part, 3, COL["ffn_conv"] + ch0, FC, i, j, 2 * i + j, 0)
                        dve.wait_ge(tile_done, TILE0[part] + 2 * j + 2 + 4 * i)
                        dve.wait_ge(gated, ch0 + j + 1 + 2 * i)
                        if ch0 or j:
                            dve.wait_ge(split_done, sp_.at)
                        V.tensor_tensor(sqt[:, :], bank(1), act_o[:, j * S:(j + 1) * S], ALU.mult).then_inc(evac[1], 1)
                        dve.wait_ge(evac[1], TILE0[part] // 2 + j + 1 + 2 * i)
                        split(sqt[:, :], cols(big_r, 2 * S * i + j * S), cols(big_r, 2 * S * i + (16 + j) * S))
                d.leave(steps)
                sp_.leave(steps)

            ffn_hidden("ffn_up_a", HALF["ffn_a"] // 2, 0)
            residual("ffn_down_a", 4, 2, 0)
            ffn_hidden("ffn_up_b", HALF["ffn_b"] // 2, HALF["ffn_a"])
            residual("ffn_down_b", 4, 2, 2)
            scale_of(4)
            step(V.tensor_tensor(sqt[:, :], rstd[:, :], rstd[:, :], ALU.mult))
            settle()
            dve.wait_ge(stat, 6)
            V.tensor_tensor(acc[:, :], bank(3), sqt[:, :], ALU.mult).then_inc(product_sum, 1)
            dve.wait_ge(std_done, 6)
            step(V.reciprocal(rstd2, rstd2))
            settle()
            step(V.tensor_tensor(rstd2, rstd2, rstd[:, :], ALU.mult))
            settle()
            norm(5, "mix2", xc, h_hi, h_lo, by=(gains[:, KD:2 * KD], rstd2))
            for c in range(KD):
                g0 = COL["final"] + c
                step(V.scalar_tensor_tensor(out=xc(c), in0=xc(c), scalar=params[:, g0:g0 + 1], in1=rstd[:, :],
                                            op0=ALU.mult, op1=ALU.mult))
            with dve.Fori(0, 2) as i:
                d.enter(i, 12)
                for k in range(4):
                    dve.wait_ge(tile_done, TILE0["ml_qk"] + k + 1 + 4 * i)
                    dve.wait_ge(gated, FC + k - 1 + 4 * i)
                    convolve("ml_qk", 4, COL["ml_conv"], 8, i, k, 4 * i + k, k % 2)
            d.leave(2)
            ml = ml_step
            dve.wait_ge(tile_done, TILE0["ml_if"] + 2)
            V.tensor_scalar(fz[:, :], psum[0:MLH, 1, :], params[0:MLH, COL["b_f"]:COL["b_f"] + 1], None, ALU.add) \
                .then_inc(evac[1], 1)
            dve.wait_ge(evac[1], TILE0["ml_v"] // 2)
            V.tensor_scalar(fe[:, :], fz[:, :], -1.0, None, ALU.mult).then_inc(ml["z"], 1)
            dve.wait_ge(ml["z"], 1)
            V.tensor_tensor(fe[:, :], fe[:, :], fz[:, :], ALU.max).then_inc(ml["z"], 1)
            step(V.memset(sqt[:, :], 1.0))
            dve.wait_ge(ml["l"], 1)
            V.scalar_tensor_tensor(out=fz[:, :], in0=fz[:, :], scalar=0.0, in1=fe[:, :], op0=ALU.min,
                                   op1=ALU.subtract).then_inc(ml["rows"], 1)
            settle()
            dve.wait_ge(ml["rows"], 1)
            V.tensor_tensor_scan(fcum[:, :], sqt[0:MLH, :], fz[:, :], 0.0, ALU.mult, ALU.add).then_inc(ml["rows"], 1)
            dve.wait_ge(ml["rows"], 2)
            dve.wait_ge(evac[0], TILE0["ml_v"] // 2)
            V.tensor_tensor(u_row[:, :], ig[:, :], fcum[:, :], ALU.subtract).then_inc(ml["rows"], 1)
            dve.wait_ge(ml["rows"], 3)
            V.tensor_tensor_scan(m_row[:, :], u_row[:, :], u_row[:, :], 0.0, ALU.max, ALU.max).then_inc(ml["rows"], 1)
            dve.wait_ge(ml["rows"], 4)
            V.scalar_tensor_tensor(out=nm_row[:, :], in0=fcum[:, :], scalar=-1.0, in1=m_row[:, :], op0=ALU.mult,
                                   op1=ALU.subtract).then_inc(ml["rows"], 1)

            def mask(h):
                dve.wait_ge(ml["bc_used"], 2 * h + 1)
                V.tensor_tensor(q_st[:, S:2 * S].rearrange("p (c t) -> p c t", c=NT),
                                q_st[:, 0:S].rearrange("p (c t) -> p c t", c=NT),
                                ml_mask[:, :].unsqueeze(1).to_broadcast([P, NT, P]), ALU.add).then_inc(ml["decay"], 1)

            def weigh(h):
                if h >= 2:
                    dve.wait_ge(ml["sums"], h - 1)
                for st in range(NT):
                    dve.wait_ge(ml["scores"], NT * h + st + 1)
                    dve.wait_ge(ml["decay"], (NT + 1) * h + st + 2)
                    w = S - st * P
                    p0, e0 = ML_AT[st], 24 * S + ML_AT[st]
                    V.scalar_tensor_tensor(out=ml_weights[h % 2][:, p0:p0 + w], in0=psum[:, 2 + st, 0:w],
                                           scalar=float(P) ** -0.5, in1=big[:, e0:e0 + w], op0=ALU.mult,
                                           op1=ALU.mult).then_inc(ml["weighted"], 1)

            def quotient(h):
                dve.wait_ge(ml["sums"], h + 1)
                dve.wait_ge(ml["bc_used"], 2 * h + 2)
                V.scalar_tensor_tensor(out=tmp[:, S:2 * S], in0=bank(6), scalar=-1.0, in1=chunk(30 + h % 2),
                                       op0=ALU.mult, op1=ALU.max).then_inc(ml["recip"], 1)
                dve.wait_ge(ml["recip"], 3 * h + 1)
                V.tensor_tensor(tmp[:, S:2 * S], bank(6), tmp[:, S:2 * S], ALU.max).then_inc(ml["recip"], 1)
                dve.wait_ge(ml["recip"], 3 * h + 2)
                V.reciprocal(sqt[:, :], tmp[:, S:2 * S]).then_inc(ml["recip"], 1)
                dve.wait_ge(ml["recip"], 3 * h + 3)
                for dv in range(2):
                    V.tensor_tensor(ml_h[h % 2][dv], bank(dv), sqt[:, :], ALU.mult).then_inc(ml["h"], 1)

            def output(h):
                dve.wait_ge(ml["std"], h + 1)
                step(V.reciprocal(rstd[:, :], rstd[:, :]))
                settle()
                if h:
                    dve.wait_ge(ml["y"], 2 * h)
                for dv in range(2):
                    w = COL["mlstm"] + 2 * h + dv
                    V.scalar_tensor_tensor(out=ml_y[dv], in0=ml_h[h % 2][dv], scalar=params[:, w:w + 1], in1=rstd[:, :], op0=ALU.mult, op1=ALU.mult).then_inc(ml["scaled"], 1)
                dve.wait_ge(ml["scaled"], 2 * h + 2)

            mask(0)
            weigh(0)
            mask(1)
            for h in range(MLH):
                if h + 1 < MLH:
                    weigh(h + 1)
                quotient(h)
                if h:
                    output(h - 1)
                if h + 2 < MLH:
                    mask(h + 2)
            output(MLH - 1)
            with dve.Fori(0, 4) as i:
                for j in range(2):
                    dve.wait_ge(tile_done, TILE0["merge_a"] + 2 * j + 2 + 4 * i)
                    dve.wait_ge(evac[0], TILE0["merge_a"] // 2 + j + 1 + 2 * i)
                    V.tensor_tensor(cols(big, 2 * S * i + (8 + j) * S), bank(1), act_o[:, j * S:(j + 1) * S], ALU.mult) \
                        .then_inc(evac[1], 1)
            s = att["sw"]

            def maxima(u):
                par, (_, nk), quad = u % 2, sw_keys(u % NT), u // NT
                sink = slice(4 * quad, 4 * quad + 4)
                nm_ = negmax[:, 4 * par:4 * par + 4]
                dve.wait_ge(s["scores"], u + 1)
                step(V.tensor_reduce(nm_.rearrange("p (b x) -> p b x", b=2),
                                     psum[:, 2 + 2 * par:4 + 2 * par, :].rearrange("p b (x k) -> p b x k", k=SWK)
                                     [:, :, :, 0:nk], axis=AX_X, op=ALU.max, negate=True))
                settle()
                step(V.tensor_tensor(nm_, nm_, neg_sink[:, sink], ALU.min))
                settle()
                V.tensor_tensor(sink_arg[:, 4 * par:4 * par + 4], nm_, neg_sink[:, sink], ALU.subtract) \
                    .then_inc(s["negmax"], 1)

            def copy(u):
                par, (_, nk) = u % 2, sw_keys(u % NT)
                dve.wait_ge(s["transposed"], u + 1)
                if u >= 2:
                    dve.wait_ge(s["summed"], u - 1)
                V.tensor_copy(sw_pairs(probs_t[:, par * 2 * S + S:par * 2 * S + 2 * S], nk), sw_pairs(bank(7), nk)) \
                    .then_inc(s["copied_d"], 1)

            def weights(u):
                c = slice(4 * (u % 2), 4 * (u % 2) + 4)
                step(V.tensor_tensor(total[:, c], total[:, c], sink_e[:, c], ALU.add))
                settle()
                step(V.reciprocal(coef[:, c], total[:, c]))

            def combine(u):
                settle()
                dve.wait_ge(s["summed"], u + 1)
                for x in range(4):
                    o0 = (x // 2) * S + (u % NT) * P + (x % 2) * HD
                    s0 = x * P + (x % 2) * HD
                    c = 4 * (u % 2) + x
                    last = V.tensor_scalar(sw_o[u // NT % 2][:, o0:o0 + HD], psum[:, 0, s0:s0 + HD], coef[:, c:c + 1], None,
                                           ALU.mult)
                last.then_inc(s["combined"], 1)

            def low(quad, g):
                dve.wait_ge(s["stored"], 2 * quad + g + 1)
                n = 4 * g + quad
                V.tensor_tensor(chunk_r(n + 16), bank(1), plain(chunk_r(n)), ALU.subtract) \
                    .then_inc(s["split"], 1)

            maxima(0)
            for u in range(SW_UNITS):
                if u + 1 < SW_UNITS:
                    maxima(u + 1)
                if u >= 1:
                    combine(u - 1)
                    if u >= NT and u % NT in (1, 2):
                        low(u // NT - 1, u % NT - 1)
                copy(u)
                weights(u)
            combine(SW_UNITS - 1)
            for g in range(2):
                low(SW_UNITS // NT - 1, g)
            with dve.Fori(0, 4) as i:
                d.enter(i, 4)
                sp_.enter(i, 2)
                for j in range(2):
                    y = tmp[:, j * S:(j + 1) * S]
                    n0 = 2 * S * i + j * S
                    dve.wait_ge(tile_done, TILE0["merge_b"] + 2 * j + 2 + 4 * i)
                    dve.wait_ge(evac[0], TILE0["merge_b"] // 2 + j + 1 + 2 * i)
                    dve.wait_ge(split_done, sp_.at)
                    V.tensor_tensor(y, bank(1), act_o[:, j * S:(j + 1) * S], ALU.mult).then_inc(evac[1], 1)
                    dve.wait_ge(evac[1], TILE0["merge_b"] // 2 + j + 1 + 2 * i)
                    step(V.tensor_tensor(y, cols(big, n0 + 8 * S), y, ALU.add))
                    settle()
                    split(y, cols(big_r, n0 + 8 * S), cols(big_r, n0 + 24 * S))
            d.leave(4)
            sp_.leave(4)
            dve.wait_ge(ple_in, 16)
            V.tensor_copy(ple_hi, ple_raw).then_inc(small_split, 1)
            dve.wait_ge(small_split, 5)
            V.tensor_tensor(ple_lo, ple_raw, plain(ple_hi), ALU.subtract).then_inc(small_split, 1)
            residual("mix_out", 2, 4)
            norm(6, "mlp2", xc, h_hi, h_lo)

            def mlp_hidden(n0):
                with dve.Fori(0, 4) as i:
                    d.enter(i, 4)
                    sp_.enter(i, 4)
                    for k in range(4):
                        dve.wait_ge(squared, n0 + k + 1 + 4 * i)
                        n = 4 * S * i + k * S
                        split(tmp[:, (k % 2) * S:(k % 2 + 1) * S], cols(big_r, n), cols(big_r, n + 16 * S))
                d.leave(4)
                sp_.leave(4)

            mlp_hidden(0)
            residual("mlp_down_a", 4, 2, 0)
            mlp_hidden(F2C // 2)
            residual("mlp_down_b", 4, 2)
            norm(7, "ple2", xc, h_hi, h_lo)
            clear_acc()
            with dve.Fori(0, 2) as i:
                d.enter(i, 8)
                sq.enter(i, 4)
                for k in range(4):
                    b = k % 2
                    y = tmp[:, b * S:(b + 1) * S]
                    c0 = 4 * S * i + k * S
                    dve.wait_ge(evac[b], TILE0["ple_g"] // 2 + k // 2 + 1 + 2 * i)
                    V.tensor_tensor(y, cols(big, c0), act_o[:, b * S:(b + 1) * S], ALU.mult).then_inc(gate_used, 1)
                    dve.wait_ge(gate_used, 4 * i + (k + 1))
                    step(V.tensor_tensor(cols(xt, c0), cols(xt, c0), y, ALU.add))
                    settle()
                    square(cols(xt, c0))
            d.leave(2)
            sq.leave(2)
            scale_of(8)
            for c in range(KD):
                g0 = COL["final2"] + c
                V.scalar_tensor_tensor(out=chunk(c), in0=xc(c), scalar=params[:, g0:g0 + 1], in1=rstd[:, :],
                                       op0=ALU.mult, op1=ALU.mult).then_inc(final_out, 1)

        @block.gpsimd
        def _(pool):
            g = nc.gpsimd
            for buf, value in ((ident, 0.0), (ones, 1.0), (causal, 0.0), (band, 0.0), (cmp_mask, 0.0), (cmp_any, 1.0),
                               (ml_mask, 0.0), (eps, EPS)):
                last = g.memset(buf[:, :], value)
            last.then_inc(pool_step, 1)
            g.memset(start[:, 0:1], 0.0).then_inc(tile_done, 2)
            g.memset(start[:, 1:2], 0.0).then_inc(evac[0], 1)
            g.memset(start[:, 2:3], 0.0).then_inc(evac[1], 1)
            pool.wait_ge(pool_step, 1)

            def keep(buf, pattern, base, per_row, fill, compare=ALU.is_ge):
                return g.affine_select(out=buf, in_=buf, pattern=pattern, compare_op=compare, fill=fill, base=base,
                                       channel_multiplier=per_row)

            keep(ident[:, :], [[-1, P]], 0, 1, 1.0, ALU.not_equal).then_inc(pool_step, 1)
            keep(causal[:, :], [[-1, P]], 0, 1, NEG)
            keep(band[:, 0:P], [[1, P]], -1, -1, NEG)
            keep(band[:, P:2 * P], [[-1, P]], 0, 1, NEG)
            keep(cmp_mask[:, :], [[P, NT], [-16, NCMP]], -31, 1, NEG)
            keep(cmp_any[:, :], [[P, NT]], -31, 1, 0.0)
            keep(ml_mask[:, :], [[1, P]], 0, -1, -NEG)
            pool.wait_ge(pool_step, 2)
            g.tensor_copy(ident_bf[:, :], ident[:, :]).then_inc(consts, 1)

            def low(first, count):
                with loop(pool, count) as i:
                    for j in range(2):
                        p = slice(j * PANEL, (j + 1) * PANEL)
                        pool.wait_ge(hi_done[j], first + 1 + i)
                        g.tensor_tensor(w_lo[:, p], ring[:, p], plain(w_hi[:, p]), ALU.subtract).then_inc(lo_done[j], 1)

            def stage(dst, src, done):
                for hd in range(2):
                    rows = slice(64 * hd, 64 * hd + 64)
                    last = g.tensor_copy(dst(hd)[rows], src[rows])
                last.then_inc(done, 1)

            def taken(phase):
                for b in range(2):
                    pool.wait_ge(evac[b], TILE0[phase] // 2)

            low(0, PAIR0["cmp_w1"])
            for i in range(2):
                for j in range(2):
                    pool.wait_ge(hi_done[j], PAIR0["cmp_w1"] + i + 1)
                    at_ = 3 + 2 * i + j
                    g.memset(start[:, at_:at_ + 1], 0.0).then_inc(lo_done[j], 1)
            s = att["nsa"]
            nsa_q = lambda half_: lambda hd: q_st[:, (2 * half_ + hd) * S:(2 * half_ + hd + 1) * S]
            g.memset(q_st[:, :], 0.0).then_inc(zeroed, 1)
            pool.wait_ge(zeroed, 1)
            taken("cmp_w1")
            for half_ in range(2):
                stage(nsa_q(half_), chunk(4 * half_), s["staged"])
            pool.wait_ge(s["staged"], 2)
            low(PAIR0["mem_k"], 1)
            pool.wait_ge(lo_done[1], PAIR0["mem_k"] + 1)
            with pool.Fori(1, PAIRS // 2) as i:
                for half_ in range(2):
                    pool.wait_ge(s["turned"], 2 * i + half_ - 1)
                    pool.wait_ge(evac[0], TILE0["cmp_w1"] // 2)
                    stage(nsa_q(half_), cols(big, 4 * half_ * S + S * i), s["staged"])
            low(PAIR0["mem_k"] + 1, PAIR0["merge_a"] - PAIR0["mem_k"])
            for h in range(MLH):
                for dv in range(2):
                    pool.wait_ge(ml_step["scaled"], 2 * h + dv + 1)
                    g.tensor_tensor(ml_y[dv], chunk(16 + 2 * h + dv), ml_y[dv], ALU.mult).then_inc(ml_step["gate"], 1)
                for dv in range(2):
                    pool.wait_ge(ml_step["y_hi"], 2 * h + dv + 1)
                    g.tensor_tensor(chunk_r(h + 4 * dv), ml_y[dv], plain(chunk_r(16 + 2 * h + dv)), ALU.subtract) \
                        .then_inc(ml_step["y"], 1)
            low(PAIR0["merge_a"] + 1, PAIR0["merge_b"] - PAIR0["merge_a"] - 1)
            s = att["sw"]
            for n, buf in enumerate(sw_q):
                g.memset(buf, 0.0).then_inc(zeroed, 1)
            pool.wait_ge(zeroed, 3)
            taken("sw_kv")

            def stage_quad(quad, src):
                for half_ in range(2):
                    stage(lambda hd: sw_q[quad][:, (2 * half_ + hd) * S:(2 * half_ + hd + 1) * S], src(half_),
                          s["staged"])

            for quad in range(2):
                stage_quad(quad, lambda half_: chunk(4 * half_ + quad))
            pool.wait_ge(s["staged"], 4)
            low(PAIR0["merge_b"], 1)
            pool.wait_ge(lo_done[1], PAIR0["merge_b"] + 1)
            for quad in range(2):
                pool.wait_ge(s["scores"], NT * (quad + 1))
                stage_quad(quad, lambda half_: chunk(4 * half_ + quad + 2))
            low(PAIR0["merge_b"] + 1, NPAIRS - PAIR0["merge_b"] - 1)


def lay_out(x):
    def tiles(w):
        k, n = w.shape
        return w.reshape(k // P, P, n // P, P).transpose(0, 2, 1, 3)

    def by_output(w):
        t = tiles(w)
        k, n = t.shape[:2]
        return t.reshape(k, n // 2, 2, P, P).transpose(1, 3, 2, 0, 4).reshape(n // 2, P, 2 * k * P)

    def by_token(w):
        k, n = w.shape
        return w.reshape(2, 4, P, n // S, S).transpose(3, 0, 2, 1, 4).reshape(-1, P, PANEL)

    def in_pairs(v, w):
        tv, tw = tiles(v), tiles(w)
        n = tv.shape[1]
        return np.concatenate([t.transpose(1, 2, 0, 3).reshape(n, P, -1) for t in (tv, tw)], axis=2)

    def down(w, k0, k1):
        t = tiles(w)[k0:k1]
        return pad(t.transpose(1, 2, 0, 3).reshape(t.shape[1], P, (k1 - k0) * P))

    def pad(p):
        return np.concatenate([p, np.zeros((*p.shape[:2], PANEL - p.shape[2]), p.dtype)], axis=2)

    def heads(w):
        return w.reshape(-1, 2, 2, 4, HD).transpose(0, 1, 3, 2, 4).reshape(w.shape)

    def feature_rows(w):
        return heads(w.T).T

    def column(v):
        return v.reshape(-1, P).T

    ws = x["nsa_w_in"][0]
    q, kc, vc, ks, vs, kw, vw, gl = np.split(ws, [D + 256 * i for i in range(7)], axis=1)
    w1 = [x[n][0].reshape(2, 8, P, 256).transpose(0, 2, 1, 3).reshape(2, P, PANEL) for n in ("nsa_ck_w1", "nsa_cv_w1")]
    w = x["w_in_2"][0]
    qk, v_ml, o_ml, if_, q_sw, k_sw, v_sw, g_a, g_b = np.split(w, np.cumsum([D, D, D, 8, D, 256, 256, D]), axis=1)
    up = x["ffn_w_up"][0]
    wkv = x["ca_wkv"][0]
    parts = {
        "mem_k": by_output(wkv[:, :D]), "mem_v": by_token(wkv[:, D:]),
        "nsa_v": by_token(np.concatenate([vs, vw], axis=1)), "cmp_kv": by_output(np.concatenate([kc, vc], axis=1)),
        "nsa_k": by_output(np.concatenate([ks, kw], axis=1)), "cmp_w1": np.concatenate(w1),
        "nsa_q": by_output(heads(q)), "nsa_out": by_output(feature_rows(x["nsa_w_out"][0])),
        "ca_q": by_output(x["ca_wq"][0]), "ca_out": by_output(x["ca_wo"][0]),
        "ffn_up_a": in_pairs(up[:, :FF], up[:, FF:])[:HALF["ffn_a"]], "ffn_down_a": down(x["ffn_w_down"][0], 0, HALF["ffn_a"]),
        "ffn_up_b": in_pairs(up[:, :FF], up[:, FF:])[HALF["ffn_a"]:], "ffn_down_b": down(x["ffn_w_down"][0], HALF["ffn_a"], FC),
        "ml_qk": by_output(qk), "ml_v": by_token(v_ml), "ml_o": by_output(o_ml),
        "merge_a": in_pairs(g_a, x["w_branch_a_2"][0]), "sw_q": by_output(heads(q_sw)),
        "sw_kv": np.concatenate([by_output(k_sw), v_sw.reshape(KD, P, 256).transpose(1, 0, 2).reshape(1, P, PANEL)]),
        "merge_b": in_pairs(g_b, feature_rows(x["w_branch_b_2"][0])), "mix_out": by_output(x["w_out_2"][0]),
        "mlp_up_a": by_output(x["w_up_2"][0])[:F2C // 4], "mlp_down_a": down(x["w_down_2"][0], 0, F2C // 2),
        "mlp_up_b": by_output(x["w_up_2"][0])[F2C // 4:], "mlp_down_b": down(x["w_down_2"][0], F2C // 2, F2C),
        "ple_v": np.concatenate([np.zeros((1, P, PANEL), w.dtype),
                                 by_output(x["w_ple_proj_2"][0]).transpose(1, 0, 2).reshape(1, P, PANEL)]),
        "ple_g": by_output(x["w_ple_gate_2"][0]),
    }
    for name, pairs, _ in PHASES:
        assert not pairs or len(parts[name]) == 2 * pairs, name
    gl = gl.reshape(D, 2, 2, 4, 3).transpose(0, 1, 3, 2, 4).reshape(D, 48)
    sinks = x["sinks_2"][0].reshape(2, 2, 4).transpose(2, 0, 1).reshape(1, 16)
    norms = [x["mem_norm_w"], x["norm_mix_w"][0], x["norm_cross_w"][0], x["norm_ffn_w"][0], x["final_norm_w"],
             x["norm_mix_g_2"][0], x["norm_mlp_g_2"][0], x["norm_ple_g_2"][0], x["final_norm_g_2"],
             x["mlstm_norm_g_2"][0]]
    b_if = np.zeros((P, 2), np.float32)
    b_if[0:MLH] = x["b_if_2"][0].reshape(2, MLH).T
    params = np.concatenate(
        [column(v) for v in norms] + [column(v) for v in x["ffn_conv_w"][0]] + [column(v) for v in x["conv_qk_2"][0]]
        + [column(x["nsa_pe_k"][0].reshape(-1)), column(x["nsa_pe_v"][0].reshape(-1)), np.repeat(sinks, P, axis=0), b_if],
        axis=1)

    def chunks(v):
        return v.T.reshape(-1, P, v.shape[0]).transpose(1, 0, 2).reshape(P, -1)

    def rows(v):
        return v.reshape(-1, P, v.shape[1]).transpose(1, 0, 2).reshape(P, -1)

    ck2 = x["nsa_ck_w2"][0]
    return {
        "panels": np.concatenate([parts[n] for n, pairs, _ in PHASES if pairs]), "params": params,
        "x": chunks(x["x"][0]), "mem": chunks(x["mem"][0]), "ple": chunks(x["p_2"][0, 0]),
        "w_gate": rows(gl), "w_if": rows(if_), "w2_k": rows(np.concatenate([ck2, ck2], axis=1)),
        "w2_v": rows(x["nsa_cv_w2"][0]),
    }


def kernel(**inputs):
    import concourse.bacc as _bacc
    from concourse.bass_utils import run_bass_kernel_spmd as _run

    nc = _bacc.Bacc("TRN2", target_bir_lowering=False, num_devices=1)
    arrays, args = {}, {}
    for name, v in lay_out({k: np.asarray(v) for k, v in inputs.items()}).items():
        v = np.ascontiguousarray(v)
        arrays[f"in_{name}"] = v
        args[name] = nc.dram_tensor(f"in_{name}", v.shape, mybir.dt.from_np(v.dtype), kind="ExternalInput").ap()
    out = nc.dram_tensor("out", (P, KD * S), F32, kind="ExternalOutput").ap()
    program(nc, args, out)
    r = _run(nc, [arrays], core_ids=[0])
    y = r.results[0]["out"]
    return np.ascontiguousarray(y.reshape(P, KD, S).transpose(2, 1, 0).reshape(1, S, D))
```
